# Optimizing a Trainium2 kernel written in Bass

```python
import jax, jax.numpy as jnp
from jax import lax
import numpy as np
import math

D_MODEL = 2048
BATCH = 1
SEQ = 256
DEPTH = 1

MLA_HEADS = 16
Q_LORA = 512
KV_LORA = 512
QK_NOPE = 128
QK_ROPE = 64
V_HEAD = 128
QK_HEAD = QK_NOPE + QK_ROPE
ROPE_THETA = 10000.0
Q_BLOCK = 128
SGU_WIDTH = D_MODEL
SGU_GROUPS = 8
SGU_GROUP_DIM = SGU_WIDTH // SGU_GROUPS
CHUNK = 128
PEER_HEADS = 8
N_KEYS = 128
N_EXPERTS = N_KEYS * N_KEYS
PEER_TOPK = 16
KEY_DIM = 128
TOKEN_BLOCK = 128
EPS = 1e-6

OFF_CQ = Q_LORA
OFF_CKV = OFF_CQ + KV_LORA
OFF_KPE = OFF_CKV + QK_ROPE
OFF_SGU = OFF_KPE + 2 * SGU_WIDTH
IN_COLS = OFF_SGU + 2 * D_MODEL


def rmsnorm(x, g):
    xf = x.astype(jnp.float32)
    r = lax.rsqrt(jnp.mean(xf * xf, axis=-1, keepdims=True) + EPS)
    return (xf * r).astype(x.dtype) * g

def layernorm(x, g, b):
    xf = x.astype(jnp.float32)
    mu = jnp.mean(xf, axis=-1, keepdims=True)
    var = jnp.mean(jnp.square(xf - mu), axis=-1, keepdims=True)
    return ((xf - mu) * lax.rsqrt(var + EPS)).astype(x.dtype) * g + b

def rope(x, positions):
    d = x.shape[-1]
    freqs = ROPE_THETA ** (-jnp.arange(0, d, 2, dtype=jnp.float32) / d)
    ang = positions.astype(jnp.float32)[..., None] * freqs
    cos = jnp.cos(ang)[:, :, None, :].astype(x.dtype)
    sin = jnp.sin(ang)[:, :, None, :].astype(x.dtype)
    x1, x2 = x[..., : d // 2], x[..., d // 2 :]
    return jnp.concatenate([x1 * cos - x2 * sin, x1 * sin + x2 * cos], axis=-1)

def causal_block_attention(q, k, v):
    B, S, H, Dq = q.shape
    Dv = v.shape[-1]
    nb = S // Q_BLOCK
    qb = q.reshape(B, nb, Q_BLOCK, H, Dq).transpose(1, 0, 2, 3, 4)
    key_pos = jnp.arange(S)
    scale = Dq ** -0.5

    def one_block(args):
        q_blk, blk = args
        s = jnp.einsum("bqhd,bkhd->bhqk", q_blk, k).astype(jnp.float32) * scale
        q_pos = blk * Q_BLOCK + jnp.arange(Q_BLOCK)
        mask = q_pos[:, None] >= key_pos[None, :]
        s = jnp.where(mask[None, None], s, -jnp.inf)
        p = jax.nn.softmax(s, axis=-1).astype(v.dtype)
        return jnp.einsum("bhqk,bkhd->bqhd", p, v)

    o = lax.map(one_block, (qb, jnp.arange(nb)))
    return o.transpose(1, 0, 2, 3, 4).reshape(B, S, H * Dv)

def mla_branch(c_q, c_kv, k_pe, positions, g_q_a, w_uq, g_kv_a, w_ukv):
    B, S, _ = c_q.shape
    q = jnp.einsum("bsr,rhd->bshd", rmsnorm(c_q, g_q_a), w_uq)
    q = jnp.concatenate([q[..., :QK_NOPE], rope(q[..., QK_NOPE:], positions)], axis=-1)
    kv = jnp.einsum("bsr,rhd->bshd", rmsnorm(c_kv, g_kv_a), w_ukv)
    k_nope, v = kv[..., :QK_NOPE], kv[..., QK_NOPE:]
    k_pe = rope(k_pe[:, :, None, :], positions)
    k = jnp.concatenate([k_nope, jnp.broadcast_to(k_pe, (B, S, MLA_HEADS, QK_ROPE))], axis=-1)
    return causal_block_attention(q, k, v)

def sgu_branch(z, ln_g, ln_b, w_spatial, b_spatial):
    z = jax.nn.gelu(z)
    u, v = z[..., :SGU_WIDTH], z[..., SGU_WIDTH:]
    v = layernorm(v, ln_g, ln_b)
    B, S, _ = v.shape
    vg = v.reshape(B, S // CHUNK, CHUNK, SGU_GROUPS, SGU_GROUP_DIM)
    w = w_spatial * jnp.tril(jnp.ones((CHUNK, CHUNK), dtype=w_spatial.dtype))[None]
    mixed = jnp.einsum("gts,bcsgd->bctgd", w, vg) + b_spatial.T[None, None, :, :, None]
    return u * mixed.reshape(B, S, SGU_WIDTH)

def peer_ffn(h, w_pq, peer_keys, peer_u, peer_v):
    B, S, D = h.shape
    q = jnp.einsum("bsd,dhk->bshk", h, w_pq).reshape(B, S, PEER_HEADS, 2, KEY_DIM)
    sub = jnp.einsum("bshpk,hpnk->bshpn", q, peer_keys).astype(jnp.float32)
    s, i = lax.top_k(sub, PEER_TOPK)
    cand = (s[..., 0, :, None] + s[..., 1, None, :]).reshape(B, S, PEER_HEADS, PEER_TOPK * PEER_TOPK)
    cidx = (i[..., 0, :, None] * N_KEYS + i[..., 1, None, :]).reshape(B, S, PEER_HEADS, PEER_TOPK * PEER_TOPK)
    top_s, pos = lax.top_k(cand, PEER_TOPK)
    idx = jnp.take_along_axis(cidx, pos, axis=-1)
    gate = jax.nn.softmax(top_s, axis=-1).astype(h.dtype)
    nt = (B * S) // TOKEN_BLOCK
    hb = h.reshape(nt, TOKEN_BLOCK, D)
    ib = idx.reshape(nt, TOKEN_BLOCK, PEER_HEADS, PEER_TOPK)
    gb = gate.reshape(nt, TOKEN_BLOCK, PEER_HEADS, PEER_TOPK)

    def one_block(args):
        x_blk, i_blk, g_blk = args
        u = jnp.take(peer_u, i_blk, axis=0)
        a = jax.nn.gelu(jnp.einsum("td,thkd->thk", x_blk, u)) * g_blk
        v = jnp.take(peer_v, i_blk, axis=0)
        return jnp.einsum("thk,thkd->td", a, v)

    return lax.map(one_block, (hb, ib, gb)).reshape(B, S, D)

def first_inputs(seed: int = 0) -> dict:
    key = jax.random.key(seed)
    ks = jax.random.split(key, 24)
    f32 = jnp.float32
    nrm = lambda k, shape, scale: jax.random.normal(k, shape, f32) * scale
    gain = lambda k, shape: 1.0 + 0.05 * jax.random.normal(k, shape, f32)
    L = DEPTH
    x = jax.random.normal(ks[0], (BATCH, SEQ, D_MODEL), f32)
    offsets = jax.random.randint(ks[1], (BATCH, 1), 0, 4096, dtype=jnp.int32)
    positions = offsets + jnp.arange(SEQ, dtype=jnp.int32)[None, :]
    return {
        "x": x,
        "positions": positions,
        "g_norm1": gain(ks[2], (L, D_MODEL)),
        "w_in": nrm(ks[3], (L, D_MODEL, IN_COLS), D_MODEL ** -0.5),
        "g_q_a": gain(ks[4], (L, Q_LORA)),
        "w_uq": nrm(ks[5], (L, Q_LORA, MLA_HEADS, QK_HEAD), Q_LORA ** -0.5),
        "g_kv_a": gain(ks[6], (L, KV_LORA)),
        "w_ukv": nrm(ks[7], (L, KV_LORA, MLA_HEADS, QK_NOPE + V_HEAD), KV_LORA ** -0.5),
        "sgu_ln_g": gain(ks[8], (L, SGU_WIDTH)),
        "sgu_ln_b": nrm(ks[9], (L, SGU_WIDTH), 0.02),
        "w_spatial": nrm(ks[10], (L, SGU_GROUPS, CHUNK, CHUNK), CHUNK ** -0.5),
        "b_spatial": gain(ks[11], (L, SGU_GROUPS, CHUNK)),
        "b_gate": nrm(ks[12], (L, 2 * D_MODEL), 0.01),
        "w_out": nrm(ks[13], (L, D_MODEL, D_MODEL), D_MODEL ** -0.5),
        "g_norm2": gain(ks[14], (L, D_MODEL)),
        "w_peer_q": nrm(ks[15], (L, D_MODEL, PEER_HEADS, 2 * KEY_DIM), D_MODEL ** -0.5),
        "peer_keys": nrm(ks[16], (L, PEER_HEADS, 2, N_KEYS, KEY_DIM), KEY_DIM ** -0.5),
        "peer_u": nrm(ks[17], (L, N_EXPERTS, D_MODEL), D_MODEL ** -0.5),
        "peer_v": nrm(ks[18], (L, N_EXPERTS, D_MODEL), PEER_HEADS ** -0.5),
        "g_final": gain(ks[19], (D_MODEL,)),
    }

def first_block(x, positions, g_norm1, w_in, g_q_a, w_uq, g_kv_a, w_ukv, sgu_ln_g, sgu_ln_b,
              w_spatial, b_spatial, b_gate, w_out, g_norm2, w_peer_q, peer_keys, peer_u,
              peer_v, g_final):
    for l in range(DEPTH):
        h = rmsnorm(x, g_norm1[l])
        proj = h @ w_in[l]
        c_q = proj[..., :OFF_CQ]
        c_kv = proj[..., OFF_CQ:OFF_CKV]
        k_pe = proj[..., OFF_CKV:OFF_KPE]
        z_sgu = proj[..., OFF_KPE:OFF_SGU]
        gates = jax.nn.sigmoid(proj[..., OFF_SGU:] + b_gate[l])
        o_a = mla_branch(c_q, c_kv, k_pe, positions, g_q_a[l], w_uq[l], g_kv_a[l], w_ukv[l])
        o_b = sgu_branch(z_sgu, sgu_ln_g[l], sgu_ln_b[l], w_spatial[l], b_spatial[l])
        merged = gates[..., :D_MODEL] * o_a + gates[..., D_MODEL:] * o_b
        x = x + merged @ w_out[l]
        h2 = rmsnorm(x, g_norm2[l])
        x = x + peer_ffn(h2, w_peer_q[l], peer_keys[l], peer_u[l], peer_v[l])
    return rmsnorm(x, g_final)


HEAD_DIM = 128
N_ATTN_HEADS = 8
ATTN_WIDTH = N_ATTN_HEADS * HEAD_DIM
MOBA_BLOCK = 256
MOBA_TOPK = 3
Q_CHUNK = 32
SSM_WIDTH = D_MODEL // 2
SSM_GROUP = 16
SSM_GROUPS = SSM_WIDTH // SSM_GROUP
SSM_STATE = 64
FFN_HIDDEN = 5632
CONV_WIDTH = 3
N_BRANCHES = 2
N_MOD = 6
IN_WIDTH = 3 * ATTN_WIDTH + SSM_WIDTH + N_BRANCHES * D_MODEL
NEG_INF = -1e30


def rms_norm(x, g):
    xf = x.astype(jnp.float32)
    y = xf * lax.rsqrt(jnp.mean(xf * xf, axis=-1, keepdims=True) + EPS)
    return y.astype(x.dtype) * g

def rotary(x, positions):
    half = HEAD_DIM // 2
    inv_freq = ROPE_THETA ** (-jnp.arange(half, dtype=jnp.float32) / half)
    ang = positions.astype(jnp.float32)[..., None] * inv_freq
    cos = jnp.cos(ang)[:, :, None, :].astype(x.dtype)
    sin = jnp.sin(ang)[:, :, None, :].astype(x.dtype)
    x1, x2 = x[..., :half], x[..., half:]
    return jnp.concatenate([x1 * cos - x2 * sin, x1 * sin + x2 * cos], axis=-1)

def moba_attention(q, k, v):
    b, h, s, dh = q.shape
    n_blocks = -(-s // MOBA_BLOCK)
    s_pad = n_blocks * MOBA_BLOCK
    topk = min(MOBA_TOPK, n_blocks)
    pad = ((0, 0), (0, 0), (0, s_pad - s), (0, 0))
    k_p = jnp.pad(k, pad)
    v_p = jnp.pad(v, pad)
    k_blocks = k_p.reshape(b, h, n_blocks, MOBA_BLOCK, dh)
    v_blocks = v_p.reshape(b, h, n_blocks, MOBA_BLOCK, dh)
    k_mean = jnp.mean(k_blocks.astype(jnp.float32), axis=3).astype(k.dtype)
    scale = HEAD_DIM ** -0.5
    gather = jax.vmap(jax.vmap(lambda blocks, idx: blocks[idx]))

    def chunk(ci):
        start = ci * Q_CHUNK
        q_c = lax.dynamic_slice_in_dim(q, start, Q_CHUNK, axis=2)
        t = start + jnp.arange(Q_CHUNK)
        cur = start // MOBA_BLOCK
        blk_scores = jnp.einsum('bhqd,bhnd->bhqn', q_c, k_mean).astype(jnp.float32)
        past = jnp.arange(n_blocks) < cur
        blk_scores = jnp.where(past, blk_scores, NEG_INF)
        _, idx = lax.top_k(blk_scores, topk)
        slot_ok = jnp.arange(topk) < cur
        k_sel = gather(k_blocks, idx)
        v_sel = gather(v_blocks, idx)
        s_sel = jnp.einsum('bhqd,bhqnjd->bhqnj', q_c, k_sel).astype(jnp.float32) * scale
        s_sel = jnp.where(slot_ok[:, None], s_sel, NEG_INF).reshape(b, h, Q_CHUNK, topk * MOBA_BLOCK)
        k_own = lax.dynamic_slice_in_dim(k_p, cur * MOBA_BLOCK, MOBA_BLOCK, axis=2)
        v_own = lax.dynamic_slice_in_dim(v_p, cur * MOBA_BLOCK, MOBA_BLOCK, axis=2)
        s_own = jnp.einsum('bhqd,bhjd->bhqj', q_c, k_own).astype(jnp.float32) * scale
        key_pos = cur * MOBA_BLOCK + jnp.arange(MOBA_BLOCK)
        s_own = jnp.where(key_pos[None, :] <= t[:, None], s_own, NEG_INF)
        p = jax.nn.softmax(jnp.concatenate([s_sel, s_own], axis=-1), axis=-1).astype(v.dtype)
        p_sel = p[..., :topk * MOBA_BLOCK].reshape(b, h, Q_CHUNK, topk, MOBA_BLOCK)
        p_own = p[..., topk * MOBA_BLOCK:]
        return (jnp.einsum('bhqnj,bhqnjd->bhqd', p_sel, v_sel)
                + jnp.einsum('bhqj,bhjd->bhqd', p_own, v_own))

    out = lax.map(chunk, jnp.arange(s // Q_CHUNK))
    return out.transpose(1, 2, 0, 3, 4).reshape(b, h, s, dh)

def s5_branch(u, lam_re, lam_im, log_dt, b_re, b_im, c_re, c_im, d_skip, w_glu, b_glu):
    bsz, s, _ = u.shape
    f32 = jnp.float32
    ug = u.reshape(bsz, s, SSM_GROUPS, SSM_GROUP).astype(f32)
    dt = jnp.exp(log_dt.astype(f32))[:, None]
    lr = lam_re.astype(f32)
    li = lam_im.astype(f32)
    mag = jnp.exp(lr * dt)
    ab_re = mag * jnp.cos(li * dt)
    ab_im = mag * jnp.sin(li * dt)
    den = lr * lr + li * li
    nr = ab_re - 1.0
    ni = ab_im
    coef_re = (nr * lr + ni * li) / den
    coef_im = (ni * lr - nr * li) / den
    bu_re = jnp.einsum('bsgh,gph->bsgp', ug, b_re.astype(f32))
    bu_im = jnp.einsum('bsgh,gph->bsgp', ug, b_im.astype(f32))
    x_re0 = coef_re * bu_re - coef_im * bu_im
    x_im0 = coef_re * bu_im + coef_im * bu_re
    a_re = jnp.broadcast_to(ab_re, x_re0.shape)
    a_im = jnp.broadcast_to(ab_im, x_re0.shape)

    def combine(e1, e2):
        a1r, a1i, b1r, b1i = e1
        a2r, a2i, b2r, b2i = e2
        return (a2r * a1r - a2i * a1i, a2r * a1i + a2i * a1r,
                a2r * b1r - a2i * b1i + b2r, a2r * b1i + a2i * b1r + b2i)

    _, _, xr, xi = lax.associative_scan(combine, (a_re, a_im, x_re0, x_im0), axis=1)
    y = (jnp.einsum('bsgp,ghp->bsgh', xr, c_re.astype(f32))
         - jnp.einsum('bsgp,ghp->bsgh', xi, c_im.astype(f32))
         + d_skip.astype(f32).reshape(SSM_GROUPS, SSM_GROUP) * ug)
    y = jax.nn.gelu(y.reshape(bsz, s, SSM_WIDTH)).astype(u.dtype)
    return y * jax.nn.sigmoid(y @ w_glu + b_glu)

def causal_dwconv(u, w, bias):
    ch = u.shape[-1]
    y = lax.conv_general_dilated(u, w[:, None, :].astype(u.dtype), window_strides=(1,),
                                 padding=[(CONV_WIDTH - 1, 0)],
                                 dimension_numbers=('NWC', 'WIO', 'NWC'),
                                 feature_group_count=ch)
    return y + bias

def second_inputs(seed: int = 0) -> dict:
    key = jax.random.key(seed)
    ks = jax.random.split(key, 32)
    nrm = jax.random.normal
    L = DEPTH
    x = nrm(ks[0], (BATCH, SEQ, D_MODEL), jnp.float32)
    c = nrm(ks[1], (BATCH, D_MODEL), jnp.float32)
    offsets = jax.random.randint(ks[2], (BATCH, 1), 0, 1024, dtype=jnp.int32)
    positions = offsets + jnp.arange(SEQ, dtype=jnp.int32)[None, :]
    w_mod = nrm(ks[3], (L, D_MODEL, N_MOD * D_MODEL), jnp.float32) * (0.5 * D_MODEL ** -0.5)
    b_mod = nrm(ks[4], (L, N_MOD * D_MODEL), jnp.float32) * 0.01
    norm1_g = 1.0 + 0.02 * nrm(ks[5], (L, D_MODEL), jnp.float32)
    w_in = nrm(ks[6], (L, D_MODEL, IN_WIDTH), jnp.float32) * D_MODEL ** -0.5
    q_norm_g = 1.0 + 0.02 * nrm(ks[7], (L, HEAD_DIM), jnp.float32)
    k_norm_g = 1.0 + 0.02 * nrm(ks[8], (L, HEAD_DIM), jnp.float32)
    n_idx = jnp.arange(SSM_STATE, dtype=jnp.float32)
    ssm_lambda_re = -0.5 + 0.01 * nrm(ks[9], (L, SSM_GROUPS, SSM_STATE), jnp.float32)
    ssm_lambda_im = math.pi * n_idx + 0.01 * nrm(ks[10], (L, SSM_GROUPS, SSM_STATE), jnp.float32)
    ssm_log_dt = jax.random.uniform(ks[11], (L, SSM_GROUPS), jnp.float32, math.log(1e-3), math.log(1e-1))
    b_scale = (2.0 * SSM_GROUP) ** -0.5
    ssm_b_re = nrm(ks[12], (L, SSM_GROUPS, SSM_STATE, SSM_GROUP), jnp.float32) * b_scale
    ssm_b_im = nrm(ks[13], (L, SSM_GROUPS, SSM_STATE, SSM_GROUP), jnp.float32) * b_scale
    c_scale = (2.0 * SSM_STATE) ** -0.5
    ssm_c_re = nrm(ks[14], (L, SSM_GROUPS, SSM_GROUP, SSM_STATE), jnp.float32) * c_scale
    ssm_c_im = nrm(ks[15], (L, SSM_GROUPS, SSM_GROUP, SSM_STATE), jnp.float32) * c_scale
    ssm_d = nrm(ks[16], (L, SSM_WIDTH), jnp.float32)
    w_glu = nrm(ks[17], (L, SSM_WIDTH, SSM_WIDTH), jnp.float32) * SSM_WIDTH ** -0.5
    b_glu = nrm(ks[18], (L, SSM_WIDTH), jnp.float32) * 0.01
    w_attn_br = nrm(ks[19], (L, ATTN_WIDTH, D_MODEL), jnp.float32) * ATTN_WIDTH ** -0.5
    w_ssm_br = nrm(ks[20], (L, SSM_WIDTH, D_MODEL), jnp.float32) * SSM_WIDTH ** -0.5
    w_out = nrm(ks[21], (L, D_MODEL, D_MODEL), jnp.float32) * D_MODEL ** -0.5
    norm2_g = 1.0 + 0.02 * nrm(ks[22], (L, D_MODEL), jnp.float32)
    w_up = nrm(ks[23], (L, D_MODEL, 2 * FFN_HIDDEN), jnp.float32) * D_MODEL ** -0.5
    conv_w = nrm(ks[24], (L, CONV_WIDTH, 2 * FFN_HIDDEN), jnp.float32) * CONV_WIDTH ** -0.5
    conv_b = nrm(ks[25], (L, 2 * FFN_HIDDEN), jnp.float32) * 0.01
    w_down = nrm(ks[26], (L, FFN_HIDDEN, D_MODEL), jnp.float32) * FFN_HIDDEN ** -0.5
    return {'x': x, 'c': c, 'positions': positions, 'w_mod': w_mod, 'b_mod': b_mod,
            'norm1_g': norm1_g, 'w_in': w_in, 'q_norm_g': q_norm_g, 'k_norm_g': k_norm_g,
            'ssm_lambda_re': ssm_lambda_re, 'ssm_lambda_im': ssm_lambda_im, 'ssm_log_dt': ssm_log_dt,
            'ssm_b_re': ssm_b_re, 'ssm_b_im': ssm_b_im, 'ssm_c_re': ssm_c_re, 'ssm_c_im': ssm_c_im,
            'ssm_d': ssm_d, 'w_glu': w_glu, 'b_glu': b_glu, 'w_attn_br': w_attn_br,
            'w_ssm_br': w_ssm_br, 'w_out': w_out, 'norm2_g': norm2_g, 'w_up': w_up,
            'conv_w': conv_w, 'conv_b': conv_b, 'w_down': w_down}

def second_block(x, c, positions, w_mod, b_mod, norm1_g, w_in, q_norm_g, k_norm_g,
              ssm_lambda_re, ssm_lambda_im, ssm_log_dt, ssm_b_re, ssm_b_im, ssm_c_re, ssm_c_im,
              ssm_d, w_glu, b_glu, w_attn_br, w_ssm_br, w_out, norm2_g, w_up, conv_w, conv_b,
              w_down):
    bsz, s, _ = x.shape
    split_pts = [ATTN_WIDTH, 2 * ATTN_WIDTH, 3 * ATTN_WIDTH, 3 * ATTN_WIDTH + SSM_WIDTH]
    for l in range(DEPTH):
        mod = jax.nn.silu(c) @ w_mod[l] + b_mod[l]
        sh1, sc1, g1, sh2, sc2, g2 = jnp.split(mod, N_MOD, axis=-1)

        h = rms_norm(x, norm1_g[l]) * (1.0 + sc1[:, None]) + sh1[:, None]
        proj = h @ w_in[l]
        q, k, v, u, gates = jnp.split(proj, split_pts, axis=-1)
        q = rotary(rms_norm(q.reshape(bsz, s, N_ATTN_HEADS, HEAD_DIM), q_norm_g[l]), positions)
        k = rotary(rms_norm(k.reshape(bsz, s, N_ATTN_HEADS, HEAD_DIM), k_norm_g[l]), positions)
        v = v.reshape(bsz, s, N_ATTN_HEADS, HEAD_DIM)
        attn = moba_attention(q.transpose(0, 2, 1, 3), k.transpose(0, 2, 1, 3), v.transpose(0, 2, 1, 3))
        y_attn = attn.transpose(0, 2, 1, 3).reshape(bsz, s, ATTN_WIDTH)
        y_ssm = s5_branch(u, ssm_lambda_re[l], ssm_lambda_im[l], ssm_log_dt[l], ssm_b_re[l], ssm_b_im[l],
                          ssm_c_re[l], ssm_c_im[l], ssm_d[l], w_glu[l], b_glu[l])
        gate_a, gate_s = jnp.split(gates, N_BRANCHES, axis=-1)
        merged = (jax.nn.sigmoid(gate_a) * (y_attn @ w_attn_br[l])
                  + jax.nn.sigmoid(gate_s) * (y_ssm @ w_ssm_br[l]))
        x = x + g1[:, None] * (merged @ w_out[l])

        h2 = rms_norm(x, norm2_g[l]) * (1.0 + sc2[:, None]) + sh2[:, None]
        up = causal_dwconv(h2 @ w_up[l], conv_w[l], conv_b[l])
        val, gt = jnp.split(up, 2, axis=-1)
        x = x + g2[:, None] * ((jax.nn.silu(gt) * val) @ w_down[l])
    return x


def setup_inputs(seed=0):
    out = dict(first_inputs(seed))
    for name, value in second_inputs(seed + 1).items():
        if name != "x":
            out[name + "_2"] = value
    return out


def reference(
    x, positions, g_norm1, w_in, g_q_a, w_uq, g_kv_a, w_ukv, sgu_ln_g, sgu_ln_b, w_spatial,
    b_spatial, b_gate, w_out, g_norm2, w_peer_q, peer_keys, peer_u, peer_v, g_final, c_2,
    positions_2, w_mod_2, b_mod_2, norm1_g_2, w_in_2, q_norm_g_2, k_norm_g_2, ssm_lambda_re_2,
    ssm_lambda_im_2, ssm_log_dt_2, ssm_b_re_2, ssm_b_im_2, ssm_c_re_2, ssm_c_im_2, ssm_d_2,
    w_glu_2, b_glu_2, w_attn_br_2, w_ssm_br_2, w_out_2, norm2_g_2, w_up_2, conv_w_2, conv_b_2,
    w_down_2,
):
    x = first_block(
        x, positions, g_norm1, w_in, g_q_a, w_uq, g_kv_a, w_ukv, sgu_ln_g, sgu_ln_b, w_spatial,
        b_spatial, b_gate, w_out, g_norm2, w_peer_q, peer_keys, peer_u, peer_v, g_final,
    )
    return second_block(
        x, c_2, positions_2, w_mod_2, b_mod_2, norm1_g_2, w_in_2, q_norm_g_2, k_norm_g_2,
        ssm_lambda_re_2, ssm_lambda_im_2, ssm_log_dt_2, ssm_b_re_2, ssm_b_im_2, ssm_c_re_2,
        ssm_c_im_2, ssm_d_2, w_glu_2, b_glu_2, w_attn_br_2, w_ssm_br_2, w_out_2, norm2_g_2,
        w_up_2, conv_w_2, conv_b_2, w_down_2,
    )


_drawn_inputs = setup_inputs


def setup_inputs(seed=0):
    import zlib

    import numpy as np

    out = dict(_drawn_inputs(seed))
    spreads = {}
    factors = {'g_q_a': 4.303,
     'g_kv_a': 3.484,
     'sgu_ln_b': 4.538,
     'b_gate': 7.101,
     'b_mod_2': 6.229,
     'norm1_g_2': 8.0,
     'q_norm_g_2': 8.0,
     'k_norm_g_2': 8.0,
     'ssm_lambda_re_2': 64.0,
     'ssm_lambda_im_2': 64.0,
     'ssm_log_dt_2': 64.0,
     'ssm_b_re_2': 64.0,
     'ssm_b_im_2': 64.0,
     'ssm_c_re_2': 64.0,
     'ssm_c_im_2': 64.0,
     'b_glu_2': 63.957,
     'norm2_g_2': 8.0,
     'conv_b_2': 32.635}
    for name, (base, spread) in spreads.items():
        noise = np.random.default_rng([zlib.crc32(name.encode()), seed]).standard_normal(out[name].shape)
        drawn = base * np.exp(spread * noise) if base else spread * noise
        out[name] = __import__('jax').numpy.asarray(drawn.astype(out[name].dtype))
    for name, factor in factors.items():
        out[name] = (out[name] * factor).astype(out[name].dtype)
    return out
```

```python
import math
from contextlib import ExitStack

import numpy as np

import concourse.bass as bass
from concourse import mybir

F32 = mybir.dt.float32
F32R = mybir.dt.float32r
I32 = mybir.dt.int32
U32 = mybir.dt.uint32
ALU = mybir.AluOpType
ACT = mybir.ActivationFunctionType
AX = mybir.AxisListType.X

P = 128
S, TT = 256, 2
D, KD = 2048, 16
CH = 512
TW = 4 * CH
RAW, SPL = 4, 2
EPS = 1e-6
HEADS, NOPE, ROPE, VH = 16, 128, 64, 128
LORA, KL = 512, 4
GROUP = 4
SGU_G, SGU_W = 8, 256
PH, NKEY, TOPK = 8, 128, 16
HK = PH * TOPK
NEXP = NKEY * NKEY
EB = CH
NBLK = NEXP // EB
JB = EB // NKEY
AH, AD, AW = 8, 128, 1024
NG, GH, NST = 64, 16, 64
STT = NG * NST // P
SB = 4
FFN = 5632
FB = FFN // CH
NEG = -1e30

STREAM = [("w_in", 72), ("kpe", 1), ("mla", 16), ("out", 16), ("pq", 16), ("peer", 8 * NBLK),
          ("in2", 64), ("glu", 4), ("abr", 8), ("sbr", 8), ("out2", 16), ("ffn", 12 * FB)]
BASE, _n = {}, 0
for _name, _count in STREAM:
    BASE[_name] = _n
    _n += _count
TOTAL = _n

TURNS = [("h1", 8), ("cq", 2), ("ckv", 2), ("merged", 8), ("h2", 8), ("h3", 8), ("ya", 4),
         ("merged2", 8), ("h4", 8)]
TBASE, _n = {}, 0
for _name, _count in TURNS:
    TBASE[_name] = _n
    _n += _count

COLS = [("g1", 16), ("gqa", 4), ("gkva", 4), ("g2", 16), ("g3", 16), ("g4", 16), ("bsp", 8),
        ("c", 16), ("dskip", 8), ("lre", 32), ("lim", 32), ("ldt", 32), ("conv", FB * 32)]
COFF, _n = {}, 0
for _name, _count in COLS:
    COFF[_name] = _n
    _n += _count
NCOLS = _n

CONST = [("ident", 128), ("ones", 128), ("mask", 384), ("triu", 128), ("iota", 256),
         ("freq", 32), ("freq2", 64)]
KOFF, _n = {}, 0
for _name, _count in CONST:
    KOFF[_name] = _n
    _n += _count
NCONST = _n

TWO_PI = 2.0 * math.pi
INV_2PI = 1.0 / TWO_PI
C1 = 6.28125
C2 = float(np.float32(0.0019350051879882812))
C3 = TWO_PI - C1 - C2
MAGIC = 12582912.0
PI_IN = 3.1415925
TURN = 6.283185


class Steps:

    def __init__(self, eng, sem):
        self.eng, self.sem, self.base, self.k = eng, sem, 0, 0

    def step(self, ins):
        ins.then_inc(self.sem, 1)
        self.k += 1

    def wait(self):
        self.eng.wait_ge(self.sem, self.base + self.k)

    def link(self, ins):
        self.step(ins)
        self.wait()

    def enter(self, per, it):
        self.outer = self.base + self.k
        self.base, self.k = per * it + self.outer, 0

    def leave(self, per, count):
        assert self.k == per, (self.k, per)
        self.base, self.k = self.outer + per * count, 0


def build(nc, A, out):
    V, SC, PE_, GP = nc.vector, nc.scalar, nc.tensor, nc.gpsimd
    ctx = ExitStack()
    with ctx:
        base0 = 16512

        def at(name, shape, kb, dt=F32):
            return nc.alloc_sbuf_tensor_at(name, shape, dt, offset=base0 + int(kb * 1024)).ap()

        def sem(name):
            return ctx.enter_context(nc.semaphore(name))

        raw = at("raw", [P, RAW, TW], 0)
        hi = at("hi", [P, SPL, TW], 32, F32R)
        lo = at("lo", [P, SPL, TW], 48, F32R)
        xh = at("xh", [P, KD, S], 64, F32R)
        xl = at("xl", [P, KD, S], 80, F32R)
        X = at("X", [P, TT, D], 96)
        const = at("const", [P, NCONST], 112)
        cols = at("cols", [P, NCOLS], 112 + 4.5)
        stat = at("stat", [P, 256], 112 + 4.5 + 2.25)
        trig = at("trig", [P, 2, 192], 112 + 4.5 + 3.25)
        W0 = 112 + 4.5 + 3.25 + 1.5

        def K(name):
            return const[:, KOFF[name]:KOFF[name] + dict(CONST)[name]]

        def C(name, i, n=1):
            return cols[:, COFF[name] + i:COFF[name] + i + n]

        ident, ones, iota = K("ident"), K("ones"), K("iota")

        Z = at("Z", [P, TT, 2 * D], W0)
        GT = at("GT", [P, TT, 2 * D], W0 + 32)
        CQ = at("CQ", [P, TT, LORA], W0 + 64)
        CKV = at("CKV", [P, TT, LORA], W0 + 68)
        KPE = at("KPE", [P, TT, ROPE], W0 + 72)
        brow = at("brow", [1, 2 * CH], W0 + 73)
        wsp = at("wsp", [P, SGU_G, P], W0 + 77)
        KPR = at("KPR", [P, TT, P], W0 + 81)
        KPT = at("KPT", [P, S], W0 + 82)
        ktmp = at("ktmp", [P, TT, 64], W0 + 83)
        N1 = at("N1", [P, TT, D], W0)
        ang = at("ang", [P, 6, 192], W0 + 16)
        posi = at("posi", [P, 4], W0 + 22, I32)
        posf = at("posf", [P, 4], W0 + 22.25)
        junk = at("junk", [P, D], W0 + 24)
        lng = at("lng", [P, D], 80)
        lnb = at("lnb", [P, D], 88)
        cqh = at("cqh", [P, KL, S], 64, F32R)
        cql = at("cql", [P, KL, S], 68, F32R)
        ckh = at("ckh", [P, KL, S], 72, F32R)
        ckl = at("ckl", [P, KL, S], 76, F32R)
        junk2 = at("junk2", [P, D], 64)
        qn = at("qn", [P, TT, CH], W0)
        kn = at("kn", [P, TT, CH], W0 + 4)
        vv = at("vv", [P, TT, CH], W0 + 8)
        qr = at("qr", [P, TT, GROUP * ROPE], W0 + 12)
        qrr = at("qrr", [P, TT, GROUP * ROPE], W0 + 14)
        qtmp = at("qtmp", [P, TT, GROUP * 32], W0 + 16)
        qT = at("qT", [P, GROUP, S], W0 + 17)
        kT = at("kT", [P, GROUP, S], W0 + 21)
        qrT = at("qrT", [P, GROUP // 2, S], W0 + 25)
        sc = at("sc", [P, 2, 384], W0 + 73)
        pr = at("pr", [P, 2, 384], W0 + 76)
        pT = at("pT", [P, 2, 384], W0 + 27)
        N2 = at("N2", [P, TT, D], W0)
        Q = at("Q", [P, TT, D], W0)
        QT = at("QT", [P, 16, S], W0 + 16)
        keys = at("keys", [P, 16, NKEY], W0 + 32)
        sub = at("sub", [P, 32, NKEY], W0 + 40)
        sub2 = at("sub2", [P, 32, NKEY], W0 + 56)
        vals = at("vals", [P, 32, TOPK], W0 + 72)
        vidx = at("vidx", [P, 32, TOPK], W0 + 74, U32)
        vidf = at("vidf", [P, 32, TOPK], W0 + 76)
        cand = at("cand", [P, 16, 256], W0)
        cand2 = at("cand2", [P, 16, 256], W0 + 16)
        tops = at("tops", [P, 16, TOPK], W0 + 78)
        tpos = at("tpos", [P, 16, TOPK], W0 + 79, U32)
        tab = at("tab", [P, 2, 16 * TOPK], W0 + 80, U32)
        tabf = at("tabf", [P, 2, 16 * TOPK], W0 + 82)
        eq = at("eq", [P, 8, TOPK, TOPK], W0 + 40)
        sel = at("sel", [P, 3, TT, HK], W0 + 48)
        selT = at("selT", [P, 3, S], W0 + 81)
        oh1 = at("oh1", [P, 2, 8, P], W0)
        oh2 = at("oh2", [P, 2, 8, P], W0 + 8)
        gst = at("gst", [P, NKEY, P], W0 + 17)
        Gb = at("Gb", [P, TT, JB, P], W0)
        Ab = at("Ab", [P, TT, EB], W0 + 4)
        P32 = at("P32", [P, JB, S], W0 + 8)
        Ph = at("Ph", [P, JB, S], W0 + 12, F32R)
        Pl = at("Pl", [P, JB, S], W0 + 16, F32R)
        macc = at("macc", [P, 3, D], W0 + 20)
        mraw = at("mraw", [P, 3, D], W0 + 44)
        mrow = at("mrow", [1, D], W0 + 68)
        gfin = at("gfin", [P, D], W0)
        N3 = at("N3", [P, TT, D], W0)
        mcol = at("mcol", [P, 4, KD], W0 + 84)
        t3 = at("t3", [P, 2, S], W0 + 16)
        QKVU = at("QKVU", [P, TT, 4 * AW], W0)
        G2 = at("G2", [P, TT, 2 * D], W0 + 32)
        gqk = at("gqk", [P, 2, AD], W0 + 85)
        neghalf = at("neghalf", [P, 32], W0 + 86.25)
        sq2 = at("sq2", [P, 2 * AW], 64)
        rt = at("rt", [P, 2, AW], 72)
        rqk = at("rqk", [P, TT, 2 * AW], 80)
        qT2 = at("qT2", [P, AH, S], 64)
        kT2 = at("kT2", [P, AH, S], 72)
        sc2 = at("sc2", [P, 2, 384], W0 + 64)
        pr2 = at("pr2", [P, 2, 384], W0 + 67)
        pT2 = at("pT2", [P, 2, 384], W0 + 70)
        YA = at("YA", [P, TT, AW], W0 + 76)
        uT = at("uT", [P, 8, S], W0)
        ssmB = at("ssmB", [P, 2, STT, GH], W0 + 8)
        ssmC = at("ssmC", [P, 2, STT, GH], W0 + 12)
        cB = at("cB", [P, 2, STT, GH], W0 + 16)
        sv = at("sv", [P, 20, STT], W0 + 64)
        bM = at("bM", [P, 2, SB, P], W0 + 20)
        bL = at("bL", [P, 2, SB, P], W0 + 24)
        cM = at("cM", [P, 2, SB, P], W0 + 28)
        scol = at("scol", [P, 2, SB], W0 + 67)
        ph = at("ph", [P, 2, SB, S], 64)
        cs = at("cs", [P, 2, SB, S], 72)
        rb = at("rb", [P, 2, SB, S], 80)
        rz = at("rz", [P, 2, SB, S], 88)
        yT = at("yT", [P, 8, S], W0 + 68)
        yh = at("yh", [P, 8, S], 64, F32R)
        yl = at("yl", [P, 8, S], 72, F32R)
        SG = at("SG", [P, TT, AW], W0)
        bglu = at("bglu", [1, AW], W0 + 8)
        Y32 = at("Y32", [P, 2, S], W0 + 12)
        yah = at("yah", [P, 8, S], 80, F32R)
        yal = at("yal", [P, 8, S], 88, F32R)
        M2 = at("M2", [P, TT, D], W0)
        btmp = at("btmp", [P, 2, CH], W0 + 16)
        g1b = at("g1b", [P, D], W0 + 20)
        N4 = at("N4", [P, TT, D], W0 + 32)
        t4 = at("t4", [P, 2, S], W0 + 29)
        Y = at("Y", [P, TT, D], W0)
        g2b = at("g2b", [P, D], W0 + 16)
        UP = at("UP", [P, 2, TT, CH], W0 + 32)
        cv = at("cv", [P, 2, 4, S], W0 + 40)
        ccol = at("ccol", [P, 32], W0 + 48)
        sil = at("sil", [P, 4, S], W0 + 50)
        F32t = at("F32t", [P, 4, S], W0 + 54)
        Fh = at("Fh", [P, 4, S], W0 + 58, F32R)
        Fl = at("Fl", [P, 4, S], W0 + 62, F32R)

        ps = ctx.enter_context(nc.psum_tensor("ps", [P, 8, CH], F32)).ap()

        gdram = nc.dram_tensor("gate_scratch", [TT, P, NKEY, P], F32, kind="Internal").ap()
        mdram = nc.dram_tensor("mod_scratch", [2, D], F32, kind="Internal").ap()

        raw_ready = [sem(f"raw_ready{i}") for i in range(RAW)]
        hi_ready = sem("hi_ready")
        lo_ready = sem("lo_ready")
        tile_used = sem("tile_used")
        acc_free = [sem("accA_free"), sem("accB_free")]
        turned = sem("turned")
        turn_hi = sem("turn_hi")
        turn_lo = sem("turn_lo")
        x_in = sem("x_in")
        small_in = sem("small_in")
        var_ready = sem("var_ready")
        rstd_ready = sem("rstd_ready")
        sq_ready = sem("sq_ready")
        normed = sem("normed")
        act_step, dve_step = sem("act_step"), sem("dve_step")
        trig_arg, trig_ok = sem("trig_arg"), sem("trig_ok")
        bias_in, bias_used = sem("bias_in"), sem("bias_used")
        kpe_out = sem("kpe_out")
        ln_in, keys_in = sem("ln_in"), sem("keys_in")
        ln_sum, ln_mu = sem("ln_sum"), sem("ln_mu")
        ln_done, mixed, mixed_out = sem("ln_done"), sem("mixed"), sem("mixed_out")
        kpr_ok, kpt_ps, kpt_ok = sem("kpr_ok"), sem("kpt_ps"), sem("kpt_ok")
        m_evac, m_rope, m_tr = sem("m_evac"), sem("m_rope"), sem("m_tr")
        m_ta, m_tv = sem("m_ta"), sem("m_tv")
        s_ready, s_max, p_ready = sem("s_ready"), sem("s_max"), sem("p_ready")
        pt_ps, pt_ok, o_ready, o_out = sem("pt_ps"), sem("pt_ok"), sem("o_ready"), sem("o_out")
        merged_ok = sem("merged_ok")
        q_out, qt_ps, qt_ok = sem("q_out"), sem("qt_ps"), sem("qt_ok")
        sub_ps, sub_ok = sem("sub_ps"), sem("sub_ok")
        gate_in, gate_exp = sem("gate_in"), sem("gate_exp")
        sel_ok, selT_ps, selT_ok = sem("sel_ok"), sem("selT_ps"), sem("selT_ok")
        oh_ready, g_ps, g_out = ([sem(f"{n}{b}") for b in range(2)] for n in ("oh_ready", "g_ps", "g_out"))
        g_stored = sem("g_stored")
        g_in, gated = sem("g_in"), sem("gated")
        a_ok, a_T, ph_ok, pl_ok = sem("a_ok"), sem("a_T"), sem("ph_ok"), sem("pl_ok")
        v_out = sem("v_out")
        mod_in = [sem(f"mod_in{i}") for i in range(3)]
        mod_used, mod_zero = sem("mod_used"), sem("mod_zero")
        csil = sem("csil")
        bmod_in, mod_ps, mod_row, mod_st = sem("bmod_in"), sem("mod_ps"), sem("mod_row"), sem("mod_st")
        gfin_in, mod_col = sem("gfin_in"), sem("mod_col")
        mcol_ok = sem("mcol_ok")
        in2_out = sem("in2_out")
        qk_sq, qk_rope, qk_tr, qk_out = sem("qk_sq"), sem("qk_rope"), sem("qk_tr"), sem("qk_out")
        ut_ps, ut_ok = sem("ut_ps"), sem("ut_ok")
        ssm_in, sv_a, sv_p, sv_s = sem("ssm_in"), sem("sv_a"), sem("sv_p"), sem("sv_s")
        bm_ok, bl_ps, bl_ok, bu_ps = sem("bm_ok"), sem("bl_ps"), sem("bl_ok"), sem("bu_ps")
        ph_arg, cs_ok, st_ok, y_ps, y_ok = (sem(n) for n in
                                            ("ph_arg", "cs_ok", "st_ok", "y_ps", "y_ok"))
        y_sum = sem("y_sum")
        yspl_h, yspl_l = sem("yspl_h"), sem("yspl_l")
        sg_T, y32_ok, yg_h, yg_l = (sem(n) for n in ("sg_T", "y32_ok", "yg_h", "yg_l"))
        br_out, bglu_in = sem("br_out"), sem("bglu_in")
        g1b_in, g2b_in = sem("g1b_in"), sem("g2b_in")
        up_out, up_T, cv_base, cv_ok, sil_ok, f32_ok, fh_ok, fl_ok, dn_out = (
            sem(n) for n in ("up_out", "up_T", "cv_base", "cv_ok", "sil_ok", "f32_ok", "fh_ok",
                             "fl_ok", "dn_out"))
        cc_ok = sem("cc_ok")
        y_done, o_st = sem("y_done"), sem("o_st")

        PAIRS = [("w_in", 9), ("out", 2), ("pq", 2), ("in2", 8), ("glu", 1), ("abr", 2),
                 ("sbr", 2), ("out2", 2)]
        PB, n = {}, 0
        for name, count in PAIRS:
            PB[name] = n
            n += count

        def heads_rows(ap, h, w):
            return ap.rearrange("p (h w) -> p h w", h=h, w=w)

        block = ctx.enter_context(nc.Block())

        @block.sync
        def _(sp):
            def load(src, n0, off=0, w=TW):
                if n0 >= RAW:
                    sp.wait_ge(lo_ready, n0 - RAW + 1 + off)
                sp.dma_start(raw[:, n0 % RAW, 0:w], src).then_inc(raw_ready[n0 % RAW], 16)

            def tile(name, i):
                if isinstance(i, int):
                    return A[name][i]
                return A[name][bass.ds(i, 1)].rearrange("a p n -> p (a n)")

            def section(name, count):
                n0 = BASE[name]
                with sp.Fori(0, count // 4) as it:
                    for j in range(4):
                        load(tile(name, it * 4 + j), n0 + j, it * 4)

            sp.dma_start(X[:], A["x"]).then_inc(x_in, 16)
            for j in range(4):
                load(tile("w_in", j), j)
            with sp.Fori(1, 10) as it:
                for j in range(4):
                    load(tile("w_in", it * 4 + j), j + 4, it * 4 - 4)
            with sp.Fori(0, 4) as it:
                sp.wait_ge(bias_used, it)
                sp.dma_start(brow[:], A["b_gate"][bass.ds(it, 1), :]).then_inc(bias_in, 16)
                for j in range(8):
                    load(tile("w_in", it * 8 + (40 + j)), 40 + j, it * 8)
            load(A["kpe"], BASE["kpe"], w=KD * ROPE)
            with sp.Fori(0, 4) as it:
                for j in range(4):
                    n0 = BASE["mla"] + j
                    if j == 1:
                        load(A["mla_r"][bass.ds(it, 1)].rearrange("a p n -> p (a n)"), n0, it * 4, TW // 2)
                    else:
                        load(tile("mla", it * 3 + (j if j == 0 else j - 1)), n0, it * 4)
            section("out", 16)
            section("pq", 16)
            n0 = BASE["peer"]

            def up(b, n, off=0):
                for j in range(4):
                    load(tile("peer_u", b * 4 + j), n + j, off)

            def down(b, n, off=0):
                for j in range(4):
                    load(tile("peer_v", b * 4 + j), n + j, off)

            def mod(k, half, done):
                for j in range(3):
                    if not isinstance(done, int) or done:
                        sp.wait_ge(mod_used, done * 3 - 2 + j)
                    sp.dma_start(mraw[:, j], A["w_mod"][3 * half + j, bass.ds(k * P, P) if not isinstance(k, int)
                                                        else slice(k * P, k * P + P)]).then_inc(mod_in[j], 16)

            def gates(b):
                if not isinstance(b, int) or b:
                    sp.wait_ge(gated, b * 2)
                for t in range(TT):
                    sp.dma_start(Gb[:, t], gdram[t, :, bass.ds(b * JB, JB)]).then_inc(g_in, 16)

            up(0, n0)
            sp.wait_ge(g_stored, 32)
            mod(0, 0, 0)
            gates(0)
            with sp.Fori(1, 16) as b:
                up(b, n0 + 4, b * 8 - 8)
                mod(b, 0, b)
                down(b - 1, n0 + 8, b * 8 - 8)
                gates(b)
            with sp.Fori(16, 32) as b:
                up(b, n0 + 4, b * 8 - 8)
                mod(b - 16, 1, b)
                down(b - 1, n0 + 8, b * 8 - 8)
                gates(b)
            down(NBLK - 1, n0 + 8 * NBLK - 4)
            section("in2", 64)
            section("glu", 4)
            section("abr", 8)
            section("sbr", 8)
            section("out2", 16)
            n0 = BASE["ffn"]

            def ups(b, n, off=0):
                for j in range(8):
                    load(tile("w_up", b * 8 + j), n + j, off)

            def downs(b, n, off=0):
                for j in range(4):
                    load(tile("w_down", b * 4 + j), n + j, off)

            ups(0, n0)
            with sp.Fori(1, FB) as b:
                ups(b, n0 + 8, b * 12 - 12)
                downs(b - 1, n0 + 16, b * 12 - 12)
            downs(FB - 1, n0 + 12 * FB - 4)

        @block.gpsimd
        def _(pool):
            pool.dma_start(const[:], A["const"]).then_inc(small_in, 16)
            pool.dma_start(cols[:], A["cols"]).then_inc(small_in, 16)
            pool.dma_start(posi[:], A["pos"]).then_inc(small_in, 16)
            pool.dma_start(wsp[:], A["w_spatial"]).then_inc(small_in, 16)
            GP.memset(neghalf[:], -0.5).then_inc(mod_zero, 1)
            count = [0]
            pool.wait_ge(mod_zero, 1)

            def inverse_root(off, n):
                count[0] += 1
                pool.wait_ge(var_ready, count[0])
                GP.tensor_tensor(stat[:, off + n:off + 2 * n], stat[:, off:off + n], neghalf[:, 0:n],
                                 ALU.pow).then_inc(rstd_ready, 1)

            inverse_root(0, 2)
            pool.wait_ge(tile_used, BASE["kpe"] + 1)
            pool.dma_start(lng[:], A["sgu_ln_g"].partition_broadcast(P)).then_inc(ln_in, 16)
            pool.dma_start(lnb[:], A["sgu_ln_b"].partition_broadcast(P)).then_inc(ln_in, 16)
            inverse_root(0, 2)
            inverse_root(0, 4)
            pool.wait_ge(turn_lo, TBASE["merged"] + 8)
            pool.dma_start(keys[:], A["peer_keys"]).then_inc(keys_in, 16)
            inverse_root(0, 2)
            for half in range(2):
                pool.wait_ge(mod_zero, 2 + half)
                pool.dma_start(macc[0:1].rearrange("a j n -> a (j n)"), A["b_mod"][half:half + 1, :]
                               ).then_inc(bmod_in, 16)
                pool.wait_ge(mod_row, 4 * half + 4)
                pool.dma_start(mdram[half:half + 1, :], mrow[:]).then_inc(mod_st, 16)
            pool.wait_ge(mod_st, 32)
            pool.wait_ge(v_out, 8 * NBLK)
            pool.dma_start(gfin[:], A["g_final"].partition_broadcast(P)).then_inc(gfin_in, 16)
            inverse_root(0, 2)
            inverse_root(0, 2)
            pool.dma_start(gqk[:, 0], A["q_norm_g"].partition_broadcast(P)).then_inc(gfin_in, 16)
            pool.dma_start(gqk[:, 1], A["k_norm_g"].partition_broadcast(P)).then_inc(gfin_in, 16)
            inverse_root(0, 32)
            pool.wait_ge(ut_ok, 4)
            for i, n in enumerate(("ssm_b_re", "ssm_b_im")):
                pool.dma_start(ssmB[:, i], A[n]).then_inc(ssm_in, 16)
            for i, n in enumerate(("ssm_c_re", "ssm_c_im")):
                pool.dma_start(ssmC[:, i], A[n]).then_inc(ssm_in, 16)
            pool.wait_ge(sv_a, 1)
            GP.tensor_tensor(sv[:, 1], sv[:, 0], C("ldt", 0, STT), ALU.pow).then_inc(sv_p, 1)
            pool.wait_ge(sv_a, 2)
            GP.tensor_tensor(sv[:, 4], sv[:, 0], sv[:, 3], ALU.pow).then_inc(sv_p, 1)
            pool.wait_ge(yspl_l, 1)
            pool.dma_start(bglu[:], A["b_glu"]).then_inc(bglu_in, 16)
            pool.wait_ge(yg_l, 4)
            pool.dma_start(g1b[:], mdram[0].partition_broadcast(P)).then_inc(g1b_in, 16)
            inverse_root(0, 2)
            pool.wait_ge(normed, 14)
            pool.dma_start(g2b[:], mdram[1].partition_broadcast(P)).then_inc(g2b_in, 16)

        @block.scalar
        def _(act):
            st = Steps(act, act_step)

            def split(n0, off=0):
                if n0 >= TOTAL:
                    return
                act.wait_ge(raw_ready[n0 % RAW], 16 * (n0 // RAW + 1) + off * 4)
                if n0 >= SPL:
                    act.wait_ge(tile_used, n0 - SPL + 1 + off)
                SC.copy(hi[:, n0 % SPL], raw[:, n0 % RAW]).then_inc(hi_ready, 1)

            def splits(n0, count, off=0):
                for j in range(count):
                    split(n0 + SPL + j, off)

            squares = [0]

            def sumsq(junk, src, accum, bias=0.0):
                if squares[0]:
                    act.wait_ge(sq_ready, squares[0])
                squares[0] += 1
                SC.activation(junk, src, ACT.Square, bias=bias, accum_out=accum).then_inc(sq_ready, 1)

            def turn(name, rounds, h, scale=None, bias=None, after=None):
                for r in range(rounds):
                    g = TBASE[name] + r
                    act.wait_ge(turned, g + 1)
                    bank = ps[:, 4 + g % 2].rearrange("p (k t) -> p k t", k=2)
                    if r == 0 and after is not None:
                        act.wait_ge(tile_used, after)
                    for k in range(2):
                        kk = 2 * r + k
                        if scale is None:
                            if k == 0:
                                SC.copy(h[:, kk:kk + 2], bank).then_inc(turn_hi, 2)
                        elif bias is None:
                            SC.activation(h[:, kk], bank[:, k], ACT.Copy, scale=scale(kk)).then_inc(turn_hi, 1)
                        else:
                            SC.activation(h[:, kk], bank[:, k], ACT.Identity, scale=scale(kk),
                                          bias=bias(kk)).then_inc(turn_hi, 1)

            act.wait_ge(x_in, 16)
            for t in range(TT):
                sumsq(junk[:], X[:, t], stat[:, 8 + t:9 + t])
            split(0)
            split(1)
            act.wait_ge(trig_arg, 1)
            SC.activation(trig[:], ang[:, 4:6], ACT.Sin).then_inc(trig_ok, 1)
            act.wait_ge(small_in, 64)
            turn("h1", 8, xh, scale=lambda k: C("g1", k))
            def evac(pair, ab, dst, func, off=0, pinc=None):
                act.wait_ge(tile_used, pair)
                for t in range(TT):
                    SC.activation(dst(t), ps[:, 2 * ab + t], func).then_inc(acc_free[ab], 1)

            splits(0, 4)
            evac(4, 0, lambda t: CQ[:, t], ACT.Copy)
            splits(4, 4)
            evac(8, 1, lambda t: CKV[:, t], ACT.Copy)
            with act.Fori(0, 4) as it:
                for ab in range(2):
                    splits(8 + 4 * ab, 4, it * 8)
                    evac(it * 8 + (12 + 4 * ab), ab,
                         lambda t: Z[:, t, bass.ds(it * 1024 + 512 * ab, CH)], ACT.Gelu_apprx_tanh)
            with act.Fori(0, 4) as it:
                for ab in range(2):
                    splits(40 + 4 * ab, 4, it * 8)
                    evac(it * 8 + (44 + 4 * ab), ab,
                         lambda t: GT[:, t, bass.ds(it * 1024 + 512 * ab, CH)], ACT.Sigmoid)
            split(BASE["kpe"] + SPL)
            act.wait_ge(tile_used, BASE["kpe"] + 1)
            for t in range(TT):
                SC.copy(KPE[:, t], ps[:, t, 0:ROPE]).then_inc(kpe_out, 1)
            act.wait_ge(acc_free[1], 18)
            act.wait_ge(bias_used, 4)
            for t in range(TT):
                if t:
                    act.wait_ge(ln_sum, t)
                SC.activation(junk2[:], Z[:, t, D:2 * D], ACT.Copy, accum_out=stat[:, 16 + t:17 + t]
                              ).then_inc(ln_sum, 1)
            act.wait_ge(ln_sum, 2)
            act.wait_ge(ln_mu, 1)
            for t in range(TT):
                sumsq(junk2[:], Z[:, t, D:2 * D], stat[:, 8 + t:9 + t], stat[:, 18 + t:19 + t])
            for j, src in enumerate((CQ, CKV)):
                for t in range(TT):
                    sumsq(junk2[:, 0:LORA], src[:, t], stat[:, 10 + 2 * j + t:11 + 2 * j + t])
            turn("cq", 2, cqh, scale=lambda k: C("gqa", k))
            turn("ckv", 2, ckh, scale=lambda k: C("gkva", k))
            act.wait_ge(kpt_ps, 1)
            SC.copy(KPT[:], ps[:, 6, 0:S]).then_inc(kpt_ok, 1)

            def probs(h, s, p, stats, off=0):
                act.wait_ge(s_max, h + 1 + off)
                b, q = h % 2, h % 4
                if h >= 2 or not isinstance(off, int):
                    act.wait_ge(pt_ps, max(h - 1, 0) + off)
                SC.activation(p[:, b, 0:P], s[:, b, 0:P], ACT.Exp, bias=stats(q, 0),
                              accum_out=stats(q, 2)).then_inc(p_ready, 1)
                SC.activation(p[:, b, P:384], s[:, b, P:384], ACT.Exp, bias=stats(q, 1),
                              accum_out=stats(q, 3)).then_inc(p_ready, 1)

            def probsT(h, dst, bank, off=0):
                act.wait_ge(pt_ps, h + 1 + off)
                if h >= 2 or not isinstance(off, int):
                    act.wait_ge(o_ready, max(h - 1, 0) + off)
                SC.copy(dst[:, h % 2], ps[:, bank, 0:384]).then_inc(pt_ok, 1)

            def stat_col(q, i):
                return stat[:, 32 + 4 * q + i:33 + 4 * q + i]

            with act.Fori(0, 4) as it:
                n0 = BASE["mla"]
                for j, (dst, w) in enumerate(((qn, CH), (qr, GROUP * ROPE), (kn, CH), (vv, CH))):
                    split(n0 + j + SPL, it * 4)
                    act.wait_ge(tile_used, it * 4 + (n0 + j + 1))
                    if j == 0:
                        act.wait_ge(m_tr, it * 3)
                    if j == 3:
                        act.wait_ge(o_ready, it * 4)
                    for t in range(TT):
                        SC.copy(dst[:, t], ps[:, 2 * j + t, 0:w]).then_inc(m_evac, 1)
                act.wait_ge(m_tr, it * 3 + 1)
                act.wait_ge(s_ready, it * 4)
                SC.copy(qT[:].rearrange("p h t -> p (h t)"), ps[:, 0:2].rearrange("p a n -> p (a n)")
                        ).then_inc(m_ta, 1)
                act.wait_ge(m_tr, it * 3 + 3)
                SC.copy(qrT[:].rearrange("p h t -> p (h t)"), ps[:, 4]).then_inc(m_ta, 1)
                for h in range(GROUP + 1):
                    if h < GROUP:
                        probs(h, sc, pr, stat_col, it * 4)
                    if h >= 1:
                        probsT(h - 1, pT, (4, 7)[(h - 1) % 2], it * 4)
            turn("merged", 8, xh, after=BASE["out"])
            splits(BASE["out"], 16)
            act.wait_ge(acc_free[1], 22)
            for t in range(TT):
                sumsq(junk2[:], X[:, t], stat[:, 8 + t:9 + t])
            turn("h2", 8, xh, scale=lambda k: C("g2", k), after=BASE["pq"])
            for pair in range(2):
                for ab in range(2):
                    splits(BASE["pq"] + 8 * pair + 4 * ab, 4)
                    evac(BASE["pq"] + 8 * pair + 4 * ab + 4, ab,
                         lambda t: Q[:, t, 1024 * pair + 512 * ab:1024 * pair + 512 * ab + CH], ACT.Copy)
            for g in range(8):
                act.wait_ge(qt_ps, g + 1)
                SC.copy(QT[:, 2 * g:2 * g + 2], ps[:, 4 + g % 2].rearrange("p (k t) -> p k t", k=2)
                        ).then_inc(qt_ok, 1)
            for g in range(8):
                act.wait_ge(sub_ps, g + 1)
                SC.copy(sub[:, 4 * g:4 * g + 4].rearrange("p a n -> p (a n)"), ps[:, 4 + g % 4]
                        ).then_inc(sub_ok, 1)
            act.wait_ge(gate_in, 1)
            SC.activation(sel[:, 2], sel[:, 2], ACT.Exp).then_inc(gate_exp, 1)
            act.wait_ge(selT_ps, 1)
            act.wait_ge(sel_ok, 1)
            for i in range(3):
                SC.copy(selT[:, i], ps[:, 4 + i, 0:S]).then_inc(selT_ok, 1)
            for t in range(TT):
                if t:
                    act.wait_ge(g_stored, 16)
                with act.Fori(0, 8) as it:
                    for b in range(2):
                        act.wait_ge(g_ps[b], it + (1 + 8 * t))
                        SC.copy(gst[:, :, bass.ds(it * 16 + 8 * b, 8)],
                                ps[:, 4 + 2 * b:6 + 2 * b].rearrange("p a (k j) -> p j (a k)", k=4)
                                ).then_inc(g_out[b], 1)
                for b in range(2):
                    act.wait_ge(g_out[b], 8 * (t + 1))
                act.dma_start(gdram[t], gst[:]
                              ).then_inc(g_stored, 16)
            act.wait_ge(small_in, 64)
            SC.activation(stat[:, 64:80], C("c", 0, KD), ACT.Silu).then_inc(csil, 1)

            def act_block(b):
                act.wait_ge(tile_used, b * 8 + (BASE["peer"] + (4 if isinstance(b, int) else 0)))
                if not isinstance(b, int):
                    act.wait_ge(a_T, b)
                for t in range(TT):
                    SC.activation(Ab[:, t], ps[:, t], ACT.Gelu_apprx_tanh).then_inc(a_ok, 1)

            def act_high(b):
                act.wait_ge(gated, b * 2 + 2)
                if not isinstance(b, int) or b:
                    act.wait_ge(tile_used, b * 8 + BASE["peer"])
                SC.copy(Ph[:], P32[:]).then_inc(ph_ok, 1)

            n0 = BASE["peer"]
            splits(n0, 4)
            act_block(0)

            def mod_out(half):
                act.wait_ge(mod_ps, half * 2 + 1)
                SC.copy(mcol[:, 2 * half:2 * half + 2].rearrange("p j k -> p (j k)"), ps[:, 0, 0:2 * KD]
                        ).then_inc(mod_col, 1)
                act.wait_ge(mod_ps, half * 2 + 2)
                if half:
                    act.wait_ge(mod_st, 16)
                for q in range(4):
                    SC.copy(mrow[0:1, CH * q:CH * q + CH], ps[0:1, 4 + q]).then_inc(mod_row, 1)

            def act_loop(lo_, hi_):
                with act.Fori(lo_, hi_) as b:
                    off = b * 8 - 8
                    split(n0 + 6, off)
                    split(n0 + 7, off)
                    act_high(b - 1)
                    split(n0 + 8, off)
                    split(n0 + 9, off)
                    act_block(b)
                    for j in range(10, 14):
                        split(n0 + j, off)

            act_loop(1, 16)
            mod_out(0)
            act_loop(16, 32)
            mod_out(1)
            act_high(NBLK - 1)
            n0 = BASE["in2"] - 4
            splits(n0, 4)
            act.wait_ge(v_out, 8 * NBLK)
            for t in range(TT):
                sumsq(junk2[:], X[:, t], stat[:, 8 + t:9 + t])
            act.wait_ge(normed, 10)
            for t in range(TT):
                sumsq(junk2[:], X[:, t], stat[:, 8 + t:9 + t])
            act.wait_ge(mcol_ok, 1)
            turn("h3", 8, xh, scale=lambda k: mcol[:, 1, k:k + 1], bias=lambda k: mcol[:, 0, k:k + 1],
                 after=BASE["in2"])
            with act.Fori(0, 4) as it:
                for ab in range(2):
                    splits(BASE["in2"] + 4 * ab, 4, it * 8)
                    evac(it * 8 + (BASE["in2"] + 4 + 4 * ab), ab,
                         lambda t: QKVU[:, t, bass.ds(it * 1024 + 512 * ab, CH)], ACT.Copy)
            with act.Fori(0, 4) as it:
                for ab in range(2):
                    splits(BASE["in2"] + 32 + 4 * ab, 4, it * 8)
                    evac(it * 8 + (BASE["in2"] + 36 + 4 * ab), ab,
                         lambda t: G2[:, t, bass.ds(it * 1024 + 512 * ab, CH)], ACT.Sigmoid)
            act.wait_ge(acc_free[1], 2 * (PB["in2"] + 8))
            act.wait_ge(tile_used, BASE["glu"])
            for t in range(TT):
                if t:
                    act.wait_ge(qk_sq, 2)
                SC.activation(sq2[:], QKVU[:, t, 0:2 * AW], ACT.Square).then_inc(qk_sq, 1)
            for g in range(8):
                act.wait_ge(qk_tr, g + 1)
                src = ps[:, 4 + g % 2].rearrange("p (k t) -> p k t", k=2)
                dst = (qT2, kT2)[g // 4][:, 2 * (g % 4):2 * (g % 4) + 2]
                if g == 0:
                    act.wait_ge(qk_rope, 2)
                SC.copy(dst, src).then_inc(qk_out, 1)
            for h in range(AH + 1):
                if h < AH:
                    probs(h + 16, sc2, pr2, stat_col)
                if h >= 1:
                    probsT(h + 15, pT2, (4, 7)[(h - 1) % 2])
            for g in range(4):
                act.wait_ge(ut_ps, g + 1)
                SC.copy(uT[:, 2 * g:2 * g + 2], ps[:, 4 + g % 2].rearrange("p (k t) -> p k t", k=2)
                        ).then_inc(ut_ok, 1)
            act.wait_ge(sv_a, 3)
            SC.activation(sv[:, 8:10], sv[:, 6:8], ACT.Sin).then_inc(sv_s, 1)
            with act.Fori(0, 8) as it:
                act.wait_ge(bl_ps, it * 2 + 1)
                for i in range(2):
                    act.wait_ge(bl_ps, it * 2 + (i + 1))
                    SC.copy(bL[:, i].rearrange("p s n -> p (s n)"), ps[:, 6 + i]).then_inc(bl_ok, 1)
                act.wait_ge(ph_arg, it + 1)
                SC.activation(cs[:], ph[:], ACT.Sin, scale=TURN).then_inc(cs_ok, 1)
                act.wait_ge(y_sum, it + 1)
                SC.activation(yT[:, bass.ds(it, 1)].rearrange("p a t -> p (a t)"),
                              yT[:, bass.ds(it, 1)].rearrange("p a t -> p (a t)"),
                              ACT.Gelu_apprx_tanh).then_inc(y_ok, 1)
            act.wait_ge(y_ok, 8)
            act.wait_ge(st_ok, 16)
            SC.copy(yh[:], yT[:]).then_inc(yspl_h, 1)
            splits(BASE["glu"], 2)
            evac(BASE["glu"] + 2, 0, lambda t: SG[:, t, 0:CH], ACT.Sigmoid)
            splits(BASE["glu"] + 2, 2)
            evac(BASE["glu"] + 4, 1, lambda t: SG[:, t, CH:2 * CH], ACT.Sigmoid)
            for g in range(4):
                act.wait_ge(y32_ok, g + 1)
                SC.copy(yh[:, 2 * g:2 * g + 2], Y32[:]).then_inc(yg_h, 1)
            turn("ya", 4, yah, after=BASE["abr"])
            splits(BASE["abr"], 8)
            splits(BASE["sbr"], 8)
            turn("merged2", 8, xh, after=BASE["out2"])
            splits(BASE["out2"], 16)
            act.wait_ge(acc_free[1], 2 * (PB["out2"] + 2))
            for t in range(TT):
                sumsq(junk2[:], X[:, t], stat[:, 8 + t:9 + t])
            act.wait_ge(mcol_ok, 2)
            turn("h4", 8, xh, scale=lambda k: mcol[:, 3, k:k + 1], bias=lambda k: mcol[:, 2, k:k + 1],
                 after=BASE["ffn"])

            n0 = BASE["ffn"]

            def up_evac(b, half, n):
                act.wait_ge(tile_used, n)
                if half == 0 and (not isinstance(b, int) or b):
                    act.wait_ge(up_T, b * 2)
                for t in range(TT):
                    SC.copy(UP[:, half, t], ps[:, 2 * half + t]).then_inc(up_out, 1)

            def conv_base(b):
                act.wait_ge(cc_ok, b + 1)
                for half in range(2):
                    act.wait_ge(up_T, b * 2 + (half + 1))
                    for f in range(4):
                        q = 16 * half + 4 * f
                        SC.activation(cv[:, half, f], ps[:, 4 + 2 * half + f // 2, S * (f % 2):S * (f % 2) + S],
                                      ACT.Identity, scale=ccol[:, q + 2:q + 3], bias=ccol[:, q + 3:q + 4]
                                      ).then_inc(cv_base, 1)
                act.wait_ge(cv_ok, b * 2 + 2)
                SC.activation(sil[:], cv[:, 1], ACT.Silu).then_inc(sil_ok, 1)
                act.wait_ge(f32_ok, b + 1)
                if not isinstance(b, int) or b:
                    act.wait_ge(tile_used, b * 12 + n0)
                SC.copy(Fh[:], F32t[:]).then_inc(fh_ok, 1)

            splits(n0, 4)
            up_evac(0, 0, n0 + 4)
            splits(n0 + 4, 4)
            up_evac(0, 1, n0 + 8)
            with act.Fori(1, FB) as b:
                off = b * 12 - 12
                split(n0 + 10, off)
                split(n0 + 11, off)
                conv_base(b - 1)
                split(n0 + 12, off)
                split(n0 + 13, off)
                up_evac(b, 0, b * 12 + n0)
                splits(n0 + 12, 4, off)
                up_evac(b, 1, b * 12 + (n0 + 4))
                splits(n0 + 16, 4, off)
            conv_base(FB - 1)
            splits(TOTAL - 4, 4)
            for t in range(TT):
                act.wait_ge(y_done, t + 1)
                act.dma_start(out[t * P:(t + 1) * P, :], Y[:, t]).then_inc(o_st, 16)
            act.wait_ge(o_st, 32)

        @block.vector
        def _(dve):
            st = Steps(dve, dve_step)

            def split(n0, off=0):
                if n0 >= TOTAL:
                    return
                dve.wait_ge(hi_ready, n0 + 1 + off)
                V.tensor_tensor(lo[:, n0 % SPL], raw[:, n0 % RAW], hi[:, n0 % SPL].bitcast(F32),
                                ALU.subtract).then_inc(lo_ready, 1)

            def splits(n0, count, off=0):
                for j in range(count):
                    split(n0 + SPL + j, off)

            nroot = [0]
            nsq = [0]

            def mean_sq(n, width, sqs):
                nsq[0] += sqs
                dve.wait_ge(sq_ready, nsq[0])
                nroot[0] += 1
                V.tensor_scalar(stat[:, 0:n], stat[:, 8:8 + n], 1.0 / width, EPS, ALU.mult, ALU.add
                                ).then_inc(var_ready, 1)
                dve.wait_ge(rstd_ready, nroot[0])

            def turn(name, rounds, h, l, scale=None, bias=None, tmp=None):
                for r in range(rounds):
                    g = TBASE[name] + r
                    dve.wait_ge(turn_hi, 2 * g + 2)
                    bank = ps[:, 4 + g % 2].rearrange("p (k t) -> p k t", k=2)
                    kk = 2 * r
                    if scale is None:
                        V.tensor_tensor(l[:, kk:kk + 2], bank, h[:, kk:kk + 2].bitcast(F32), ALU.subtract
                                        ).then_inc(turn_lo, 1)
                        continue
                    if bias is not None:
                        if r:
                            dve.wait_ge(turn_lo, g)
                        for k in range(2):
                            st.step(V.tensor_scalar(tmp[:, k], bank[:, k], scale(kk + k), bias(kk + k),
                                                    ALU.mult, ALU.add))
                        st.wait()
                        V.tensor_tensor(l[:, kk:kk + 2], tmp[:], h[:, kk:kk + 2].bitcast(F32), ALU.subtract
                                        ).then_inc(turn_lo, 1)
                        continue
                    st.step(V.scalar_tensor_tensor(l[:, kk], bank[:, 0], scale(kk), h[:, kk].bitcast(F32),
                                                   ALU.mult, ALU.subtract))
                    V.scalar_tensor_tensor(l[:, kk + 1], bank[:, 1], scale(kk + 1), h[:, kk + 1].bitcast(F32),
                                           ALU.mult, ALU.subtract).then_inc(turn_lo, 1)

            dve.wait_ge(small_in, 64)
            st.link(V.tensor_copy(posf[:], posi[:]))
            for t in range(TT):
                st.step(V.tensor_scalar(ang[:, 0, 32 * t:32 * t + 32], K("freq"), posf[:, t:t + 1], None, ALU.mult))
                st.step(V.tensor_scalar(ang[:, 0, 64 + 64 * t:128 + 64 * t], K("freq2"), posf[:, 2 + t:3 + t],
                                        None, ALU.mult))
            st.wait()
            st.step(V.tensor_scalar(ang[:, 2], ang[:, 0], INV_2PI, None, ALU.mult))
            st.link(V.tensor_scalar(ang[:, 3], ang[:, 0], INV_2PI, 0.25, ALU.mult, ALU.add))
            st.link(V.tensor_scalar(ang[:, 2:4], ang[:, 2:4], MAGIC, None, ALU.add))
            st.link(V.tensor_scalar(ang[:, 2:4], ang[:, 2:4], MAGIC, None, ALU.subtract))
            both = ang[:, 0:1].to_broadcast([P, 2, 192])
            st.link(V.scalar_tensor_tensor(ang[:, 4:6], ang[:, 2:4], -C1, both, ALU.mult, ALU.add))
            st.link(V.scalar_tensor_tensor(ang[:, 4:6], ang[:, 2:4], -C2, ang[:, 4:6], ALU.mult, ALU.add))
            st.link(V.scalar_tensor_tensor(ang[:, 4:6], ang[:, 2:4], -C3, ang[:, 4:6], ALU.mult, ALU.add))
            st.link(V.tensor_scalar(ang[:, 5], ang[:, 5], math.pi / 2, None, ALU.add))
            V.tensor_scalar(ang[:, 4:6], ang[:, 4:6], PI_IN, -PI_IN, ALU.min, ALU.max).then_inc(trig_arg, 1)
            mean_sq(2, D, 2)
            for t in range(TT):
                V.tensor_scalar(N1[:, t], X[:, t], stat[:, 2 + t:3 + t], None, ALU.mult).then_inc(normed, 1)
            split(0)
            split(1)
            turn("h1", 8, xh, xl, scale=lambda k: C("g1", k))
            splits(0, 8)
            with dve.Fori(0, 8) as it:
                splits(8, 8, it * 8)
            split(BASE["kpe"] + SPL)
            st.link(V.tensor_tensor(wsp[:], wsp[:], K("triu").unsqueeze(1).to_broadcast([P, SGU_G, P]), ALU.mult))
            dve.wait_ge(ln_sum, 2)
            V.tensor_scalar(stat[:, 18:20], stat[:, 16:18], -1.0 / D, None, ALU.mult).then_inc(ln_mu, 1)
            mean_sq(2, D, 2)
            dve.wait_ge(ln_in, 32)
            for t in range(TT):
                v = Z[:, t, D:2 * D]
                st.link(V.tensor_scalar(v, v, stat[:, 18 + t:19 + t], stat[:, 2 + t:3 + t], ALU.add, ALU.mult))
                st.link(V.tensor_tensor(v, v, lng[:], ALU.mult))
                V.tensor_tensor(v, v, lnb[:], ALU.add).then_inc(ln_done, 1)
            nsq[0] += 4
            dve.wait_ge(sq_ready, nsq[0])
            nroot[0] += 1
            V.tensor_scalar(stat[:, 0:4], stat[:, 10:14], 1.0 / LORA, EPS, ALU.mult, ALU.add).then_inc(var_ready, 1)
            dve.wait_ge(rstd_ready, nroot[0])
            for j, src in enumerate((CQ, CKV)):
                for t in range(TT):
                    V.tensor_scalar(src[:, t], src[:, t], stat[:, 4 + 2 * j + t:5 + 2 * j + t], None, ALU.mult
                                    ).then_inc(normed, 1)
            dve.wait_ge(kpe_out, 2)
            dve.wait_ge(trig_ok, 1)

            def rope32(dst, src, tmp, nh, done=None):
                for t in range(TT):
                    sn = trig[:, 0, 32 * t:32 * t + 32].unsqueeze(1).to_broadcast([P, nh, 32])
                    cn = trig[:, 1, 32 * t:32 * t + 32].unsqueeze(1).to_broadcast([P, nh, 32])
                    s4 = src[:, t].rearrange("p (h b w) -> p h b w", h=nh, b=2)
                    d4 = dst(t)
                    t4_ = tmp[:, t].rearrange("p (h w) -> p h w", h=nh)
                    st.step(V.tensor_tensor(d4[:, :, 0], s4[:, :, 0], cn, ALU.mult))
                    st.link(V.tensor_tensor(t4_, s4[:, :, 1], sn, ALU.mult))
                    st.link(V.tensor_tensor(d4[:, :, 0], d4[:, :, 0], t4_, ALU.subtract))
                    st.step(V.tensor_tensor(d4[:, :, 1], s4[:, :, 0], sn, ALU.mult))
                    st.link(V.tensor_tensor(t4_, s4[:, :, 1], cn, ALU.mult))
                    last = V.tensor_tensor(d4[:, :, 1], d4[:, :, 1], t4_, ALU.add)
                    if done is None:
                        st.link(last)
                    else:
                        last.then_inc(done, 1)

            rope32(lambda t: KPR[:, t, 0:64].rearrange("p (h b w) -> p h b w", h=1, b=2), KPE,
                   ktmp[:, :, 0:32], 1)
            for t in range(TT):
                V.tensor_copy(KPR[:, t, 64:128], KPR[:, t, 0:64]).then_inc(kpr_ok, 1)
            for t in range(TT):
                for g in range(SGU_G):
                    dve.wait_ge(mixed, t * 4 + g // 2 + 1)
                    u = Z[:, t, g * SGU_W:(g + 1) * SGU_W]
                    bank = ((4, 5, 6, 7), (0, 1, 2, 3))[t][g // 2]
                    V.scalar_tensor_tensor(u, ps[:, bank, SGU_W * (g % 2):SGU_W * (g % 2) + SGU_W],
                                           C("bsp", g), u, ALU.add, ALU.mult).then_inc(mixed_out, 1)
                dve.wait_ge(mixed_out, 8 * (t + 1))
                st.link(V.tensor_tensor(GT[:, t, D:2 * D], GT[:, t, D:2 * D], Z[:, t, 0:D], ALU.mult))
            turn("cq", 2, cqh, cql, scale=lambda k: C("gqa", k))
            turn("ckv", 2, ckh, ckl, scale=lambda k: C("gkva", k))

            def soft_in(h, s, bank, scale, off=0):
                b, q = h % 2, h % 4
                dve.wait_ge(s_ready, h + 1 + off)
                if h >= 2 or not isinstance(off, int):
                    dve.wait_ge(p_ready, 2 * max(h - 1, 0) + off * 2)
                st.link(V.scalar_tensor_tensor(s[:, b], ps[:, bank, 0:384], scale, K("mask"), ALU.mult, ALU.add))
                st.step(V.tensor_reduce(stat[:, 144 + 2 * b:145 + 2 * b], s[:, b, 0:P], AX, ALU.max))
                st.link(V.tensor_reduce(stat[:, 145 + 2 * b:146 + 2 * b], s[:, b, P:384], AX, ALU.max))
                V.tensor_scalar(stat[:, 32 + 4 * q:34 + 4 * q], stat[:, 144 + 2 * b:146 + 2 * b], -1.0, None, ALU.mult
                                ).then_inc(s_max, 1)

            def soft_out(h, bank, dst, other, off=0):
                b, q = h % 2, h % 4
                dve.wait_ge(p_ready, 2 * h + 2 + off * 2)
                st.link(V.reciprocal(stat[:, 148 + 2 * b:150 + 2 * b], stat[:, 34 + 4 * q:36 + 4 * q]))
                dve.wait_ge(o_ready, h + 1 + off)
                for t in range(TT):
                    o = ps[:, bank, P * t:P * t + P]
                    r = stat[:, 148 + 2 * b + t:149 + 2 * b + t]
                    if other is None:
                        V.tensor_scalar(dst(t), o, r, None, ALU.mult).then_inc(o_out, 1)
                    else:
                        V.scalar_tensor_tensor(dst(t), o, r, other(t), ALU.mult, ALU.mult).then_inc(o_out, 1)

            PER = 10 + 16
            with dve.Fori(0, 4) as it:
                st.enter(PER, it)
                n0 = BASE["mla"]
                for j in range(4):
                    split(n0 + j + SPL, it * 4)
                dve.wait_ge(m_evac, it * 8 + 4)
                dve.wait_ge(m_tr, it * 3)
                rope32(lambda t: qrr[:, t].rearrange("p (h b w) -> p h b w", h=GROUP, b=2), qr, qtmp, GROUP, m_rope)
                dve.wait_ge(m_tr, it * 3 + 2)
                dve.wait_ge(s_ready, it * 4)
                V.tensor_copy(kT[:].rearrange("p h t -> p (h t)"), ps[:, 2:4].rearrange("p a n -> p (a n)")
                              ).then_inc(m_tv, 1)
                for h in range(GROUP + 2):
                    if h < GROUP:
                        soft_in(h, sc, 5 + h % 2, float(NOPE + ROPE) ** -0.5, it * 4)
                    if h >= 2:
                        g = h - 2
                        dst = lambda t: GT[:, t, bass.ds(it * CH + g * VH, VH)]
                        soft_out(g, g % 2, dst, dst, it * 4)
                st.leave(PER, 4)
            dve.wait_ge(o_out, 32)
            for t in range(TT):
                V.tensor_tensor(GT[:, t, 0:D], GT[:, t, 0:D], GT[:, t, D:2 * D], ALU.add).then_inc(merged_ok, 1)
            turn("merged", 8, xh, xl)
            for pair in range(2):
                for ab in range(2):
                    n = BASE["out"] + 8 * pair + 4 * ab
                    splits(n, 4)
                    dve.wait_ge(tile_used, n + 4)
                    for t in range(TT):
                        xs = X[:, t, 1024 * pair + 512 * ab:1024 * pair + 512 * ab + CH]
                        V.tensor_tensor(xs, xs, ps[:, 2 * ab + t], ALU.add).then_inc(acc_free[ab], 1)
            dve.wait_ge(acc_free[0], 22)
            dve.wait_ge(acc_free[1], 22)
            mean_sq(2, D, 2)
            for t in range(TT):
                V.tensor_scalar(N2[:, t], X[:, t], stat[:, 2 + t:3 + t], None, ALU.mult).then_inc(normed, 1)
            turn("h2", 8, xh, xl, scale=lambda k: C("g2", k))
            splits(BASE["pq"], 16)

            dve.wait_ge(sub_ok, 8)
            for i in range(32):
                st.step(V.max(vals[:, i, 0:8], sub[:, i]))
            st.wait()
            for i in range(32):
                st.step(V.max_index(vidx[:, i, 0:8], vals[:, i, 0:8], sub[:, i]))
                st.step(V.match_replace(sub2[:, i], vals[:, i, 0:8], sub[:, i], -3e38))
            st.wait()
            for i in range(32):
                st.step(V.max(vals[:, i, 8:16], sub2[:, i]))
            st.wait()
            for i in range(32):
                st.step(V.max_index(vidx[:, i, 8:16], vals[:, i, 8:16], sub2[:, i]))
            st.wait()
            v5 = vals[:].rearrange("p (h q t) k -> p t h q k", h=PH, q=2, t=TT)
            f5 = vidf[:].rearrange("p (h q t) k -> p t h q k", h=PH, q=2, t=TT)
            st.step(V.tensor_copy(vidf[:], vidx[:]))
            for t in range(TT):
                st.step(V.tensor_tensor(
                    cand[:, 8 * t:8 * t + 8].rearrange("p h (a b) -> p h a b", a=TOPK),
                    v5[:, t, :, 0].unsqueeze(3).to_broadcast([P, PH, TOPK, TOPK]),
                    v5[:, t, :, 1].unsqueeze(2).to_broadcast([P, PH, TOPK, TOPK]), ALU.add))
            st.wait()
            for i in range(16):
                st.step(V.max(tops[:, i, 0:8], cand[:, i]))
            st.wait()
            for i in range(16):
                st.step(V.max_index(tpos[:, i, 0:8], tops[:, i, 0:8], cand[:, i]))
                st.step(V.match_replace(cand2[:, i], tops[:, i, 0:8], cand[:, i], -3e38))
            st.wait()
            for i in range(16):
                st.step(V.max(tops[:, i, 8:16], cand2[:, i]))
            st.wait()
            for i in range(16):
                st.step(V.max_index(tpos[:, i, 8:16], tops[:, i, 8:16], cand2[:, i]))
            tg = sel[:, 2].rearrange("p t (h k) -> p (t h) k", h=PH)
            V.tensor_tensor(tg, tops[:], tops[:, :, 0:1].to_broadcast([P, 16, TOPK]), ALU.subtract
                            ).then_inc(gate_in, 1)
            st.wait()
            tp = tpos[:].rearrange("p i k -> p (i k)")
            st.step(V.tensor_scalar(tab[:, 0], tp, 4, None, ALU.logical_shift_right))
            st.link(V.tensor_scalar(tab[:, 1], tp, 15, None, ALU.bitwise_and))
            st.link(V.tensor_copy(tabf[:], tab[:]))
            for q in range(2):
                for t in range(TT):
                    sl = tabf[:, q, 128 * t:128 * t + 128].rearrange("p (h k) -> p h k", h=PH)
                    st.link(V.tensor_tensor(eq[:], sl.unsqueeze(3).to_broadcast([P, PH, TOPK, TOPK]),
                                            iota[:, 0:TOPK].unsqueeze(1).unsqueeze(1).to_broadcast([P, PH, TOPK, TOPK]),
                                            ALU.is_equal))
                    st.link(V.tensor_tensor(eq[:], eq[:],
                                            f5[:, t, :, q].unsqueeze(2).to_broadcast([P, PH, TOPK, TOPK]), ALU.mult))
                    st.link(V.tensor_reduce(sel[:, q, t].rearrange("p (h k) -> p h k", h=PH), eq[:], AX, ALU.add))
            dve.wait_ge(gate_exp, 1)
            st.link(V.tensor_reduce(stat[:, 80:96], tg, AX, ALU.add))
            st.link(V.reciprocal(stat[:, 96:112], stat[:, 80:96]))
            V.tensor_tensor(tg, tg, stat[:, 96:112].unsqueeze(2).to_broadcast([P, 16, TOPK]), ALU.mult
                            ).then_inc(sel_ok, 1)
            dve.wait_ge(selT_ok, 3)
            with dve.Fori(0, 16) as it:
                for b in range(2):
                    c0 = it * 16 + 8 * b
                    dve.wait_ge(g_ps[b], it)
                    V.tensor_tensor(oh1[:, b], iota[:, 0:P].unsqueeze(1).to_broadcast([P, 8, P]),
                                    selT[:, 0, bass.ds(c0, 8)].unsqueeze(2).to_broadcast([P, 8, P]),
                                    ALU.is_equal).then_inc(oh_ready[b], 1)
                    for k in range(8):
                        V.tensor_scalar(oh2[:, b, k], iota[:, 0:P], selT[:, 1, bass.ds(it * 16 + (8 * b + k), 1)],
                                        selT[:, 2, bass.ds(it * 16 + (8 * b + k), 1)], ALU.is_equal, ALU.mult
                                        ).then_inc(oh_ready[b], 1)

            n0 = BASE["peer"]
            dve.wait_ge(csil, 1)
            dve.wait_ge(g_stored, 32)
            V.memset(macc[:], 0.0).then_inc(mod_zero, 1)
            dve.wait_ge(bmod_in, 16)

            def mod(j, k, off, done):
                dve.wait_ge(mod_in[j], done * 16 + 16)
                if not isinstance(done, int) or done:
                    dve.wait_ge(mod_used, done * 3 - 2 + j)
                V.scalar_tensor_tensor(macc[:, j], mraw[:, j], stat[:, bass.ds(k + 64, 1)]
                                       if not isinstance(k, int) else stat[:, 64 + k:65 + k],
                                       macc[:, j], ALU.mult, ALU.add).then_inc(mod_used, 1)

            def gate(b):
                dve.wait_ge(a_T, b + 1)
                dve.wait_ge(g_in, b * 32 + 32)
                if not isinstance(b, int) or b:
                    dve.wait_ge(ph_ok, b)
                    dve.wait_ge(pl_ok, b)
                for q in range(2):
                    V.tensor_tensor(P32[:, 2 * q:2 * q + 2].rearrange("p k (t n) -> p k t n", t=TT),
                                    ps[:, 2 + q].rearrange("p (k t n) -> p k t n", k=2, t=TT),
                                    Gb[:, :, 2 * q:2 * q + 2].rearrange("p t k n -> p k t n"), ALU.mult
                                    ).then_inc(gated, 1)

            def low(b):
                dve.wait_ge(ph_ok, b + 1)
                dve.wait_ge(gated, b * 2 + 2)
                V.tensor_tensor(Pl[:], P32[:], Ph[:].bitcast(F32), ALU.subtract).then_inc(pl_ok, 1)

            def v_add(b, c, n):
                dve.wait_ge(tile_used, n)
                if not isinstance(b, int) or b:
                    dve.wait_ge(v_out, b * 8)
                for t in range(TT):
                    xs = X[:, t, c * CH:(c + 1) * CH]
                    V.tensor_tensor(xs, xs, ps[:, 4 + 2 * (c % 2) + t], ALU.add).then_inc(v_out, 1)

            splits(n0, 4)
            for j in range(3):
                mod(j, 0, 0, 0)

            def dve_loop(lo_, hi_, half):
                with dve.Fori(lo_, hi_) as b:
                    off = b * 8 - 8
                    split(n0 + 6, off)
                    gate(b - 1)
                    split(n0 + 7, off)
                    low(b - 1)
                    k = b - 16 * half
                    mod(0, k, off, b)
                    split(n0 + 8, off)
                    split(n0 + 9, off)
                    mod(1, k, off, b)
                    split(n0 + 10, off)
                    v_add(b - 1, 0, b * 8 + (n0 + 1))
                    split(n0 + 11, off)
                    v_add(b - 1, 1, b * 8 + (n0 + 2))
                    split(n0 + 12, off)
                    v_add(b - 1, 2, b * 8 + (n0 + 3))
                    mod(2, k, off, b)
                    split(n0 + 13, off)
                    v_add(b - 1, 3, b * 8 + (n0 + 4))

            dve_loop(1, 16, 0)
            dve.wait_ge(mod_used, 48)
            dve.wait_ge(mod_ps, 2)
            V.memset(macc[:], 0.0).then_inc(mod_zero, 1)
            dve.wait_ge(bmod_in, 32)
            dve_loop(16, 32, 1)
            gate(NBLK - 1)
            low(NBLK - 1)
            n1 = BASE["in2"] - 4
            for c in range(4):
                split(n1 + SPL + c)
                v_add(NBLK - 1, c, n1 + c + 1)
            dve.wait_ge(v_out, 8 * NBLK)
            mean_sq(2, D, 2)
            dve.wait_ge(gfin_in, 16)
            for t in range(TT):
                V.scalar_tensor_tensor(X[:, t], X[:, t], stat[:, 2 + t:3 + t], gfin[:], ALU.mult, ALU.mult
                                       ).then_inc(normed, 1)
            dve.wait_ge(mod_col, 2)
            V.scalar_tensor_tensor(mcol[:, 1], mcol[:, 1], 1.0, C("g3", 0, KD), ALU.add, ALU.mult).then_inc(mcol_ok, 1)
            dve.wait_ge(normed, 10)
            mean_sq(2, D, 2)
            for t in range(TT):
                V.tensor_scalar(N3[:, t], X[:, t], stat[:, 2 + t:3 + t], None, ALU.mult).then_inc(normed, 1)
            dve.wait_ge(mcol_ok, 1)
            turn("h3", 8, xh, xl, scale=lambda k: mcol[:, 1, k:k + 1], bias=lambda k: mcol[:, 0, k:k + 1], tmp=t3)
            with dve.Fori(0, 8) as it:
                splits(BASE["in2"], 8, it * 8)
            for t in range(TT):
                dve.wait_ge(qk_sq, 1 + 2 * t)
                V.tensor_reduce(stat[:, 112 + 16 * t:128 + 16 * t], heads_rows(sq2[:], 16, AD), AX, ALU.add
                                ).then_inc(qk_sq, 1)
            dve.wait_ge(qk_sq, 4)
            nroot[0] += 1
            V.tensor_scalar(stat[:, 0:32], stat[:, 112:144], 1.0 / AD, EPS, ALU.mult, ALU.add).then_inc(var_ready, 1)
            dve.wait_ge(rstd_ready, nroot[0])
            dve.wait_ge(gfin_in, 48)
            for t in range(TT):
                v = QKVU[:, t, 0:2 * AW]
                v3 = heads_rows(v, 16, AD)
                st.link(V.tensor_tensor(v3, v3, stat[:, 32 + 16 * t:48 + 16 * t].unsqueeze(2).to_broadcast([P, 16, AD]),
                                        ALU.mult))
                v4 = v.rearrange("p (a h w) -> p a h w", a=2, h=AH)
                st.link(V.tensor_tensor(v4, v4, gqk[:].unsqueeze(2).to_broadcast([P, 2, AH, AD]), ALU.mult))
                sn = trig[:, 0, 64 + 64 * t:128 + 64 * t].unsqueeze(1).to_broadcast([P, 16, 64])
                cn = trig[:, 1, 64 + 64 * t:128 + 64 * t].unsqueeze(1).to_broadcast([P, 16, 64])
                x4 = v.rearrange("p (h b w) -> p h b w", h=16, b=2)
                d4 = rqk[:, t].rearrange("p (h b w) -> p h b w", h=16, b=2)
                ta, tb = (rt[:, i].rearrange("p (h w) -> p h w", h=16) for i in range(2))
                st.step(V.tensor_tensor(ta, x4[:, :, 0], cn, ALU.mult))
                st.link(V.tensor_tensor(tb, x4[:, :, 1], sn, ALU.mult))
                st.link(V.tensor_tensor(d4[:, :, 0], ta, tb, ALU.subtract))
                st.step(V.tensor_tensor(ta, x4[:, :, 0], sn, ALU.mult))
                st.link(V.tensor_tensor(tb, x4[:, :, 1], cn, ALU.mult))
                V.tensor_tensor(d4[:, :, 1], ta, tb, ALU.add).then_inc(qk_rope, 1)
                dve.wait_ge(qk_rope, t + 1)
            for h in range(AH + 2):
                if h < AH:
                    soft_in(h + 16, sc2, 5 + h % 2, float(AD) ** -0.5)
                if h >= 2:
                    g = h - 2
                    soft_out(g + 16, g % 2, lambda t: YA[:, t, g * AD:(g + 1) * AD], None)
            dve.wait_ge(o_out, 48)
            dve.wait_ge(ut_ok, 4)
            V.memset(sv[:, 0], math.e).then_inc(sv_a, 1)
            st.link(V.memset(bM[:], 0.0))
            st.link(V.memset(cM[:], 0.0))
            dve.wait_ge(sv_p, 1)
            st.step(V.tensor_tensor(sv[:, 2], C("lim", 0, STT), sv[:, 1], ALU.mult))
            V.tensor_tensor(sv[:, 3], C("lre", 0, STT), sv[:, 1], ALU.mult).then_inc(sv_a, 1)
            st.wait()
            st.step(V.tensor_scalar(sv[:, 10], sv[:, 2], INV_2PI, None, ALU.mult))
            st.link(V.tensor_scalar(sv[:, 11], sv[:, 2], INV_2PI, 0.25, ALU.mult, ALU.add))
            st.link(V.tensor_scalar(sv[:, 10:12], sv[:, 10:12], MAGIC, None, ALU.add))
            st.link(V.tensor_scalar(sv[:, 10:12], sv[:, 10:12], MAGIC, None, ALU.subtract))
            both = sv[:, 2:3].to_broadcast([P, 2, STT])
            st.link(V.scalar_tensor_tensor(sv[:, 6:8], sv[:, 10:12], -C1, both, ALU.mult, ALU.add))
            st.link(V.scalar_tensor_tensor(sv[:, 6:8], sv[:, 10:12], -C2, sv[:, 6:8], ALU.mult, ALU.add))
            st.link(V.scalar_tensor_tensor(sv[:, 6:8], sv[:, 10:12], -C3, sv[:, 6:8], ALU.mult, ALU.add))
            st.step(V.tensor_scalar(sv[:, 5], sv[:, 6], INV_2PI, None, ALU.mult))
            st.link(V.tensor_scalar(sv[:, 7], sv[:, 7], math.pi / 2, None, ALU.add))
            V.tensor_scalar(sv[:, 6:8], sv[:, 6:8], PI_IN, -PI_IN, ALU.min, ALU.max).then_inc(sv_a, 1)
            st.step(V.tensor_tensor(sv[:, 12], C("lre", 0, STT), C("lre", 0, STT), ALU.mult))
            st.link(V.tensor_tensor(sv[:, 13], C("lim", 0, STT), C("lim", 0, STT), ALU.mult))
            st.link(V.tensor_tensor(sv[:, 12], sv[:, 12], sv[:, 13], ALU.add))
            st.link(V.reciprocal(sv[:, 12], sv[:, 12]))
            dve.wait_ge(sv_s, 1)
            dve.wait_ge(sv_p, 2)
            st.step(V.tensor_tensor(sv[:, 14], sv[:, 4], sv[:, 9], ALU.mult))
            st.link(V.tensor_tensor(sv[:, 15], sv[:, 4], sv[:, 8], ALU.mult))
            st.link(V.tensor_scalar(sv[:, 14], sv[:, 14], -1.0, None, ALU.add))
            st.step(V.tensor_tensor(sv[:, 16], sv[:, 14], C("lre", 0, STT), ALU.mult))
            st.step(V.tensor_tensor(sv[:, 17], sv[:, 15], C("lim", 0, STT), ALU.mult))
            st.step(V.tensor_tensor(sv[:, 18], sv[:, 15], C("lre", 0, STT), ALU.mult))
            st.link(V.tensor_tensor(sv[:, 19], sv[:, 14], C("lim", 0, STT), ALU.mult))
            st.step(V.tensor_tensor(sv[:, 16], sv[:, 16], sv[:, 17], ALU.add))
            st.link(V.tensor_tensor(sv[:, 18], sv[:, 18], sv[:, 19], ALU.subtract))
            st.step(V.tensor_tensor(sv[:, 16], sv[:, 16], sv[:, 12], ALU.mult))
            st.link(V.tensor_tensor(sv[:, 18], sv[:, 18], sv[:, 12], ALU.mult))
            cr = sv[:, 16].unsqueeze(2).to_broadcast([P, STT, GH])
            ci = sv[:, 18].unsqueeze(2).to_broadcast([P, STT, GH])
            tmp = ph[:, 0].rearrange("p s t -> p (s t)")[:, 0:STT * GH].rearrange("p (s h) -> p s h", s=STT)
            dve.wait_ge(ssm_in, 64)
            st.step(V.tensor_tensor(cB[:, 0], ssmB[:, 0], cr, ALU.mult))
            st.link(V.tensor_tensor(tmp, ssmB[:, 1], ci, ALU.mult))
            st.link(V.tensor_tensor(cB[:, 0], cB[:, 0], tmp, ALU.subtract))
            st.step(V.tensor_tensor(cB[:, 1], ssmB[:, 1], cr, ALU.mult))
            st.link(V.tensor_tensor(tmp, ssmB[:, 0], ci, ALU.mult))
            st.link(V.tensor_tensor(cB[:, 1], cB[:, 1], tmp, ALU.add))

            def diagonal(m, half):
                flat = m.rearrange("p s n -> p (s n)")
                lo_p = 64 * half
                return [flat[lo_p:lo_p + 64, s * P + 32 * s + 16 * half:s * P + 32 * s + 16 * half + GH]
                        for s in range(SB)]

            PER = 2 + 2 * SB + 2 + 6 + 2 * SB + 4 + 1
            with dve.Fori(0, 8) as it:
                st.enter(PER, it)
                dve.wait_ge(bl_ps, it * 2)
                dve.wait_ge(y_ps, it)
                dve.wait_ge(y_sum, it)
                for m, src, sign in ((bM, cB, (1.0, 1.0)), (cM, ssmC, (1.0, -1.0))):
                    for i in range(2):
                        for half in range(2):
                            dst = diagonal(m[:, i], half)
                            for s in range(SB):
                                V.tensor_scalar(dst[s], src[64 * half:64 * half + 64, i,
                                                            bass.ds(it * SB + s, 1)].rearrange("p a h -> p (a h)"),
                                                sign[i], None, ALU.mult).then_inc(bm_ok, 1)
                st.step(V.tensor_copy(scol[:, 0], sv[:, 4, bass.ds(it * SB, SB)]))
                st.link(V.tensor_copy(scol[:, 1], sv[:, 5, bass.ds(it * SB, SB)]))
                for s in range(SB):
                    st.step(V.tensor_scalar(ph[:, 0, s], iota, scol[:, 1, s:s + 1], None, ALU.mult))
                    st.step(V.tensor_scalar(ph[:, 1, s], iota, scol[:, 1, s:s + 1], 0.25, ALU.mult, ALU.add))
                st.wait()
                st.link(V.tensor_scalar(rb[:], ph[:], MAGIC, None, ALU.add))
                st.link(V.tensor_scalar(rb[:], rb[:], MAGIC, None, ALU.subtract))
                V.tensor_tensor(ph[:], ph[:], rb[:], ALU.subtract).then_inc(ph_arg, 1)
                dve.wait_ge(cs_ok, it + 1)
                dve.wait_ge(bu_ps, it + 1)
                bre = ps[:, 0:2].rearrange("p a n -> p (a n)").rearrange("p (s t) -> p s t", s=SB)
                bim = ps[:, 2:4].rearrange("p a n -> p (a n)").rearrange("p (s t) -> p s t", s=SB)
                st.step(V.tensor_tensor(rb[:, 0], bre, cs[:, 1], ALU.mult))
                st.step(V.tensor_tensor(rz[:, 0], bim, cs[:, 0], ALU.mult))
                st.step(V.tensor_tensor(rb[:, 1], bim, cs[:, 1], ALU.mult))
                st.link(V.tensor_tensor(rz[:, 1], bre, cs[:, 0], ALU.mult))
                st.step(V.tensor_tensor(rb[:, 0], rb[:, 0], rz[:, 0], ALU.add))
                st.link(V.tensor_tensor(rb[:, 1], rb[:, 1], rz[:, 1], ALU.subtract))
                for s in range(SB):
                    for i in range(2):
                        st.step(V.tensor_tensor_scan(rz[:, i, s], scol[:, 0, s:s + 1].to_broadcast([P, S]), rb[:, i, s],
                                                       0.0, ALU.mult, ALU.add))
                st.wait()
                st.step(V.tensor_tensor(rb[:, 0], rz[:, 0], cs[:, 1], ALU.mult))
                st.step(V.tensor_tensor(ph[:, 0], rz[:, 1], cs[:, 0], ALU.mult))
                st.step(V.tensor_tensor(rb[:, 1], rz[:, 0], cs[:, 0], ALU.mult))
                st.link(V.tensor_tensor(ph[:, 1], rz[:, 1], cs[:, 1], ALU.mult))
                V.tensor_tensor(rb[:, 0], rb[:, 0], ph[:, 0], ALU.subtract).then_inc(st_ok, 1)
                V.tensor_tensor(rb[:, 1], rb[:, 1], ph[:, 1], ALU.add).then_inc(st_ok, 1)
                st.link(V.tensor_copy(scol[:, 0, 0:1], cols[:, bass.ds(it + COFF["dskip"], 1)]))
                dve.wait_ge(y_ps, it + 1)
                V.scalar_tensor_tensor(yT[:, bass.ds(it, 1)].rearrange("p a t -> p (a t)"),
                                       uT[:, bass.ds(it, 1)].rearrange("p a t -> p (a t)"), scol[:, 0, 0:1],
                                       ps[:, 4, 0:S], ALU.mult, ALU.add).then_inc(y_sum, 1)
                st.leave(PER, 8)
            dve.wait_ge(yspl_h, 1)
            V.tensor_tensor(yl[:], yT[:], yh[:].bitcast(F32), ALU.subtract).then_inc(yspl_l, 1)
            splits(BASE["glu"], 4)
            for g in range(4):
                dve.wait_ge(sg_T, g + 1)
                if g:
                    dve.wait_ge(yg_l, g)
                V.tensor_tensor(Y32[:], ps[:, 4 + g % 2].rearrange("p (k t) -> p k t", k=2),
                                yT[:, 2 * g:2 * g + 2], ALU.mult).then_inc(y32_ok, 1)
                dve.wait_ge(yg_h, g + 1)
                V.tensor_tensor(yl[:, 2 * g:2 * g + 2], Y32[:], yh[:, 2 * g:2 * g + 2].bitcast(F32), ALU.subtract
                                ).then_inc(yg_l, 1)
            turn("ya", 4, yah, yal)
            for br, name in enumerate(("abr", "sbr")):
                for pair in range(2):
                    for ab in range(2):
                        n = BASE[name] + 4 * pair + 2 * ab
                        splits(n, 2)
                        dve.wait_ge(tile_used, n + 2)
                        for t in range(TT):
                            c0 = 1024 * pair + 512 * ab
                            g = G2[:, t, br * D + c0:br * D + c0 + CH]
                            m = M2[:, t, c0:c0 + CH]
                            if br == 0:
                                V.tensor_tensor(m, ps[:, 2 * ab + t], g, ALU.mult).then_inc(acc_free[ab], 1)
                            else:
                                V.tensor_tensor(btmp[:, t], ps[:, 2 * ab + t], g, ALU.mult).then_inc(acc_free[ab], 1)
                                dve.wait_ge(acc_free[ab], 2 * (PB[name] + pair) + t + 1)
                                V.tensor_tensor(m, m, btmp[:, t], ALU.add).then_inc(br_out, 1)
            turn("merged2", 8, xh, xl)
            dve.wait_ge(g1b_in, 16)
            for pair in range(2):
                for ab in range(2):
                    n = BASE["out2"] + 8 * pair + 4 * ab
                    splits(n, 4)
                    dve.wait_ge(tile_used, n + 4)
                    for t in range(TT):
                        c0 = 1024 * pair + 512 * ab
                        st.link(V.tensor_tensor(btmp[:, t], ps[:, 2 * ab + t], g1b[:, c0:c0 + CH], ALU.mult))
                        xs = X[:, t, c0:c0 + CH]
                        V.tensor_tensor(xs, xs, btmp[:, t], ALU.add).then_inc(acc_free[ab], 1)
            dve.wait_ge(acc_free[0], 2 * (PB["out2"] + 2))
            dve.wait_ge(acc_free[1], 2 * (PB["out2"] + 2))
            mean_sq(2, D, 2)
            V.scalar_tensor_tensor(mcol[:, 3], mcol[:, 3], 1.0, C("g4", 0, KD), ALU.add, ALU.mult).then_inc(mcol_ok, 1)
            for t in range(TT):
                V.tensor_scalar(N4[:, t], X[:, t], stat[:, 2 + t:3 + t], None, ALU.mult).then_inc(normed, 1)
            dve.wait_ge(mcol_ok, 2)
            turn("h4", 8, xh, xl, scale=lambda k: mcol[:, 3, k:k + 1], bias=lambda k: mcol[:, 2, k:k + 1], tmp=t4)

            st.link(V.memset(Y[:], 0.0))
            n0 = BASE["ffn"]

            def conv(b):
                for half in range(2):
                    for tap in range(2):
                        if tap == 0:
                            dve.wait_ge(cv_base, b * 8 + (4 * half + 4))
                        else:
                            st.wait()
                        for f in range(4):
                            q = 16 * half + 4 * f
                            d = 1 + tap
                            src = ps[:, 4 + 2 * half + f // 2, S * (f % 2):S * (f % 2) + S - d]
                            dst = cv[:, half, f, d:S]
                            ins = V.scalar_tensor_tensor(dst, src, ccol[:, q + 1 - tap:q + 2 - tap], dst,
                                                         ALU.mult, ALU.add)
                            if tap and f == 3:
                                ins.then_inc(cv_ok, 1)
                            else:
                                st.step(ins)

            def conv_cols(b):
                V.tensor_copy(ccol[:], cols[:, bass.ds(b * 32 + COFF["conv"], 32)] if not isinstance(b, int)
                              else C("conv", 32 * b, 32)).then_inc(cc_ok, 1)
                dve.wait_ge(cc_ok, b + 1)

            def product(b):
                dve.wait_ge(sil_ok, b + 1)
                dve.wait_ge(cv_ok, b * 2 + 2)
                V.tensor_tensor(F32t[:], cv[:, 0], sil[:], ALU.mult).then_inc(f32_ok, 1)

            def flow(b):
                dve.wait_ge(fh_ok, b + 1)
                dve.wait_ge(f32_ok, b + 1)
                V.tensor_tensor(Fl[:], F32t[:], Fh[:].bitcast(F32), ALU.subtract).then_inc(fl_ok, 1)

            def y_add(b, c, n):
                dve.wait_ge(tile_used, n)
                if not isinstance(b, int) or b:
                    dve.wait_ge(dn_out, b * 8)
                for t in range(TT):
                    ys = Y[:, t, c * CH:(c + 1) * CH]
                    V.tensor_tensor(ys, ys, ps[:, 4 + 2 * (c % 2) + t], ALU.add).then_inc(dn_out, 1)

            splits(n0, 8)
            with dve.Fori(1, FB) as b:
                st.enter(14, b - 1)
                off = b * 12 - 12
                conv_cols(b - 1)
                split(n0 + 10, off)
                split(n0 + 11, off)
                conv(b - 1)
                product(b - 1)
                split(n0 + 12, off)
                split(n0 + 13, off)
                flow(b - 1)
                splits(n0 + 12, 4, off)
                split(n0 + 18, off)
                y_add(b - 1, 0, b * 12 + (n0 + 5))
                split(n0 + 19, off)
                y_add(b - 1, 1, b * 12 + (n0 + 6))
                split(n0 + 20, off)
                y_add(b - 1, 2, b * 12 + (n0 + 7))
                split(n0 + 21, off)
                y_add(b - 1, 3, b * 12 + (n0 + 8))
                st.leave(14, FB - 1)
            conv_cols(FB - 1)
            conv(FB - 1)
            product(FB - 1)
            flow(FB - 1)
            splits(TOTAL - 4, 4)
            for c in range(4):
                y_add(FB - 1, c, TOTAL - 3 + c)
            dve.wait_ge(dn_out, 8 * FB)
            dve.wait_ge(g2b_in, 16)
            for t in range(TT):
                st.link(V.tensor_tensor(Y[:, t], Y[:, t], g2b[:], ALU.mult))
                V.tensor_tensor(Y[:, t], Y[:, t], X[:, t], ALU.add).then_inc(y_done, 1)

        @block.tensor
        def _(pe):
            def tile(n0, off, xhi, xlo, k0, banks, start, stop_, w=CH):
                pe.wait_ge(lo_ready, n0 + 1 + off)
                for k in range(4):
                    H = hi[:, n0 % SPL, k * w:(k + 1) * w]
                    L = lo[:, n0 % SPL, k * w:(k + 1) * w]
                    for t in range(TT):
                        acc = ps[:, banks + t, 0:w]
                        xs = slice(t * P, (t + 1) * P)
                        s0 = start and k == 0
                        s1 = stop_ and k == 3
                        PE_.matmul(acc, xhi[:, k0 + k, xs], H, start=s0, stop=False)
                        PE_.matmul(acc, xhi[:, k0 + k, xs], L, start=False, stop=False)
                        mm = PE_.matmul(acc, xlo[:, k0 + k, xs], H, start=False, stop=s1)
                mm.then_inc(tile_used, 1)

            def chunk(n0, off, tiles, ab, pair, xhi, xlo, bias=None):
                if not isinstance(pair, int) or pair:
                    pe.wait_ge(acc_free[ab], pair * 2)
                if bias is not None:
                    for t in range(TT):
                        mm = PE_.matmul(ps[:, 2 * ab + t], ones[0:1, :], bias, start=True, stop=False)
                    if ab:
                        mm.then_inc(bias_used, 1)
                for j in range(tiles):
                    tile(n0 + j, off, xhi, xlo, 4 * j, 2 * ab, bias is None and j == 0, j == tiles - 1)

            def turn(name, rounds, src):
                for r in range(rounds):
                    g = TBASE[name] + r
                    if g >= 2:
                        pe.wait_ge(turn_lo, g - 1)
                    for k in range(2):
                        for t in range(TT):
                            c0 = (2 * r + k) * P
                            mm = PE_.transpose(ps[:, 4 + g % 2, k * S + t * P:k * S + (t + 1) * P],
                                               src[:, t, c0:c0 + P], ident)
                    mm.then_inc(turned, 1)

            pe.wait_ge(small_in, 64)
            pe.wait_ge(normed, 2)
            turn("h1", 8, N1)
            pe.wait_ge(turn_lo, 8)
            for ab in range(2):
                chunk(4 * ab, 0, 4, ab, 0, xh, xl)
            with pe.Fori(0, 4) as it:
                for ab in range(2):
                    chunk(8 + 4 * ab, it * 8, 4, ab, it + 1, xh, xl)
            with pe.Fori(0, 4) as it:
                pe.wait_ge(bias_in, it * 16 + 16)
                for ab in range(2):
                    chunk(40 + 4 * ab, it * 8, 4, ab, it + 5, xh, xl, bias=brow[0:1, ab * CH:(ab + 1) * CH])
            n0 = BASE["kpe"]
            pe.wait_ge(lo_ready, n0 + 1)
            pe.wait_ge(acc_free[0], 18)
            for t in range(TT):
                for k in range(KD):
                    H = hi[:, n0 % SPL, k * ROPE:(k + 1) * ROPE]
                    L = lo[:, n0 % SPL, k * ROPE:(k + 1) * ROPE]
                    xs = slice(t * P, (t + 1) * P)
                    acc = ps[:, t, 0:ROPE]
                    PE_.matmul(acc, xh[:, k, xs], H, start=k == 0, stop=False)
                    PE_.matmul(acc, xh[:, k, xs], L, start=False, stop=False)
                    mm = PE_.matmul(acc, xl[:, k, xs], H, start=False, stop=k == KD - 1)
            mm.then_inc(tile_used, 1)
            pe.wait_ge(kpe_out, 2)
            pe.wait_ge(acc_free[0], 18)
            pe.wait_ge(acc_free[1], 18)
            for t in range(TT):
                pe.wait_ge(ln_done, t + 1)
                for g in range(SGU_G):
                    bank = ((4, 5, 6, 7), (0, 1, 2, 3))[t][g // 2]
                    mm = PE_.matmul(ps[:, bank, SGU_W * (g % 2):SGU_W * (g % 2) + SGU_W], wsp[:, g],
                                    Z[:, t, D + g * SGU_W:D + (g + 1) * SGU_W], start=True, stop=True)
                    if g % 2:
                        mm.then_inc(mixed, 1)
            pe.wait_ge(normed, 6)
            pe.wait_ge(mixed_out, 8)
            turn("cq", 2, CQ)
            turn("ckv", 2, CKV)
            pe.wait_ge(kpr_ok, 2)
            for t in range(TT):
                mm = PE_.transpose(ps[:, 6, t * P:(t + 1) * P], KPR[:, t], ident)
            mm.then_inc(kpt_ps, 1)

            def scores(h, bank, parts, off=0):
                if h >= 2 or not isinstance(off, int):
                    pe.wait_ge(s_max, max(h - 1, 0) + off)
                for q, (c0, w) in enumerate(((0, P), (P, S))):
                    for i, (l, r) in enumerate(parts):
                        mm = PE_.matmul(ps[:, bank, c0:c0 + w], l[:, q * P:(q + 1) * P], r[:, 0:w],
                                        start=i == 0, stop=i == len(parts) - 1)
                mm.then_inc(s_ready, 1)

            def probsT(h, src, bank, off=0):
                pe.wait_ge(p_ready, 2 * h + 2 + off * 2)
                if h >= 2 or not isinstance(off, int):
                    pe.wait_ge(pt_ok, max(h - 1, 0) + off)
                for j in range(3):
                    mm = PE_.transpose(ps[:, bank, j * P:(j + 1) * P], src[:, h % 2, j * P:(j + 1) * P], ident)
                mm.then_inc(pt_ps, 1)

            def values(h, src, bank, v, off=0):
                pe.wait_ge(pt_ok, h + 1 + off)
                if h >= 2 or not isinstance(off, int):
                    pe.wait_ge(o_out, 2 * max(h - 1, 0) + off * 2)
                b = h % 2
                PE_.matmul(ps[:, bank, 0:P], src[:, b, 0:P], v(0), start=True, stop=True)
                PE_.matmul(ps[:, bank, P:S], src[:, b, P:2 * P], v(0), start=True, stop=False)
                PE_.matmul(ps[:, bank, P:S], src[:, b, 2 * P:3 * P], v(1), start=False, stop=True
                           ).then_inc(o_ready, 1)

            pe.wait_ge(turn_lo, TBASE["merged"])
            pe.wait_ge(mixed_out, 16)
            pe.wait_ge(kpt_ok, 1)
            with pe.Fori(0, 4) as it:
                n0 = BASE["mla"]
                for j, (l_h, l_l, w) in enumerate(((cqh, cql, CH), (cqh, cql, GROUP * ROPE),
                                                   (ckh, ckl, CH), (ckh, ckl, CH))):
                    if j == 0:
                        pe.wait_ge(o_out, it * 8)
                    tile(n0 + j, it * 4, l_h, l_l, 0, 2 * j, True, True, w)
                pe.wait_ge(m_evac, it * 8 + 2)
                for h in range(GROUP):
                    for t in range(TT):
                        mm = PE_.transpose(ps[:, h // 2, (h % 2) * S + t * P:(h % 2) * S + (t + 1) * P],
                                           qn[:, t, h * P:(h + 1) * P], ident)
                mm.then_inc(m_tr, 1)
                pe.wait_ge(m_evac, it * 8 + 6)
                for h in range(GROUP):
                    for t in range(TT):
                        mm = PE_.transpose(ps[:, 2 + h // 2, (h % 2) * S + t * P:(h % 2) * S + (t + 1) * P],
                                           kn[:, t, h * P:(h + 1) * P], ident)
                mm.then_inc(m_tr, 1)
                pe.wait_ge(m_rope, it * 2 + 2)
                for h in range(GROUP // 2):
                    for t in range(TT):
                        mm = PE_.transpose(ps[:, 4, h * S + t * P:h * S + (t + 1) * P],
                                           qrr[:, t, h * P:(h + 1) * P], ident)
                mm.then_inc(m_tr, 1)
                pe.wait_ge(m_ta, it * 2 + 2)
                pe.wait_ge(m_tv, it + 1)
                pe.wait_ge(m_evac, it * 8 + 8)
                for h in range(GROUP + 2):
                    if h < GROUP:
                        r0 = 64 * (h % 2)
                        scores(h, 5 + h % 2, ((qT[:, h], kT[:, h]),
                                              (qrT[r0:r0 + 64, h // 2], KPT[r0:r0 + 64])), it * 4)
                    if 1 <= h <= GROUP:
                        probsT(h - 1, pr, (4, 7)[(h - 1) % 2], it * 4)
                    if h >= 2:
                        g = h - 2
                        values(g, pT, g % 2, lambda t: vv[:, t, g * VH:(g + 1) * VH], it * 4)
            pe.wait_ge(merged_ok, 2)
            pe.wait_ge(pt_ok, 16)
            turn("merged", 8, GT)
            pe.wait_ge(turn_lo, TBASE["merged"] + 8)
            for pair in range(2):
                for ab in range(2):
                    chunk(BASE["out"] + 8 * pair + 4 * ab, 0, 4, ab, PB["out"] + pair, xh, xl)
            pe.wait_ge(normed, 8)
            turn("h2", 8, N2)
            pe.wait_ge(turn_lo, TBASE["h2"] + 8)
            for pair in range(2):
                for ab in range(2):
                    chunk(BASE["pq"] + 8 * pair + 4 * ab, 0, 4, ab, PB["pq"] + pair, xh, xl)
            pe.wait_ge(acc_free[0], 2 * (PB["pq"] + 2))
            pe.wait_ge(acc_free[1], 2 * (PB["pq"] + 2))
            for g in range(8):
                if g >= 2:
                    pe.wait_ge(qt_ok, g - 1)
                for k in range(2):
                    for t in range(TT):
                        c0 = (2 * g + k) * P
                        mm = PE_.transpose(ps[:, 4 + g % 2, k * S + t * P:k * S + (t + 1) * P], Q[:, t, c0:c0 + P],
                                           ident)
                mm.then_inc(qt_ps, 1)
            pe.wait_ge(keys_in, 16)
            pe.wait_ge(qt_ok, 8)
            for g in range(8):
                if g >= 4:
                    pe.wait_ge(sub_ok, g - 3)
                for j in range(4):
                    hp, t = 2 * g + j // 2, j % 2
                    mm = PE_.matmul(ps[:, 4 + g % 4, j * P:(j + 1) * P], QT[:, hp, t * P:(t + 1) * P], keys[:, hp],
                                    start=True, stop=True)
                mm.then_inc(sub_ps, 1)
            pe.wait_ge(sel_ok, 1)
            pe.wait_ge(sub_ok, 8)
            for i in range(3):
                for t in range(TT):
                    mm = PE_.transpose(ps[:, 4 + i, t * P:(t + 1) * P], sel[:, i, t], ident)
            mm.then_inc(selT_ps, 1)
            pe.wait_ge(selT_ok, 3)
            with pe.Fori(0, 16) as it:
                for b in range(2):
                    pe.wait_ge(g_out[b], it)
                    pe.wait_ge(oh_ready[b], it * 9 + 9)
                    for k in range(8):
                        mm = PE_.matmul(ps[:, 4 + 2 * b + k // 4, (k % 4) * P:(k % 4 + 1) * P], oh1[:, b, k],
                                        oh2[:, b, k], start=True, stop=True)
                    mm.then_inc(g_ps[b], 1)

            n0 = BASE["peer"]

            def u_block(b, n, off=0):
                if not isinstance(b, int) or b:
                    pe.wait_ge(a_ok, b * 2)
                for j in range(4):
                    tile(n + j, off, xh, xl, 4 * j, 0, j == 0, j == 3)

            def u_turn(b):
                pe.wait_ge(a_ok, b * 2 + 2)
                if not isinstance(b, int) or b:
                    pe.wait_ge(gated, b * 2)
                for k in range(JB):
                    for t in range(TT):
                        mm = PE_.transpose(ps[:, 2 + k // 2, (k % 2) * S + t * P:(k % 2) * S + (t + 1) * P],
                                           Ab[:, t, k * P:(k + 1) * P], ident)
                mm.then_inc(a_T, 1)

            def v_block(b, n, off=0):
                pe.wait_ge(pl_ok, b + 1)
                for c in range(4):
                    pe.wait_ge(v_out, b * 8 + max(2 * c - 2, 0))
                    tile(n + c, off, Ph, Pl, 0, 4 + 2 * (c % 2), True, True)

            def mod_sum(half):
                pe.wait_ge(mod_used, 48 * (half + 1))
                for j in range(2):
                    for k in range(KD):
                        mm = PE_.matmul(ps[:, 0, j * KD + k:j * KD + k + 1], macc[:, j, k * P:(k + 1) * P],
                                        ones[:, 0:1], start=True, stop=True)
                mm.then_inc(mod_ps, 1)
                pe.wait_ge(v_out, 120 + 128 * half)
                for q in range(4):
                    mm = PE_.matmul(ps[0:1, 4 + q], ones[:, 0:1], macc[:, 2, q * CH:(q + 1) * CH],
                                    start=True, stop=True)
                mm.then_inc(mod_ps, 1)
                pe.wait_ge(mod_col, half + 1)
                pe.wait_ge(mod_row, 4 * half + 4)

            pe.wait_ge(acc_free[0], 2 * (PB["pq"] + 2))
            for b in range(2):
                pe.wait_ge(g_out[b], 16)
            u_block(0, n0)
            u_turn(0)

            def pe_loop(lo_, hi_):
                with pe.Fori(lo_, hi_) as b:
                    u_block(b, n0 + 4, b * 8 - 8)
                    v_block(b - 1, n0 + 8, b * 8 - 8)
                    u_turn(b)

            pe_loop(1, 16)
            mod_sum(0)
            pe_loop(16, 32)
            mod_sum(1)
            v_block(NBLK - 1, n0 + 8 * NBLK - 4)

            pe.wait_ge(v_out, 8 * NBLK)
            pe.wait_ge(normed, 12)
            turn("h3", 8, N3)
            pe.wait_ge(turn_lo, TBASE["h3"] + 8)
            with pe.Fori(0, 8) as it:
                for ab in range(2):
                    chunk(BASE["in2"] + 4 * ab, it * 8, 4, ab, it + PB["in2"], xh, xl)
            pe.wait_ge(acc_free[0], 2 * (PB["in2"] + 8))
            pe.wait_ge(acc_free[1], 2 * (PB["in2"] + 8))
            pe.wait_ge(qk_rope, 2)
            for g in range(8):
                if g >= 2:
                    pe.wait_ge(qk_out, g - 1)
                for k in range(2):
                    for t in range(TT):
                        c0 = (2 * g + k) * P
                        mm = PE_.transpose(ps[:, 4 + g % 2, k * S + t * P:k * S + (t + 1) * P], rqk[:, t, c0:c0 + P],
                                           ident)
                mm.then_inc(qk_tr, 1)
            pe.wait_ge(qk_out, 8)
            for h in range(AH + 2):
                if h < AH:
                    scores(h + 16, 5 + h % 2, ((qT2[:, h], kT2[:, h]),))
                if 1 <= h <= AH:
                    probsT(h + 15, pr2, (4, 7)[(h - 1) % 2])
                if h >= 2:
                    g = h - 2
                    values(g + 16, pT2, g % 2, lambda t: QKVU[:, t, 2 * AW + g * AD:2 * AW + (g + 1) * AD])
            pe.wait_ge(pt_ok, 24)
            for g in range(4):
                if g >= 2:
                    pe.wait_ge(ut_ok, g - 1)
                for k in range(2):
                    for t in range(TT):
                        c0 = 3 * AW + (2 * g + k) * P
                        mm = PE_.transpose(ps[:, 4 + g % 2, k * S + t * P:k * S + (t + 1) * P],
                                           QKVU[:, t, c0:c0 + P], ident)
                mm.then_inc(ut_ps, 1)
            pe.wait_ge(ut_ok, 4)
            with pe.Fori(0, 8) as it:
                pe.wait_ge(bm_ok, it * 32 + 16)
                pe.wait_ge(bl_ok, it * 2)
                for i in range(2):
                    for s in range(SB):
                        mm = PE_.transpose(ps[:, 6 + i, s * P:(s + 1) * P], bM[:, i, s], ident)
                    mm.then_inc(bl_ps, 1)
                pe.wait_ge(bl_ok, it * 2 + 2)
                pe.wait_ge(st_ok, it * 2)
                for i in range(2):
                    for s in range(SB):
                        mm = PE_.matmul(ps[:, 2 * i + s // 2, (s % 2) * S:(s % 2) * S + S], bL[:, i, s],
                                        uT[:, bass.ds(it, 1)].rearrange("p a t -> p (a t)"), start=True, stop=True)
                mm.then_inc(bu_ps, 1)
                pe.wait_ge(st_ok, it * 2 + 2)
                pe.wait_ge(bm_ok, it * 32 + 32)
                pe.wait_ge(y_sum, it)
                for i in range(2):
                    for s in range(SB):
                        mm = PE_.matmul(ps[:, 4, 0:S], cM[:, i, s], rb[:, i, s], start=i + s == 0,
                                        stop=i == 1 and s == SB - 1)
                mm.then_inc(y_ps, 1)
            pe.wait_ge(yspl_l, 1)
            pe.wait_ge(bglu_in, 16)
            for ab in range(2):
                chunk(BASE["glu"] + 2 * ab, 0, 2, ab, PB["glu"], yh, yl, bias=bglu[0:1, ab * CH:(ab + 1) * CH])
            pe.wait_ge(y_sum, 8)
            pe.wait_ge(acc_free[1], 2 * (PB["glu"] + 1))
            for g in range(4):
                pe.wait_ge(acc_free[g // 2], 2 * (PB["glu"] + 1))
                if g >= 2:
                    pe.wait_ge(y32_ok, g - 1)
                for k in range(2):
                    for t in range(TT):
                        c0 = (2 * g + k) * P
                        mm = PE_.transpose(ps[:, 4 + g % 2, k * S + t * P:k * S + (t + 1) * P], SG[:, t, c0:c0 + P],
                                           ident)
                mm.then_inc(sg_T, 1)
            pe.wait_ge(y32_ok, 4)
            turn("ya", 4, YA)
            pe.wait_ge(turn_lo, TBASE["ya"] + 4)
            for pair in range(2):
                for ab in range(2):
                    chunk(BASE["abr"] + 4 * pair + 2 * ab, 0, 2, ab, PB["abr"] + pair, yah, yal)
            pe.wait_ge(yg_l, 4)
            for pair in range(2):
                for ab in range(2):
                    chunk(BASE["sbr"] + 4 * pair + 2 * ab, 0, 2, ab, PB["sbr"] + pair, yh, yl)
            pe.wait_ge(br_out, 8)
            turn("merged2", 8, M2)
            pe.wait_ge(turn_lo, TBASE["merged2"] + 8)
            for pair in range(2):
                for ab in range(2):
                    chunk(BASE["out2"] + 8 * pair + 4 * ab, 0, 4, ab, PB["out2"] + pair, xh, xl)
            pe.wait_ge(normed, 14)
            turn("h4", 8, N4)
            pe.wait_ge(turn_lo, TBASE["h4"] + 8)
            n0 = BASE["ffn"]

            def up_block(b, n, off=0):
                for half in range(2):
                    if not isinstance(b, int) or b:
                        pe.wait_ge(up_out, b * 4 + (2 * half - 2))
                    for j in range(4):
                        tile(n + 4 * half + j, off, xh, xl, 4 * j, 2 * half, j == 0, j == 3)

            def up_turn(b):
                for half in range(2):
                    pe.wait_ge(up_out, b * 4 + (2 * half + 2))
                    if not isinstance(b, int) or b:
                        pe.wait_ge(dn_out, b * 8 - (2, 0)[half])
                    for f in range(4):
                        for t in range(TT):
                            mm = PE_.transpose(ps[:, 4 + 2 * half + f // 2, (f % 2) * S + t * P:(f % 2) * S + (t + 1) * P],
                                               UP[:, half, t, f * P:(f + 1) * P], ident)
                    mm.then_inc(up_T, 1)

            def down_block(b, n, off=0):
                pe.wait_ge(fl_ok, b + 1)
                for c in range(4):
                    if c >= 2:
                        pe.wait_ge(dn_out, b * 8 + (2 * c - 2))
                    tile(n + c, off, Fh, Fl, 0, 4 + 2 * (c % 2), True, True)

            pe.wait_ge(acc_free[0], 2 * (PB["out2"] + 2))
            pe.wait_ge(acc_free[1], 2 * (PB["out2"] + 2))
            up_block(0, n0)
            up_turn(0)
            with pe.Fori(1, FB) as b:
                up_block(b, n0 + 8, b * 12 - 12)
                down_block(b - 1, n0 + 16, b * 12 - 12)
                up_turn(b)
            down_block(FB - 1, n0 + 12 * FB - 4)


def constants():
    c = np.zeros((P, NCONST), np.float32)

    def put(name, a):
        c[:, KOFF[name]:KOFF[name] + a.shape[-1]] = a

    put("ident", np.eye(P, dtype=np.float32))
    put("ones", np.ones((P, P), np.float32))
    causal = np.where(np.arange(P)[:, None] >= np.arange(P)[None], 0.0, NEG).astype(np.float32)
    put("mask", np.concatenate([causal, np.zeros((P, P), np.float32), causal], 1))
    put("triu", np.triu(np.ones((P, P), np.float32)))
    put("iota", np.arange(2 * P, dtype=np.float32)[None].repeat(P, 0))
    f = np.float32(10000.0) ** (-np.arange(0, 64, 2, dtype=np.float32) / np.float32(64))
    put("freq", f.astype(np.float32)[None].repeat(P, 0))
    f = np.float32(10000.0) ** (-np.arange(64, dtype=np.float32) / np.float32(64))
    put("freq2", f.astype(np.float32)[None].repeat(P, 0))
    return c


def weight_tiles(w):
    k, n = w.shape
    return np.ascontiguousarray(
        w.reshape(k // CH, 4, P, n // CH, CH).transpose(3, 0, 2, 1, 4).reshape(-1, P, TW))


def columns(v):
    return v.reshape(-1, P).T


def prepare(i):
    g = {k: np.asarray(v) for k, v in i.items()}
    a = {}
    a["const"] = constants()
    a["x"] = np.ascontiguousarray(g["x"][0].reshape(TT, P, D).transpose(1, 0, 2))
    a["pos"] = np.ascontiguousarray(np.concatenate([g["positions"].reshape(TT, P).T,
                                                    g["positions_2"].reshape(TT, P).T], 1))
    w = g["w_in"][0]
    o = 2 * LORA
    order = np.concatenate([w[:, 0:o], w[:, o + ROPE:]], 1)
    a["w_in"] = weight_tiles(order)
    a["kpe"] = np.ascontiguousarray(w[:, o:o + ROPE].reshape(KD, P, ROPE).transpose(1, 0, 2).reshape(P, KD * ROPE))
    a["b_gate"] = np.ascontiguousarray(g["b_gate"][0].reshape(4, 2 * CH))
    uq, ukv = g["w_uq"][0], g["w_ukv"][0]
    parts = []
    for r in range(HEADS // GROUP):
        hs = slice(r * GROUP, (r + 1) * GROUP)
        for m in (uq[:, hs, :NOPE], ukv[:, hs, :NOPE], ukv[:, hs, NOPE:]):
            parts.append(weight_tiles(m.reshape(LORA, CH))[0])
    a["mla"] = np.stack(parts)
    a["mla_r"] = np.ascontiguousarray(
        uq[:, :, NOPE:].reshape(KL, P, HEADS // GROUP, GROUP * ROPE).transpose(2, 1, 0, 3).reshape(HEADS // GROUP, P, TW // 2))
    a["w_spatial"] = np.ascontiguousarray(g["w_spatial"][0].transpose(2, 0, 1))
    a["sgu_ln_g"], a["sgu_ln_b"] = g["sgu_ln_g"][0], g["sgu_ln_b"][0]
    a["out"] = weight_tiles(g["w_out"][0])
    a["pq"] = weight_tiles(g["w_peer_q"][0].reshape(D, D))
    a["peer_keys"] = np.ascontiguousarray(g["peer_keys"][0].reshape(16, NKEY, P).transpose(2, 0, 1))
    u = g["peer_u"][0].reshape(P, NBLK, JB, KD, P)
    a["peer_u"] = np.ascontiguousarray(u.transpose(1, 3, 4, 2, 0).reshape(NBLK, 4, 4, P, EB)
                                       .transpose(0, 1, 3, 2, 4).reshape(NBLK * 4, P, TW))
    v = g["peer_v"][0].reshape(P, NBLK, JB, 4, CH)
    a["peer_v"] = np.ascontiguousarray(v.transpose(1, 3, 0, 2, 4).reshape(NBLK * 4, P, TW))
    a["w_mod"] = np.ascontiguousarray(g["w_mod_2"][0].reshape(D, 6, D).transpose(1, 0, 2))
    a["b_mod"] = np.ascontiguousarray(g["b_mod_2"][0].reshape(2, 3 * D))
    a["g_final"] = g["g_final"]
    a["q_norm_g"], a["k_norm_g"] = g["q_norm_g_2"][0], g["k_norm_g_2"][0]
    a["in2"] = weight_tiles(g["w_in_2"][0])
    a["glu"] = weight_tiles(g["w_glu_2"][0])
    a["b_glu"] = np.ascontiguousarray(g["b_glu_2"][0].reshape(1, AW))
    a["abr"] = weight_tiles(g["w_attn_br_2"][0])
    a["sbr"] = weight_tiles(g["w_ssm_br_2"][0])
    a["out2"] = weight_tiles(g["w_out_2"][0])
    wu = weight_tiles(g["w_up_2"][0]).reshape(2, FB, 4, P, TW)
    a["w_up"] = np.ascontiguousarray(wu.transpose(1, 0, 2, 3, 4).reshape(FB * 8, P, TW))
    wd = g["w_down_2"][0].reshape(FB, 4, P, 4, CH)
    a["w_down"] = np.ascontiguousarray(wd.transpose(0, 3, 2, 1, 4).reshape(FB * 4, P, TW))

    def states(v):
        return v.reshape(STT, P, *v.shape[2:]).swapaxes(0, 1)

    for n in ("re", "im"):
        a[f"ssm_b_{n}"] = np.ascontiguousarray(states(g[f"ssm_b_{n}_2"][0]))
        a[f"ssm_c_{n}"] = np.ascontiguousarray(states(g[f"ssm_c_{n}_2"][0].swapaxes(1, 2)))
    cols = np.zeros((P, NCOLS), np.float32)

    def put(name, m):
        cols[:, COFF[name]:COFF[name] + m.shape[1]] = m

    put("g1", columns(g["g_norm1"][0]))
    put("gqa", columns(g["g_q_a"][0]))
    put("gkva", columns(g["g_kv_a"][0]))
    put("g2", columns(g["g_norm2"][0]))
    put("g3", columns(g["norm1_g_2"][0]))
    put("g4", columns(g["norm2_g_2"][0]))
    put("bsp", g["b_spatial"][0].T)
    put("c", columns(g["c_2"][0]))
    put("dskip", columns(g["ssm_d_2"][0]))
    put("lre", states(g["ssm_lambda_re_2"][0]))
    put("lim", states(g["ssm_lambda_im_2"][0]))
    put("ldt", states(np.broadcast_to(g["ssm_log_dt_2"][0][:, None], (NG, NST))))
    taps = np.concatenate([g["conv_w_2"][0], g["conv_b_2"]], 0)
    taps = taps.reshape(4, 2, FB, 4, P).transpose(4, 2, 1, 3, 0)
    put("conv", taps.reshape(P, FB * 32))
    a["cols"] = cols
    return a


def kernel(**inputs):
    import numpy as _np
    import concourse.bacc as _bacc
    from concourse import mybir as _mybir
    from concourse.bass_utils import run_bass_kernel_spmd as _run

    arrays = prepare(inputs)
    nc = _bacc.Bacc("TRN2", target_bir_lowering=False, num_devices=1)
    aps = {}
    for name, v in arrays.items():
        aps[name] = nc.dram_tensor(f"in_{name}", v.shape, _mybir.dt.from_np(v.dtype), kind="ExternalInput").ap()
    out = nc.dram_tensor("out_0", (S, D), F32, kind="ExternalOutput").ap()
    build(nc, aps, out)
    r = _run(nc, [{f"in_{k}": v for k, v in arrays.items()}], core_ids=[0])
    return _np.asarray(r.results[0]["out_0"]).reshape(1, S, D)
```

```python
import math
from contextlib import ExitStack

import numpy as np

import concourse.bass as bass
from concourse import mybir

F32 = mybir.dt.float32
F32R = mybir.dt.float32r
I32 = mybir.dt.int32
U32 = mybir.dt.uint32
ALU = mybir.AluOpType
ACT = mybir.ActivationFunctionType
AX = mybir.AxisListType.X

P = 128
S, TT = 256, 2
D, KD = 2048, 16
CH = 512
SL = 2
TW = SL * CH
TC, TA, TL = KD // SL, 8 // SL, 4 // SL
RAW, SPL = 8, 4
EPS = 1e-6
HEADS, NOPE, ROPE, VH = 16, 128, 64, 128
LORA, KL = 512, 4
GROUP = 4
SGU_G, SGU_W = 8, 256
PH, NKEY, TOPK = 8, 128, 16
HK = PH * TOPK
NEXP = NKEY * NKEY
EB = CH
NBLK = NEXP // EB
JB = EB // NKEY
AHEAD, CHOICE = 16, 11
GATES = 4
MAIN = NBLK - AHEAD
GT4, GQ = 4, 64
AH, AD, AW = 8, 128, 1024
NG, GH, NST = 64, 16, 64
STT = NG * NST // P
SB = 4
FFN = 5632
FB = FFN // CH
NEG = -1e30

STREAM = [("w_in", 18 * TC), ("kpe", 1), ("mla", 4 * 4 * TL), ("out", 4 * TC), ("pq", 4 * TC),
          ("peer", (TC + 4 * TL) * NBLK), ("in2", 16 * TC), ("glu", 2 * TA), ("abr", 4 * TA),
          ("sbr", 4 * TA), ("out2", 4 * TC), ("ffn", (2 * TC + 4 * TL) * FB)]
BASE, _n = {}, 0
for _name, _count in STREAM:
    BASE[_name] = _n
    _n += _count
TOTAL = _n

TURNS = [("h1", 8), ("cq", 2), ("ckv", 2), ("merged", 8), ("h2", 8), ("h3", 8), ("ya", 4),
         ("merged2", 8), ("h4", 8)]
TBASE, _n = {}, 0
for _name, _count in TURNS:
    TBASE[_name] = _n
    _n += _count

COLS = [("bmod", 96), ("g1", 16), ("gqa", 4), ("gkva", 4), ("g2", 16), ("g3", 16), ("g4", 16), ("bsp", 8),
        ("c", 16), ("dskip", 8), ("lre", 32), ("lim", 32), ("ldt", 32), ("conv", FB * 32)]
COFF, _n = {}, 0
for _name, _count in COLS:
    COFF[_name] = _n
    _n += _count
NCOLS = _n

CONST = [("ident", 128), ("ones", 128), ("mask", 384), ("triu", 128), ("iota", 256),
         ("freq", 32), ("freq2", 64), ("halfpi", 1), ("magic", 1)]
KOFF, _n = {}, 0
for _name, _count in CONST:
    KOFF[_name] = _n
    _n += _count
NCONST = _n

TWO_PI = 2.0 * math.pi
INV_2PI = 1.0 / TWO_PI
C1 = 6.28125
C2 = float(np.float32(0.0019350051879882812))
C3 = TWO_PI - C1 - C2
MAGIC = 12582912.0
PI_IN = 3.1415925
TURN = 6.283185


class Steps:

    def __init__(self, eng, sem):
        self.eng, self.sem, self.base, self.k = eng, sem, 0, 0

    def step(self, ins):
        ins.then_inc(self.sem, 1)
        self.k += 1

    def wait(self):
        self.eng.wait_ge(self.sem, self.base + self.k)

    def link(self, ins):
        self.step(ins)
        self.wait()

    def enter(self, per, it):
        self.outer = self.base + self.k
        self.base, self.k = per * it + self.outer, 0

    def leave(self, per, count):
        assert self.k == per, (self.k, per)
        self.base, self.k = self.outer + per * count, 0


def build(nc, A, out):
    V, SC, PE_, GP = nc.vector, nc.scalar, nc.tensor, nc.gpsimd
    ctx = ExitStack()
    with ctx:
        base0 = 16512

        def at(name, shape, kb, dt=F32):
            return nc.alloc_sbuf_tensor_at(name, shape, dt, offset=base0 + int(kb * 1024)).ap()

        def sem(name):
            return ctx.enter_context(nc.semaphore(name))

        raw = at("raw", [P, RAW, TW], 0)
        hi = at("hi", [P, SPL, TW], 32, F32R)
        lo = at("lo", [P, SPL, TW], 48, F32R)
        xh = at("xh", [P, KD, S], 64, F32R)
        xl = at("xl", [P, KD, S], 80, F32R)
        X = at("X", [P, TT, D], 96)
        const = at("const", [P, NCONST], 112)
        cols = at("cols", [P, NCOLS], 112 + 4.5)
        stat = at("stat", [P, 256], 112 + 4.5 + 2.75)
        trig = at("trig", [P, 2, 192], 112 + 4.5 + 3.75)
        W0 = 112 + 4.5 + 3.75 + 1.5

        def K(name):
            return const[:, KOFF[name]:KOFF[name] + dict(CONST)[name]]

        def C(name, i, n=1):
            return cols[:, COFF[name] + i:COFF[name] + i + n]

        ident, ones, iota = K("ident"), K("ones"), K("iota")

        Z = at("Z", [P, TT, 2 * D], W0)
        GT = at("GT", [P, TT, 2 * D], W0 + 32)
        CQ = at("CQ", [P, TT, LORA], W0 + 64)
        CKV = at("CKV", [P, TT, LORA], W0 + 68)
        KPE = at("KPE", [P, TT, ROPE], W0 + 72)
        brow = at("brow", [1, 2 * CH], W0 + 73)
        wsp = at("wsp", [P, SGU_G, P], W0 + 77)
        KPR = at("KPR", [P, TT, P], W0 + 81)
        KPT = at("KPT", [P, S], W0 + 82)
        ktmp = at("ktmp", [P, TT, 64], W0 + 83)
        N1 = at("N1", [P, TT, D], W0)
        ang = at("ang", [P, 6, 192], W0 + 16)
        posi = at("posi", [P, 4], W0 + 22, I32)
        posf = at("posf", [P, 4], W0 + 22.25)
        junk = at("junk", [P, D], W0 + 24)
        lng = at("lng", [P, D], 80)
        lnb = at("lnb", [P, D], 88)
        cqh = at("cqh", [P, KL, S], 64, F32R)
        cql = at("cql", [P, KL, S], 68, F32R)
        ckh = at("ckh", [P, KL, S], 72, F32R)
        ckl = at("ckl", [P, KL, S], 76, F32R)
        junk2 = at("junk2", [P, D], 64)
        qn = at("qn", [P, TT, CH], W0)
        kn = at("kn", [P, TT, CH], W0 + 4)
        vv = at("vv", [P, TT, CH], W0 + 8)
        qr = at("qr", [P, TT, GROUP * ROPE], W0 + 12)
        qrr = at("qrr", [P, TT, GROUP * ROPE], W0 + 14)
        qtmp = at("qtmp", [P, TT, GROUP * 32], W0 + 16)
        qT = at("qT", [P, GROUP, S], W0 + 17)
        kT = at("kT", [P, GROUP, S], W0 + 21)
        qrT = at("qrT", [P, GROUP // 2, S], W0 + 25)
        sc = at("sc", [P, 2, 384], W0 + 73)
        pr = at("pr", [P, 2, 384], W0 + 76)
        pT = at("pT", [P, 2, 384], W0 + 27)
        N2 = at("N2", [P, TT, D], W0)
        Q = at("Q", [P, TT, D], W0)
        QT = at("QT", [P, 16, S], W0 + 16)
        keys = at("keys", [P, 16, NKEY], W0 + 32)
        sub = at("sub", [P, 32, NKEY], W0 + 40)
        sub2 = at("sub2", [P, 32, NKEY], W0 + 56)
        vals = at("vals", [P, 32, TOPK], W0 + 72)
        vidx = at("vidx", [P, 32, TOPK], W0 + 74, U32)
        vidf = at("vidf", [P, 32, TOPK], W0 + 76)
        cand = at("cand", [P, 16, 256], W0 + 56)
        cand2 = at("cand2", [P, 16, 256], W0 + 40)
        tops = at("tops", [P, 16, TOPK], W0 + 78)
        tpos = at("tpos", [P, 16, TOPK], W0 + 79, U32)
        tab = at("tab", [P, 2, 16 * TOPK], W0 + 80, U32)
        tabf = at("tabf", [P, 2, 16 * TOPK], W0 + 82)
        eq = at("eq", [P, 8, TOPK, TOPK], W0 + 40)
        sel = at("sel", [P, 3, TT, HK], W0 + 48)
        selT = at("selT", [P, 3, S], W0 + 81)
        oh1 = at("oh1", [P, 2, GT4, P], W0 + 8)
        oh2 = at("oh2", [P, 2, GT4, P], W0 + 12)
        gst = at("gst", [P, 2, NKEY, GQ], W0 + 16)
        Ab = at("Ab", [P, TT, EB], W0)
        Ain = at("Ain", [P, 2, TT, EB], W0 + 4)
        Gb = at("Gb", [P, 2, S // GQ, JB, GQ], W0 + 12)
        P32 = at("P32", [P, 2, JB, S], W0 + 20)
        Ph = at("Ph", [P, 2, JB, S], W0 + 28, F32R)
        Pl = at("Pl", [P, 2, JB, S], W0 + 36, F32R)
        macc = at("macc", [P, D], W0 + 44)
        mraw = at("mraw", [P, 4, D], W0 + 52)
        macc2 = at("macc2", [P, D], W0 + 48)
        mraw2 = at("mraw2", [P, D], W0 + 56)
        gfin = at("gfin", [P, D], W0)
        N3 = at("N3", [P, TT, D], W0)
        mcol = at("mcol", [P, 6, KD], W0 + 84)
        t3 = at("t3", [P, 2, S], W0 + 16)
        QKVU = at("QKVU", [P, TT, 4 * AW], W0)
        G2 = at("G2", [P, TT, 2 * D], W0 + 32)
        gqk = at("gqk", [P, 2, AD], W0 + 85)
        neghalf = at("neghalf", [P, 32], W0 + 84.5)
        sq2 = at("sq2", [P, TT, 2 * AW], W0 + 32)
        sc2 = at("sc2", [P, 2, 384], W0 + 64)
        pr2 = at("pr2", [P, 2, 384], W0 + 67)
        pT2 = at("pT2", [P, 2, 384], W0 + 70)
        rqk = at("rqk", [P, TT, 2, AD], W0 + 73)
        rt = at("rt", [P, 2, TT * 2 * AD // 2], W0 + 75)
        qkT = at("qkT", [P, 2, S], W0 + 77)
        YA = QKVU[:, :, 0:AW]
        uT = at("uT", [P, 8, S], W0 + 76)
        ssmB = at("ssmB", [P, 2, STT, GH], W0 + 8)
        ssmC = at("ssmC", [P, 2, STT, GH], W0 + 12)
        cB = at("cB", [P, 2, STT, GH], W0 + 4)
        sv = at("sv", [P, 20, STT], W0 + 64)
        bM = at("bM", [P, 2, SB, P], W0 + 20)
        bL = at("bL", [P, 2, SB, P], W0 + 24)
        cM = at("cM", [P, 2, SB, P], W0 + 28)
        px = at("px", [P, 2, S], 64)
        pr_ = at("pr_", [P, 2, S], 66)
        cs = at("cs", [P, 2, 2, 2, S], 68)
        rb = at("rb", [P, 2, 2, S], 76)
        rz = at("rz", [P, 2, 2, 2, S], 80)
        fw = at("fw", [P, 2, 2, 2, S], 88)
        yT = at("yT", [P, 8, S], W0 + 68)
        yh = at("yh", [P, 8, S], 64, F32R)
        yl = at("yl", [P, 8, S], 72, F32R)
        SG = at("SG", [P, TT, AW], W0 + 76)
        bglu = at("bglu", [1, AW], W0 + 12)
        Y32 = at("Y32", [P, 2, S], W0 + 28)
        yah = at("yah", [P, 8, S], 80, F32R)
        yal = at("yal", [P, 8, S], 88, F32R)
        M2 = at("M2", [P, TT, D], W0)
        btmp = at("btmp", [P, 2, CH], W0 + 16)
        g1b = at("g1b", [P, D], W0 + 20)
        dg1 = at("dg1", [P, KD, P], W0 + 4)
        dg2 = at("dg2", [P, KD, P], W0 + 24)
        N4 = at("N4", [P, TT, D], W0 + 32)
        t4 = at("t4", [P, 2, S], W0 + 29)
        Y = at("Y", [P, TT, D], W0)
        g2b = at("g2b", [P, D], W0 + 16)
        UP = at("UP", [P, 2, TT, CH], W0 + 32)
        cv = at("cv", [P, 2, 4, S], W0 + 40)
        ccol = at("ccol", [P, 32], W0 + 48)
        sil = at("sil", [P, 4, S], W0 + 50)
        F32t = at("F32t", [P, 4, S], W0 + 54)
        Fh = at("Fh", [P, 4, S], W0 + 58, F32R)
        Fl = at("Fl", [P, 4, S], W0 + 62, F32R)

        ps = ctx.enter_context(nc.psum_tensor("ps", [P, 8, CH], F32)).ap()

        gdram = nc.dram_tensor("gate_scratch", [S // GQ, P, NKEY, GQ], F32, kind="Internal").ap()
        adram = nc.dram_tensor("act_scratch", [NBLK, P, TT * EB], F32, kind="Internal").ap()

        raw_ready = [sem(f"raw_ready{i}") for i in range(RAW)]
        hi_ready = sem("hi_ready")
        lo_ready = sem("lo_ready")
        tile_used = sem("tile_used")
        acc_free = [sem("accA_free"), sem("accB_free")]
        turned = sem("turned")
        turn_hi = sem("turn_hi")
        turn_lo = sem("turn_lo")
        x_in = sem("x_in")
        small_in = sem("small_in")
        var_ready = sem("var_ready")
        rstd_ready = sem("rstd_ready")
        sq_ready = sem("sq_ready")
        normed = sem("normed")
        act_step, dve_step = sem("act_step"), sem("dve_step")
        trig_arg, trig_ok = sem("trig_arg"), sem("trig_ok")
        bias_in, bias_used = sem("bias_in"), sem("bias_used")
        kpe_out = sem("kpe_out")
        ln_in, keys_in = sem("ln_in"), sem("keys_in")
        ln_sum, ln_mu = sem("ln_sum"), sem("ln_mu")
        ln_done, mixed, mixed_out = sem("ln_done"), sem("mixed"), sem("mixed_out")
        kpr_ok, kpt_ps, kpt_ok = sem("kpr_ok"), sem("kpt_ps"), sem("kpt_ok")
        m_evac, m_rope, m_tr = sem("m_evac"), sem("m_rope"), sem("m_tr")
        m_ta, m_tv = sem("m_ta"), sem("m_tv")
        s_ready, s_max, p_ready = sem("s_ready"), sem("s_max"), sem("p_ready")
        pt_ps, pt_ok, o_ready, o_out = sem("pt_ps"), sem("pt_ok"), sem("o_ready"), sem("o_out")
        merged_ok = sem("merged_ok")
        q_out, qt_ps, qt_ok = sem("q_out"), sem("qt_ps"), sem("qt_ok")
        sub_ps, sub_ok = sem("sub_ps"), sem("sub_ok")
        gate_in, gate_exp = sem("gate_in"), sem("gate_exp")
        sel_ok, selT_ps, selT_ok = sem("sel_ok"), sem("selT_ps"), sem("selT_ok")
        oh_ready, g_ps, g_out = ([sem(f"{n}{b}") for b in range(2)] for n in ("oh_ready", "g_ps", "g_out"))
        g_st = [sem(f"g_st{b}") for b in range(2)]
        g_in, a_in = ([sem(f"{n}{b}") for b in range(2)] for n in ("g_in", "a_in"))
        gated, a_st = sem("gated"), sem("a_st")
        a_ok, a_T, ph_ok, pl_ok = sem("a_ok"), sem("a_T"), sem("ph_ok"), sem("pl_ok")
        v_out = sem("v_out")
        mod_in = [sem(f"mod_in{i}") for i in range(4)]
        mod_used, pow_ok = sem("mod_used"), sem("pow_ok")
        mod2_in, mod2_used, mod2_ps = sem("mod2_in"), sem("mod2_used"), sem("mod2_ps")
        csil, mod_ps = sem("csil"), sem("mod_ps")
        dg_ok, spread, spread_out = sem("dg_ok"), sem("spread"), sem("spread_out")
        gfin_in, mod_col = sem("gfin_in"), sem("mod_col")
        mcol_ok = sem("mcol_ok")
        in2_out = sem("in2_out")
        qk_sq, qk_rope, qk_tr, qk_out = sem("qk_sq"), sem("qk_rope"), sem("qk_tr"), sem("qk_out")
        ut_ps, ut_ok = sem("ut_ps"), sem("ut_ok")
        ssm_in, sv_a, sv_p, sv_s = sem("ssm_in"), sem("sv_a"), sem("sv_p"), sem("sv_s")
        bm_ok, bl_ps, bl_ok, bu_ps = sem("bm_ok"), sem("bl_ps"), sem("bl_ok"), sem("bu_ps")
        ph_x, ph_arg, cs_ok, rot_ok, fw_ok, y_ps, y_ok = (
            sem(n) for n in ("ph_x", "ph_arg", "cs_ok", "rot_ok", "fw_ok", "y_ps", "y_ok"))
        y_sum, cm_ok = sem("y_sum"), sem("cm_ok")
        yspl_h, yspl_l = sem("yspl_h"), sem("yspl_l")
        sg_T, y32_ok, yg_h, yg_l = (sem(n) for n in ("sg_T", "y32_ok", "yg_h", "yg_l"))
        br_out, bglu_in = sem("br_out"), sem("bglu_in")
        up_out, up_T, cv_base, cv_ok, sil_ok, f32_ok, fh_ok, fl_ok, dn_out = (
            sem(n) for n in ("up_out", "up_T", "cv_base", "cv_ok", "sil_ok", "f32_ok", "fh_ok",
                             "fl_ok", "dn_out"))
        cc_ok = sem("cc_ok")
        y_done, o_st = sem("y_done"), sem("o_st")

        PAIRS = [("w_in", 9), ("out", 2), ("pq", 2), ("in2", 8), ("glu", 1), ("abr", 2),
                 ("sbr", 2), ("out2", 2)]
        PB, n = {}, 0
        for name, count in PAIRS:
            PB[name] = n
            n += count

        def heads_rows(ap, h, w):
            return ap.rearrange("p (h w) -> p h w", h=h, w=w)

        block = ctx.enter_context(nc.Block())

        @block.sync
        def _(sp):
            def load(src, n0, off=0, w=TW):
                if n0 >= RAW:
                    sp.wait_ge(lo_ready, n0 - RAW + 1 + off)
                sp.dma_start(raw[:, n0 % RAW, 0:w], src).then_inc(raw_ready[n0 % RAW], 16)

            def tile(name, i):
                if isinstance(i, int):
                    return A[name][i]
                return A[name][bass.ds(i, 1)].rearrange("a p n -> p (a n)")

            def section(name, count):
                n0 = BASE[name]
                with sp.Fori(0, count // RAW) as it:
                    for j in range(RAW):
                        load(tile(name, it * RAW + j), n0 + j, it * RAW)

            sp.dma_start(X[:], A["x"]).then_inc(x_in, 16)
            for j in range(RAW):
                load(tile("w_in", j), j)
            with sp.Fori(1, 10) as it:
                for j in range(TC):
                    load(tile("w_in", it * TC + j), j + TC, it * TC - TC)
            with sp.Fori(0, 4) as it:
                sp.wait_ge(bias_used, it)
                sp.dma_start(brow[:], A["b_gate"][bass.ds(it, 1), :]).then_inc(bias_in, 16)
                for j in range(2 * TC):
                    load(tile("w_in", it * (2 * TC) + (10 * TC + j)), 10 * TC + j, it * (2 * TC))
            load(A["kpe"], BASE["kpe"], w=KD * ROPE)
            with sp.Fori(0, 4) as it:
                for j in range(4 * TL):
                    n0 = BASE["mla"] + j
                    if j // TL == 1:
                        load(A["mla_r"][bass.ds(it * TL + j % TL, 1)].rearrange("a p n -> p (a n)"), n0,
                             it * (4 * TL), TW // 2)
                    else:
                        load(tile("mla", it * (3 * TL) + (j if j < TL else j - TL)), n0, it * (4 * TL))
            section("out", 4 * TC)
            section("pq", 4 * TC)
            n0 = BASE["peer"]

            def up(b, n, off=0):
                for j in range(TC):
                    load(tile("peer_u", b * TC + j), n + j, off)

            def down(b, n, off=0):
                for j in range(4 * TL):
                    load(tile("peer_v", b * (4 * TL) + j), n + j, off)

            with sp.Fori(0, AHEAD) as b:
                up(b, n0, b * TC)
            with sp.Fori(0, MAIN) as b:
                up(b + AHEAD, n0 + AHEAD * TC, b * 16)
                down(b, n0 + AHEAD * TC + 8, b * 16)
            with sp.Fori(0, AHEAD) as b:
                down(b + MAIN, n0 + AHEAD * TC + 16 * MAIN, b * 8)
            section("in2", 16 * TC)
            section("glu", 2 * TA)
            section("abr", 4 * TA)
            section("sbr", 4 * TA)
            section("out2", 4 * TC)
            n0 = BASE["ffn"]

            def ups(b, n, off=0):
                for j in range(2 * TC):
                    load(tile("w_up", b * (2 * TC) + j), n + j, off)

            def downs(b, n, off=0):
                for j in range(4 * TL):
                    load(tile("w_down", b * (4 * TL) + j), n + j, off)

            ups(0, n0)
            with sp.Fori(1, FB) as b:
                ups(b, n0 + 16, b * 24 - 24)
                downs(b - 1, n0 + 32, b * 24 - 24)
            downs(FB - 1, n0 + 24 * FB - 8)

        @block.gpsimd
        def _(pool):
            pool.dma_start(const[:], A["const"]).then_inc(small_in, 16)
            pool.dma_start(cols[:], A["cols"]).then_inc(small_in, 16)
            pool.dma_start(posi[:], A["pos"]).then_inc(small_in, 16)
            pool.dma_start(wsp[:], A["w_spatial"]).then_inc(small_in, 16)
            GP.memset(neghalf[:], -0.5).then_inc(pow_ok, 1)
            count = [0]
            pool.wait_ge(pow_ok, 1)

            def inverse_root(off, n):
                count[0] += 1
                pool.wait_ge(var_ready, count[0])
                GP.tensor_tensor(stat[:, off + n:off + 2 * n], stat[:, off:off + n], neghalf[:, 0:n],
                                 ALU.pow).then_inc(rstd_ready, 1)

            inverse_root(0, 2)
            pool.wait_ge(tile_used, BASE["kpe"] + 1)
            pool.dma_start(lng[:], A["sgu_ln_g"].partition_broadcast(P)).then_inc(ln_in, 16)
            pool.dma_start(lnb[:], A["sgu_ln_b"].partition_broadcast(P)).then_inc(ln_in, 16)
            inverse_root(0, 2)
            inverse_root(0, 4)
            pool.wait_ge(turn_lo, TBASE["merged"] + 8)
            pool.dma_start(keys[:], A["peer_keys"]).then_inc(keys_in, 16)
            inverse_root(0, 2)
            def a_store(b):
                pool.wait_ge(a_ok, b * 2 + 2)
                pool.dma_start(adram[b] if isinstance(b, int) else adram[bass.ds(b, 1)].rearrange("a p n -> p (a n)"),
                               Ab[:].rearrange("p t n -> p (t n)")).then_inc(a_st, 16)

            def expert_in(v, q):
                if not isinstance(v, int) or v >= 2:
                    pool.wait_ge(a_T, v - 1)
                    pool.wait_ge(gated, v * 2 - 2)
                pool.wait_ge(a_st, v * 16 + 16)
                pool.dma_start(Ain[:, q].rearrange("p t n -> p (t n)"),
                               adram[v] if isinstance(v, int) else adram[bass.ds(v, 1)].rearrange("a p n -> p (a n)")
                               ).then_inc(a_in[q], 16)
                pool.dma_start(Gb[:, q], gdram[:, :, slice(v * JB, v * JB + JB) if isinstance(v, int)
                                               else bass.ds(v * JB, JB)].rearrange("c i j t -> i c j t")
                               ).then_inc(g_in[q], 16)

            for b in range(CHOICE):
                a_store(b)
            with pool.Fori(0, 2) as it:
                for e in range(2):
                    for b in range(2):
                        pool.wait_ge(g_out[b], it * 16 + (8 * e + 8))
                    pool.dma_start(gdram[bass.ds(it * 2 + e, 1)].rearrange("c i j t -> i (c j t)"),
                                   gst[:, e].rearrange("p j t -> p (j t)")).then_inc(g_st[e], 16)
                    a_store(it * 2 + (CHOICE + e))
            for b in range(CHOICE + GATES, AHEAD):
                a_store(b)
            for e in range(2):
                pool.wait_ge(g_st[e], 32)
            expert_in(0, 0)
            with pool.Fori(0, MAIN // 2) as it:
                for e in range(2):
                    expert_in(it * 2 + (e + 1), (e + 1) % 2)
                    a_store(it * 2 + (AHEAD + e))
            for v in range(MAIN + 1, NBLK):
                expert_in(v, v % 2)
            pool.wait_ge(v_out, 8 * NBLK)
            pool.dma_start(gfin[:], A["g_final"].partition_broadcast(P)).then_inc(gfin_in, 16)
            inverse_root(0, 2)
            inverse_root(0, 2)
            pool.dma_start(gqk[:, 0], A["q_norm_g"].partition_broadcast(P)).then_inc(gfin_in, 16)
            pool.dma_start(gqk[:, 1], A["k_norm_g"].partition_broadcast(P)).then_inc(gfin_in, 16)
            inverse_root(0, 32)
            pool.wait_ge(ut_ok, 4)
            for i, n in enumerate(("ssm_b_re", "ssm_b_im")):
                pool.dma_start(ssmB[:, i], A[n]).then_inc(ssm_in, 16)
            for i, n in enumerate(("ssm_c_re", "ssm_c_im")):
                pool.dma_start(ssmC[:, i], A[n]).then_inc(ssm_in, 16)
            pool.wait_ge(sv_a, 1)
            GP.tensor_tensor(sv[:, 1], sv[:, 0], C("ldt", 0, STT), ALU.pow).then_inc(sv_p, 1)
            pool.wait_ge(sv_a, 2)
            GP.tensor_tensor(sv[:, 4], sv[:, 0], sv[:, 3], ALU.pow).then_inc(sv_p, 1)
            pool.wait_ge(yspl_l, 1)
            pool.dma_start(bglu[:], A["b_glu"]).then_inc(bglu_in, 16)
            inverse_root(0, 2)

        @block.scalar
        def _(act):
            st = Steps(act, act_step)

            def split(n0, off=0):
                if n0 >= TOTAL:
                    return
                act.wait_ge(raw_ready[n0 % RAW], 16 * (n0 // RAW + 1) + off * (16 // RAW))
                if n0 >= SPL:
                    act.wait_ge(tile_used, n0 - SPL + 1 + off)
                SC.copy(hi[:, n0 % SPL], raw[:, n0 % RAW]).then_inc(hi_ready, 1)

            def splits(n0, count, off=0):
                for j in range(count):
                    split(n0 + SPL + j, off)

            squares = [0]

            def sumsq(junk, src, accum, bias=0.0):
                if squares[0]:
                    act.wait_ge(sq_ready, squares[0])
                squares[0] += 1
                SC.activation(junk, src, ACT.Square, bias=bias, accum_out=accum).then_inc(sq_ready, 1)

            def turn(name, rounds, h, scale=None, bias=None, after=None):
                for r in range(rounds):
                    g = TBASE[name] + r
                    act.wait_ge(turned, g + 1)
                    bank = ps[:, 4 + g % 2].rearrange("p (k t) -> p k t", k=2)
                    if r == 0 and after is not None:
                        act.wait_ge(tile_used, after)
                    for k in range(2):
                        kk = 2 * r + k
                        if scale is None:
                            if k == 0:
                                SC.copy(h[:, kk:kk + 2], bank).then_inc(turn_hi, 2)
                        elif bias is None:
                            SC.activation(h[:, kk], bank[:, k], ACT.Copy, scale=scale(kk)).then_inc(turn_hi, 1)
                        else:
                            SC.activation(h[:, kk], bank[:, k], ACT.Identity, scale=scale(kk),
                                          bias=bias(kk)).then_inc(turn_hi, 1)

            act.wait_ge(x_in, 16)
            for t in range(TT):
                sumsq(junk[:], X[:, t], stat[:, 8 + t:9 + t])
            for j in range(SPL):
                split(j)
            act.wait_ge(trig_arg, 1)
            SC.activation(trig[:], ang[:, 4:6], ACT.Sin).then_inc(trig_ok, 1)
            act.wait_ge(small_in, 64)
            turn("h1", 8, xh, scale=lambda k: C("g1", k))
            def evac(pair, ab, dst, func, off=0, pinc=None):
                act.wait_ge(tile_used, pair)
                for t in range(TT):
                    SC.activation(dst(t), ps[:, 2 * ab + t], func).then_inc(acc_free[ab], 1)

            splits(0, TC)
            evac(TC, 0, lambda t: CQ[:, t], ACT.Copy)
            splits(TC, TC)
            evac(2 * TC, 1, lambda t: CKV[:, t], ACT.Copy)
            with act.Fori(0, 4) as it:
                for ab in range(2):
                    splits((2 + ab) * TC, TC, it * (2 * TC))
                    evac(it * (2 * TC) + (3 + ab) * TC, ab,
                         lambda t: Z[:, t, bass.ds(it * 1024 + 512 * ab, CH)], ACT.Gelu_apprx_tanh)
            with act.Fori(0, 4) as it:
                for ab in range(2):
                    splits((10 + ab) * TC, TC, it * (2 * TC))
                    evac(it * (2 * TC) + (11 + ab) * TC, ab,
                         lambda t: GT[:, t, bass.ds(it * 1024 + 512 * ab, CH)], ACT.Sigmoid)
            split(BASE["kpe"] + SPL)
            act.wait_ge(tile_used, BASE["kpe"] + 1)
            for t in range(TT):
                SC.copy(KPE[:, t], ps[:, t, 0:ROPE]).then_inc(kpe_out, 1)
            act.wait_ge(acc_free[1], 18)
            act.wait_ge(bias_used, 4)
            for t in range(TT):
                if t:
                    act.wait_ge(ln_sum, t)
                SC.activation(junk2[:], Z[:, t, D:2 * D], ACT.Copy, accum_out=stat[:, 16 + t:17 + t]
                              ).then_inc(ln_sum, 1)
            act.wait_ge(ln_sum, 2)
            act.wait_ge(ln_mu, 1)
            for t in range(TT):
                sumsq(junk2[:], Z[:, t, D:2 * D], stat[:, 8 + t:9 + t], stat[:, 18 + t:19 + t])
            for j, src in enumerate((CQ, CKV)):
                for t in range(TT):
                    sumsq(junk2[:, 0:LORA], src[:, t], stat[:, 10 + 2 * j + t:11 + 2 * j + t])
            turn("cq", 2, cqh, scale=lambda k: C("gqa", k))
            turn("ckv", 2, ckh, scale=lambda k: C("gkva", k))
            act.wait_ge(kpt_ps, 1)
            SC.copy(KPT[:], ps[:, 6, 0:S]).then_inc(kpt_ok, 1)

            def probs(h, s, p, stats, off=0):
                act.wait_ge(s_max, h + 1 + off)
                b, q = h % 2, h % 2 if h >= 16 else h % 4
                if h >= 2 or not isinstance(off, int):
                    act.wait_ge(pt_ps, max(h - 1, 0) + off)
                SC.activation(p[:, b, 0:P], s[:, b, 0:P], ACT.Exp, bias=stats(q, 0),
                              accum_out=stats(q, 2)).then_inc(p_ready, 1)
                SC.activation(p[:, b, P:384], s[:, b, P:384], ACT.Exp, bias=stats(q, 1),
                              accum_out=stats(q, 3)).then_inc(p_ready, 1)

            def probsT(h, dst, bank, off=0):
                act.wait_ge(pt_ps, h + 1 + off)
                if h >= 2 or not isinstance(off, int):
                    act.wait_ge(o_ready, max(h - 1, 0) + off)
                SC.copy(dst[:, h % 2], ps[:, bank, 0:384]).then_inc(pt_ok, 1)

            def stat_col(q, i):
                return stat[:, 32 + 4 * q + i:33 + 4 * q + i]

            with act.Fori(0, 4) as it:
                n0 = BASE["mla"]
                for j, (dst, w) in enumerate(((qn, CH), (qr, GROUP * ROPE), (kn, CH), (vv, CH))):
                    splits(n0 + TL * j, TL, it * (4 * TL))
                    act.wait_ge(tile_used, it * (4 * TL) + (n0 + TL * j + TL))
                    if j == 0:
                        act.wait_ge(m_tr, it * 3)
                    if j == 3:
                        act.wait_ge(o_ready, it * 4)
                    for t in range(TT):
                        SC.copy(dst[:, t], ps[:, 2 * j + t, 0:w]).then_inc(m_evac, 1)
                act.wait_ge(m_tr, it * 3 + 1)
                act.wait_ge(s_ready, it * 4)
                SC.copy(qT[:].rearrange("p h t -> p (h t)"), ps[:, 0:2].rearrange("p a n -> p (a n)")
                        ).then_inc(m_ta, 1)
                act.wait_ge(m_tr, it * 3 + 3)
                SC.copy(qrT[:].rearrange("p h t -> p (h t)"), ps[:, 4]).then_inc(m_ta, 1)
                for h in range(GROUP + 1):
                    if h < GROUP:
                        probs(h, sc, pr, stat_col, it * 4)
                    if h >= 1:
                        probsT(h - 1, pT, (4, 7)[(h - 1) % 2], it * 4)
            turn("merged", 8, xh, after=BASE["out"])
            splits(BASE["out"], 4 * TC)
            act.wait_ge(acc_free[1], 22)
            for t in range(TT):
                sumsq(junk2[:], X[:, t], stat[:, 8 + t:9 + t])
            turn("h2", 8, xh, scale=lambda k: C("g2", k), after=BASE["pq"])
            for pair in range(2):
                for ab in range(2):
                    splits(BASE["pq"] + (2 * pair + ab) * TC, TC)
                    evac(BASE["pq"] + (2 * pair + ab + 1) * TC, ab,
                         lambda t: Q[:, t, 1024 * pair + 512 * ab:1024 * pair + 512 * ab + CH], ACT.Copy)
            for g in range(8):
                act.wait_ge(qt_ps, g + 1)
                SC.copy(QT[:, 2 * g:2 * g + 2], ps[:, 4 + g % 2].rearrange("p (k t) -> p k t", k=2)
                        ).then_inc(qt_ok, 1)
            for g in range(8):
                act.wait_ge(sub_ps, g + 1)
                SC.copy(sub[:, 4 * g:4 * g + 4].rearrange("p a n -> p (a n)"), ps[:, 4 + g % 4]
                        ).then_inc(sub_ok, 1)
            act.wait_ge(small_in, 64)
            SC.activation(stat[:, 64:80], C("c", 0, KD), ACT.Silu).then_inc(csil, 1)
            n0 = BASE["peer"]

            def gelu(b, n, bank=0):
                act.wait_ge(tile_used, n)
                if not isinstance(b, int) or b:
                    act.wait_ge(a_st, b * 16)
                for t in range(TT):
                    SC.activation(Ab[:, t], ps[:, bank + t], ACT.Gelu_apprx_tanh).then_inc(a_ok, 1)

            for b in range(CHOICE):
                splits(n0 + b * TC, TC)
                gelu(b, n0 + b * TC + TC, 2 * (b % 2))
            act.wait_ge(gate_in, 1)
            SC.activation(sel[:, 2], sel[:, 2], ACT.Exp).then_inc(gate_exp, 1)
            act.wait_ge(selT_ps, 1)
            act.wait_ge(sel_ok, 1)
            for i in range(3):
                SC.copy(selT[:, i], ps[:, 4 + i, 0:S]).then_inc(selT_ok, 1)
            with act.Fori(0, 2) as it:
                for e in range(2):
                    act.wait_ge(g_st[e], it * 16)
                    for g in range(GQ // GT4):
                        act.wait_ge(g_ps[g % 2], it * 16 + (8 * e + g // 2 + 1))
                        SC.copy(gst[:, e, :, GT4 * g:GT4 * g + GT4],
                                ps[:, 4 + g % 2].rearrange("p (k j) -> p j k", k=GT4)).then_inc(g_out[g % 2], 1)
                        if g % 2:
                            split(n0 + (CHOICE + e) * TC + SPL + g // 2, it * (2 * TC))
                    gelu(it * 2 + (CHOICE + e), it * (2 * TC) + (n0 + (CHOICE + e + 1) * TC))
            for b in range(CHOICE + GATES, AHEAD):
                splits(n0 + b * TC, TC)
                gelu(b, n0 + b * TC + TC)

            n0 = BASE["peer"] + AHEAD * TC

            def act_high(v, q, used):
                act.wait_ge(gated, v * 2 + 2)
                if used is not None:
                    act.wait_ge(tile_used, used)
                SC.copy(Ph[:, q], P32[:, q]).then_inc(ph_ok, 1)

            def mod_load(u, rr):
                act.dma_start(mraw[:, u % 4], A["w_mod"][bass.ds(rr * KD + u, 1)].rearrange("a p n -> p (a n)")
                              ).then_inc(mod_in[u % 4], 16)

            act_high(0, 0, None)
            with act.Fori(0, MAIN // 4) as rr:
                act.wait_ge(mod_used, rr * KD)
                for u in range(3):
                    mod_load(u, rr)
                for i in range(4):
                    n, off = n0 + 16 * i, rr * 64
                    for j in range(4):
                        split(n + 4 + 2 * j, off)
                        split(n + 5 + 2 * j, off)
                        u = 4 * i + j
                        if u + 3 < KD:
                            act.wait_ge(mod_used, rr * KD + u)
                            mod_load(u + 3, rr)
                    gelu(rr * 4 + (AHEAD + i), off + (n + 8))
                    split(n + 12, off)
                    split(n + 13, off)
                    act_high(rr * 4 + (i + 1), (i + 1) % 2, off + n)
                    for j in range(14, 20):
                        split(n + j, off)
            n0 += 16 * MAIN

            def act_tail(v, q, n, off):
                act.wait_ge(mod_used, v + (4 * KD - MAIN))
                act.dma_start(mraw[:, q], A["w_mod"][v + (4 * KD - MAIN)] if isinstance(v, int) else
                              A["w_mod"][bass.ds(v + (4 * KD - MAIN), 1)].rearrange("a p n -> p (a n)")
                              ).then_inc(mod_in[q], 16)
                split(n + 4, off)
                split(n + 5, off)
                if not isinstance(v, int) or v < NBLK - 1:
                    act_high(v + 1, 1 - q, off + n)
                for j in range(6, 12):
                    split(n + j, off)

            with act.Fori(0, AHEAD // 2 - 1) as it:
                for e in range(2):
                    act_tail(it * 2 + (MAIN + e), e, n0 + 8 * e, it * 16)
            act_tail(NBLK - 2, 0, n0 + 8 * AHEAD - 16, 0)
            act_tail(NBLK - 1, 1, n0 + 8 * AHEAD - 8, 0)
            act.wait_ge(v_out, 8 * NBLK)
            for t in range(TT):
                sumsq(junk2[:], X[:, t], stat[:, 8 + t:9 + t])
            act.wait_ge(normed, 10)
            for t in range(TT):
                sumsq(junk2[:], X[:, t], stat[:, 8 + t:9 + t])
            act.wait_ge(mcol_ok, 1)
            turn("h3", 8, xh, scale=lambda k: mcol[:, 1, k:k + 1], bias=lambda k: mcol[:, 0, k:k + 1],
                 after=BASE["in2"])
            def mod2_splits(n, u, it):
                for j in range(2):
                    splits(n + 4 * j, 2, it * (2 * TC))
                    act.wait_ge(mod2_used, it * 4 + (u + j))
                    act.dma_start(mraw2[:], A["w_mod"][bass.ds(it * 4 + (5 * KD + u + j), 1)]
                                  .rearrange("a p n -> p (a n)")).then_inc(mod2_in, 16)
                    splits(n + 4 * j + 2, 2, it * (2 * TC))

            def qkvu(it):
                for ab in range(2):
                    mod2_splits(BASE["in2"] + ab * TC, 2 * ab, it)
                    evac(it * (2 * TC) + (BASE["in2"] + (1 + ab) * TC), ab,
                         lambda t: QKVU[:, t, bass.ds(it * 1024 + 512 * ab, CH)], ACT.Copy)

            with act.Fori(0, 2) as it:
                qkvu(it)
            for ab in range(2):
                act.wait_ge(acc_free[ab], 2 * (PB["in2"] + 2))
            for t in range(TT):
                SC.activation(sq2[:, t], QKVU[:, t, 0:2 * AW], ACT.Square).then_inc(qk_sq, 1)
                qkvu(2 + t)
            act.wait_ge(mod2_ps, 1)
            with act.Fori(0, 4) as it:
                for ab in range(2):
                    h, n = 16 + ab, BASE["in2"] + (8 + ab) * TC
                    splits(n, 2, it * (2 * TC))
                    act.wait_ge(qk_tr, it * 2 + (ab + 1))
                    SC.copy(qkT[:].rearrange("p a t -> p (a t)"), ps[:, 7]).then_inc(qk_out, 1)
                    splits(n + 2, 2, it * (2 * TC))
                    probs(h, sc2, pr2, stat_col, it * 2)
                    splits(n + 4, 2, it * (2 * TC))
                    probsT(h, pT2, 5, it * 2)
                    splits(n + 6, 2, it * (2 * TC))
                    evac(it * (2 * TC) + (n + TC), ab,
                         lambda t: G2[:, t, bass.ds(it * 1024 + 512 * ab, CH)], ACT.Sigmoid)
            for g in range(4):
                act.wait_ge(ut_ps, g + 1)
                SC.copy(uT[:, 2 * g:2 * g + 2], ps[:, 4 + g % 2].rearrange("p (k t) -> p k t", k=2)
                        ).then_inc(ut_ok, 1)
            act.wait_ge(sv_a, 3)
            SC.activation(sv[:, 8:10], sv[:, 6:8], ACT.Sin).then_inc(sv_s, 1)
            def phase(e, q, col):
                act.wait_ge(cs_ok, q * 3)
                act.wait_ge(ph_arg, q)
                for i in range(2):
                    turns = sv[:, 5, bass.ds(col + i, 1)] if not isinstance(col, int) else sv[:, 5, col + i:col + i + 1]
                    SC.activation(px[:, i], iota, ACT.Copy, scale=turns).then_inc(ph_x, 1)
                    SC.activation(pr_[:, i], iota, ACT.Identity, scale=turns, bias=K("magic")).then_inc(ph_x, 1)
                act.wait_ge(ph_arg, q + 1)
                if not isinstance(q, int) or q >= 2:
                    act.wait_ge(fw_ok, q * 2 - 2)
                SC.activation(cs[:, e, 0], pr_[:], ACT.Sin, scale=-TURN).then_inc(cs_ok, 1)
                act.wait_ge(cs_ok, q * 3 + 1)
                SC.activation(pr_[:], pr_[:], ACT.Abs).then_inc(cs_ok, 1)
                act.wait_ge(cs_ok, q * 3 + 2)
                SC.activation(cs[:, e, 1], pr_[:], ACT.Sin, scale=-TURN, bias=K("halfpi")).then_inc(cs_ok, 1)

            def b_copy(it):
                for i in range(2):
                    act.wait_ge(bl_ps, it * 2 + (i + 1))
                    SC.copy(bL[:, i].rearrange("p s n -> p (s n)"), ps[:, 6 + i]).then_inc(bl_ok, 1)

            def y_gelu(it):
                act.wait_ge(y_sum, it + 1)
                y = (yT[:, it] if isinstance(it, int) else yT[:, bass.ds(it, 1)].rearrange("p a t -> p (a t)"))
                SC.activation(y, y, ACT.Gelu_apprx_tanh).then_inc(y_ok, 1)

            def diagonal(m, src, it, sign, done):
                for half in range(2):
                    p0 = 64 * half
                    flat = m.rearrange("p s n -> p (s n)")[p0:p0 + 64]
                    dst = bass.AP(flat.tensor, flat.offset + GH * half,
                                  [list(flat.ap[0]), [P + 2 * GH, SB], [1, GH]])
                    block = src[p0:p0 + 64, it * SB:it * SB + SB] if isinstance(it, int) else \
                        src[p0:p0 + 64, bass.ds(it * SB, SB)]
                    SC.activation(dst, block, ACT.Copy, scale=sign).then_inc(done, 1)

            def b_blocks(it):
                act.wait_ge(bl_ps, it * 2)
                for i in range(2):
                    diagonal(bM[:, i], cB[:, i], it, 1.0, bm_ok)

            def c_blocks(it):
                act.wait_ge(y_ps, it * 2)
                for i in range(2):
                    diagonal(cM[:, i], ssmC[:, i], it, (1.0, -1.0)[i], cm_ok)

            phase(0, 0, 0)
            act.wait_ge(sv_s, 2)
            b_blocks(0)
            b_copy(0)
            phase(1, 1, 2)
            c_blocks(0)
            b_blocks(1)
            b_copy(1)
            phase(0, 2, 4)
            with act.Fori(1, 7) as it:
                phase(1, it * 2 + 1, it * SB + 2)
                y_gelu(it - 1)
                c_blocks(it)
                b_blocks(it + 1)
                b_copy(it + 1)
                phase(0, it * 2 + 2, it * SB + SB)
            phase(1, 15, 30)
            y_gelu(6)
            c_blocks(7)
            y_gelu(7)

            def spread_vector(dst, n):
                for q in range(4):
                    act.wait_ge(spread, 4 * n - 3 + q)
                    SC.copy(dst[:, CH * q:CH * q + CH], ps[:, 4 + q]).then_inc(spread_out, 1)

            spread_vector(g1b, 1)
            act.wait_ge(y_ok, 8)
            SC.copy(yh[:], yT[:]).then_inc(yspl_h, 1)
            splits(BASE["glu"], TA)
            evac(BASE["glu"] + TA, 0, lambda t: SG[:, t, 0:CH], ACT.Sigmoid)
            splits(BASE["glu"] + TA, TA)
            evac(BASE["glu"] + 2 * TA, 1, lambda t: SG[:, t, CH:2 * CH], ACT.Sigmoid)
            for g in range(4):
                act.wait_ge(y32_ok, g + 1)
                SC.copy(yh[:, 2 * g:2 * g + 2], Y32[:]).then_inc(yg_h, 1)
            turn("ya", 4, yah, after=BASE["abr"])
            splits(BASE["abr"], 4 * TA)
            splits(BASE["sbr"], 4 * TA)
            turn("merged2", 8, xh, after=BASE["out2"])
            splits(BASE["out2"], 4 * TC)
            act.wait_ge(acc_free[1], 2 * (PB["out2"] + 2))
            for t in range(TT):
                sumsq(junk2[:], X[:, t], stat[:, 8 + t:9 + t])
            act.wait_ge(mcol_ok, 2)
            turn("h4", 8, xh, scale=lambda k: mcol[:, 3, k:k + 1], bias=lambda k: mcol[:, 2, k:k + 1],
                 after=BASE["ffn"])

            n0 = BASE["ffn"]

            def up_evac(b, half, n):
                act.wait_ge(tile_used, n)
                if half == 0 and (not isinstance(b, int) or b):
                    act.wait_ge(up_T, b * 2)
                for t in range(TT):
                    SC.copy(UP[:, half, t], ps[:, 2 * half + t]).then_inc(up_out, 1)

            def conv_base(b, half):
                act.wait_ge(cc_ok, b + 1)
                act.wait_ge(up_T, b * 2 + (half + 1))
                for f in range(4):
                    q = 16 * half + 4 * f
                    SC.activation(cv[:, half, f], ps[:, 4 + 2 * half + f // 2, S * (f % 2):S * (f % 2) + S],
                                  ACT.Identity, scale=ccol[:, q + 2:q + 3], bias=ccol[:, q + 3:q + 4]
                                  ).then_inc(cv_base, 1)

            def silu(b):
                act.wait_ge(cv_ok, b * 2 + 2)
                SC.activation(sil[:], cv[:, 1], ACT.Silu).then_inc(sil_ok, 1)

            def act_high(b):
                act.wait_ge(f32_ok, b + 1)
                if not isinstance(b, int) or b:
                    act.wait_ge(tile_used, b * 24 + n0)
                SC.copy(Fh[:], F32t[:]).then_inc(fh_ok, 1)

            def hidden(b, rest):
                rest(2)
                conv_base(b, 0)
                rest(1)
                conv_base(b, 1)
                rest(2)
                silu(b)
                rest(2)
                act_high(b)

            spread_vector(g2b, 2)
            splits(n0, TC)
            up_evac(0, 0, n0 + TC)
            splits(n0 + TC, TC)
            up_evac(0, 1, n0 + 2 * TC)
            with act.Fori(1, FB) as b:
                off = b * 24 - 24
                local = [n0 + 16 + SPL]

                def rest(k):
                    for _ in range(k):
                        split(local[0], off)
                        local[0] += 1

                hidden(b - 1, rest)
                rest(1)
                up_evac(b, 0, off + (n0 + 24))
                rest(8)
                up_evac(b, 1, off + (n0 + 32))
                rest(8)
            hidden(FB - 1, lambda k: None)
            splits(TOTAL - 8, 8)
            for t in range(TT):
                act.wait_ge(y_done, t + 1)
                act.dma_start(out[t * P:(t + 1) * P, :], Y[:, t]).then_inc(o_st, 16)
            act.wait_ge(o_st, 32)

        @block.vector
        def _(dve):
            st = Steps(dve, dve_step)

            def split(n0, off=0):
                if n0 >= TOTAL:
                    return
                dve.wait_ge(hi_ready, n0 + 1 + off)
                V.tensor_tensor(lo[:, n0 % SPL], raw[:, n0 % RAW], hi[:, n0 % SPL].bitcast(F32),
                                ALU.subtract).then_inc(lo_ready, 1)

            def splits(n0, count, off=0):
                for j in range(count):
                    split(n0 + SPL + j, off)

            nroot = [0]
            nsq = [0]

            def mean_sq(n, width, sqs):
                nsq[0] += sqs
                dve.wait_ge(sq_ready, nsq[0])
                nroot[0] += 1
                V.tensor_scalar(stat[:, 0:n], stat[:, 8:8 + n], 1.0 / width, EPS, ALU.mult, ALU.add
                                ).then_inc(var_ready, 1)
                dve.wait_ge(rstd_ready, nroot[0])

            def turn(name, rounds, h, l, scale=None, bias=None, tmp=None):
                for r in range(rounds):
                    g = TBASE[name] + r
                    dve.wait_ge(turn_hi, 2 * g + 2)
                    bank = ps[:, 4 + g % 2].rearrange("p (k t) -> p k t", k=2)
                    kk = 2 * r
                    if scale is None:
                        V.tensor_tensor(l[:, kk:kk + 2], bank, h[:, kk:kk + 2].bitcast(F32), ALU.subtract
                                        ).then_inc(turn_lo, 1)
                        continue
                    if bias is not None:
                        if r:
                            dve.wait_ge(turn_lo, g)
                        for k in range(2):
                            st.step(V.tensor_scalar(tmp[:, k], bank[:, k], scale(kk + k), bias(kk + k),
                                                    ALU.mult, ALU.add))
                        st.wait()
                        V.tensor_tensor(l[:, kk:kk + 2], tmp[:], h[:, kk:kk + 2].bitcast(F32), ALU.subtract
                                        ).then_inc(turn_lo, 1)
                        continue
                    st.step(V.scalar_tensor_tensor(l[:, kk], bank[:, 0], scale(kk), h[:, kk].bitcast(F32),
                                                   ALU.mult, ALU.subtract))
                    V.scalar_tensor_tensor(l[:, kk + 1], bank[:, 1], scale(kk + 1), h[:, kk + 1].bitcast(F32),
                                           ALU.mult, ALU.subtract).then_inc(turn_lo, 1)

            dve.wait_ge(small_in, 64)
            st.link(V.tensor_copy(posf[:], posi[:]))
            for t in range(TT):
                st.step(V.tensor_scalar(ang[:, 0, 32 * t:32 * t + 32], K("freq"), posf[:, t:t + 1], None, ALU.mult))
                st.step(V.tensor_scalar(ang[:, 0, 64 + 64 * t:128 + 64 * t], K("freq2"), posf[:, 2 + t:3 + t],
                                        None, ALU.mult))
            st.wait()
            st.step(V.tensor_scalar(ang[:, 2], ang[:, 0], INV_2PI, None, ALU.mult))
            st.link(V.tensor_scalar(ang[:, 3], ang[:, 0], INV_2PI, 0.25, ALU.mult, ALU.add))
            st.link(V.tensor_scalar(ang[:, 2:4], ang[:, 2:4], MAGIC, None, ALU.add))
            st.link(V.tensor_scalar(ang[:, 2:4], ang[:, 2:4], MAGIC, None, ALU.subtract))
            both = ang[:, 0:1].to_broadcast([P, 2, 192])
            st.link(V.scalar_tensor_tensor(ang[:, 4:6], ang[:, 2:4], -C1, both, ALU.mult, ALU.add))
            st.link(V.scalar_tensor_tensor(ang[:, 4:6], ang[:, 2:4], -C2, ang[:, 4:6], ALU.mult, ALU.add))
            st.link(V.scalar_tensor_tensor(ang[:, 4:6], ang[:, 2:4], -C3, ang[:, 4:6], ALU.mult, ALU.add))
            st.link(V.tensor_scalar(ang[:, 5], ang[:, 5], math.pi / 2, None, ALU.add))
            V.tensor_scalar(ang[:, 4:6], ang[:, 4:6], PI_IN, -PI_IN, ALU.min, ALU.max).then_inc(trig_arg, 1)
            mean_sq(2, D, 2)
            for t in range(TT):
                V.tensor_scalar(N1[:, t], X[:, t], stat[:, 2 + t:3 + t], None, ALU.mult).then_inc(normed, 1)
            for j in range(SPL):
                split(j)
            turn("h1", 8, xh, xl, scale=lambda k: C("g1", k))
            splits(0, 2 * TC)
            with dve.Fori(0, 8) as it:
                splits(2 * TC, 2 * TC, it * (2 * TC))
            split(BASE["kpe"] + SPL)
            st.link(V.tensor_tensor(wsp[:], wsp[:], K("triu").unsqueeze(1).to_broadcast([P, SGU_G, P]), ALU.mult))
            dve.wait_ge(ln_sum, 2)
            V.tensor_scalar(stat[:, 18:20], stat[:, 16:18], -1.0 / D, None, ALU.mult).then_inc(ln_mu, 1)
            mean_sq(2, D, 2)
            dve.wait_ge(ln_in, 32)
            for t in range(TT):
                v = Z[:, t, D:2 * D]
                st.link(V.tensor_scalar(v, v, stat[:, 18 + t:19 + t], stat[:, 2 + t:3 + t], ALU.add, ALU.mult))
                st.link(V.tensor_tensor(v, v, lng[:], ALU.mult))
                V.tensor_tensor(v, v, lnb[:], ALU.add).then_inc(ln_done, 1)
            nsq[0] += 4
            dve.wait_ge(sq_ready, nsq[0])
            nroot[0] += 1
            V.tensor_scalar(stat[:, 0:4], stat[:, 10:14], 1.0 / LORA, EPS, ALU.mult, ALU.add).then_inc(var_ready, 1)
            dve.wait_ge(rstd_ready, nroot[0])
            for j, src in enumerate((CQ, CKV)):
                for t in range(TT):
                    V.tensor_scalar(src[:, t], src[:, t], stat[:, 4 + 2 * j + t:5 + 2 * j + t], None, ALU.mult
                                    ).then_inc(normed, 1)
            dve.wait_ge(kpe_out, 2)
            dve.wait_ge(trig_ok, 1)

            def rope32(dst, src, tmp, nh, done=None):
                for t in range(TT):
                    sn = trig[:, 0, 32 * t:32 * t + 32].unsqueeze(1).to_broadcast([P, nh, 32])
                    cn = trig[:, 1, 32 * t:32 * t + 32].unsqueeze(1).to_broadcast([P, nh, 32])
                    s4 = src[:, t].rearrange("p (h b w) -> p h b w", h=nh, b=2)
                    d4 = dst(t)
                    t4_ = tmp[:, t].rearrange("p (h w) -> p h w", h=nh)
                    st.step(V.tensor_tensor(d4[:, :, 0], s4[:, :, 0], cn, ALU.mult))
                    st.link(V.tensor_tensor(t4_, s4[:, :, 1], sn, ALU.mult))
                    st.link(V.tensor_tensor(d4[:, :, 0], d4[:, :, 0], t4_, ALU.subtract))
                    st.step(V.tensor_tensor(d4[:, :, 1], s4[:, :, 0], sn, ALU.mult))
                    st.link(V.tensor_tensor(t4_, s4[:, :, 1], cn, ALU.mult))
                    last = V.tensor_tensor(d4[:, :, 1], d4[:, :, 1], t4_, ALU.add)
                    if done is None:
                        st.link(last)
                    else:
                        last.then_inc(done, 1)

            rope32(lambda t: KPR[:, t, 0:64].rearrange("p (h b w) -> p h b w", h=1, b=2), KPE,
                   ktmp[:, :, 0:32], 1)
            for t in range(TT):
                V.tensor_copy(KPR[:, t, 64:128], KPR[:, t, 0:64]).then_inc(kpr_ok, 1)
            for t in range(TT):
                for g in range(SGU_G):
                    dve.wait_ge(mixed, t * 4 + g // 2 + 1)
                    u = Z[:, t, g * SGU_W:(g + 1) * SGU_W]
                    bank = ((4, 5, 6, 7), (0, 1, 2, 3))[t][g // 2]
                    V.scalar_tensor_tensor(u, ps[:, bank, SGU_W * (g % 2):SGU_W * (g % 2) + SGU_W],
                                           C("bsp", g), u, ALU.add, ALU.mult).then_inc(mixed_out, 1)
                dve.wait_ge(mixed_out, 8 * (t + 1))
                st.link(V.tensor_tensor(GT[:, t, D:2 * D], GT[:, t, D:2 * D], Z[:, t, 0:D], ALU.mult))
            turn("cq", 2, cqh, cql, scale=lambda k: C("gqa", k))
            turn("ckv", 2, ckh, ckl, scale=lambda k: C("gkva", k))

            def soft_in(h, s, bank, scale, off=0):
                b, q = h % 2, h % 2 if h >= 16 else h % 4
                dve.wait_ge(s_ready, h + 1 + off)
                if h >= 2 or not isinstance(off, int):
                    dve.wait_ge(p_ready, 2 * max(h - 1, 0) + off * 2)
                st.link(V.scalar_tensor_tensor(s[:, b], ps[:, bank, 0:384], scale, K("mask"), ALU.mult, ALU.add))
                st.step(V.tensor_reduce(stat[:, 144 + 2 * b:145 + 2 * b], s[:, b, 0:P], AX, ALU.max))
                st.link(V.tensor_reduce(stat[:, 145 + 2 * b:146 + 2 * b], s[:, b, P:384], AX, ALU.max))
                V.tensor_scalar(stat[:, 32 + 4 * q:34 + 4 * q], stat[:, 144 + 2 * b:146 + 2 * b], -1.0, None, ALU.mult
                                ).then_inc(s_max, 1)

            def soft_out(h, bank, dst, other, off=0):
                b, q = h % 2, h % 2 if h >= 16 else h % 4
                dve.wait_ge(p_ready, 2 * h + 2 + off * 2)
                st.link(V.reciprocal(stat[:, 148 + 2 * b:150 + 2 * b], stat[:, 34 + 4 * q:36 + 4 * q]))
                dve.wait_ge(o_ready, h + 1 + off)
                for t in range(TT):
                    o = ps[:, bank, P * t:P * t + P]
                    r = stat[:, 148 + 2 * b + t:149 + 2 * b + t]
                    if other is None:
                        V.tensor_scalar(dst(t), o, r, None, ALU.mult).then_inc(o_out, 1)
                    else:
                        V.scalar_tensor_tensor(dst(t), o, r, other(t), ALU.mult, ALU.mult).then_inc(o_out, 1)

            PER = 10 + 16
            with dve.Fori(0, 4) as it:
                st.enter(PER, it)
                n0 = BASE["mla"]
                splits(n0, 4 * TL, it * (4 * TL))
                dve.wait_ge(m_evac, it * 8 + 4)
                dve.wait_ge(m_tr, it * 3)
                rope32(lambda t: qrr[:, t].rearrange("p (h b w) -> p h b w", h=GROUP, b=2), qr, qtmp, GROUP, m_rope)
                dve.wait_ge(m_tr, it * 3 + 2)
                dve.wait_ge(s_ready, it * 4)
                V.tensor_copy(kT[:].rearrange("p h t -> p (h t)"), ps[:, 2:4].rearrange("p a n -> p (a n)")
                              ).then_inc(m_tv, 1)
                for h in range(GROUP + 2):
                    if h < GROUP:
                        soft_in(h, sc, 5 + h % 2, float(NOPE + ROPE) ** -0.5, it * 4)
                    if h >= 2:
                        g = h - 2
                        dst = lambda t: GT[:, t, bass.ds(it * CH + g * VH, VH)]
                        soft_out(g, g % 2, dst, dst, it * 4)
                st.leave(PER, 4)
            dve.wait_ge(o_out, 32)
            for t in range(TT):
                V.tensor_tensor(GT[:, t, 0:D], GT[:, t, 0:D], GT[:, t, D:2 * D], ALU.add).then_inc(merged_ok, 1)
            turn("merged", 8, xh, xl)
            for pair in range(2):
                for ab in range(2):
                    n = BASE["out"] + (2 * pair + ab) * TC
                    splits(n, TC)
                    dve.wait_ge(tile_used, n + TC)
                    for t in range(TT):
                        xs = X[:, t, 1024 * pair + 512 * ab:1024 * pair + 512 * ab + CH]
                        V.tensor_tensor(xs, xs, ps[:, 2 * ab + t], ALU.add).then_inc(acc_free[ab], 1)
            dve.wait_ge(acc_free[0], 22)
            dve.wait_ge(acc_free[1], 22)
            mean_sq(2, D, 2)
            for t in range(TT):
                V.tensor_scalar(N2[:, t], X[:, t], stat[:, 2 + t:3 + t], None, ALU.mult).then_inc(normed, 1)
            turn("h2", 8, xh, xl, scale=lambda k: C("g2", k))
            splits(BASE["pq"], 4 * TC)

            early = [BASE["peer"] + SPL]

            def stream():
                split(early[0])
                early[0] += 1

            dve.wait_ge(sub_ok, 8)
            for i in range(32):
                st.step(V.max(vals[:, i, 0:8], sub[:, i]))
                if i % 4 == 3:
                    stream()
            st.wait()
            for i in range(32):
                st.step(V.max_index(vidx[:, i, 0:8], vals[:, i, 0:8], sub[:, i]))
                st.step(V.match_replace(sub2[:, i], vals[:, i, 0:8], sub[:, i], -3e38))
                if i % 2 == 1:
                    stream()
            st.wait()
            for i in range(32):
                st.step(V.max(vals[:, i, 8:16], sub2[:, i]))
                if i % 4 == 3:
                    stream()
            st.wait()
            for i in range(32):
                st.step(V.max_index(vidx[:, i, 8:16], vals[:, i, 8:16], sub2[:, i]))
                if i % 4 == 3:
                    stream()
            st.wait()
            v5 = vals[:].rearrange("p (h q t) k -> p t h q k", h=PH, q=2, t=TT)
            f5 = vidf[:].rearrange("p (h q t) k -> p t h q k", h=PH, q=2, t=TT)
            st.step(V.tensor_copy(vidf[:], vidx[:]))
            for t in range(TT):
                st.step(V.tensor_tensor(
                    cand[:, 8 * t:8 * t + 8].rearrange("p h (a b) -> p h a b", a=TOPK),
                    v5[:, t, :, 0].unsqueeze(3).to_broadcast([P, PH, TOPK, TOPK]),
                    v5[:, t, :, 1].unsqueeze(2).to_broadcast([P, PH, TOPK, TOPK]), ALU.add))
                stream()
            st.wait()
            for i in range(16):
                st.step(V.max(tops[:, i, 0:8], cand[:, i]))
                if i % 4 == 3:
                    stream()
            st.wait()
            for i in range(16):
                st.step(V.max_index(tpos[:, i, 0:8], tops[:, i, 0:8], cand[:, i]))
                st.step(V.match_replace(cand2[:, i], tops[:, i, 0:8], cand[:, i], -3e38))
                if i % 2 == 1:
                    stream()
            st.wait()
            for i in range(16):
                st.step(V.max(tops[:, i, 8:16], cand2[:, i]))
                if i % 4 == 3:
                    stream()
            st.wait()
            for i in range(16):
                st.step(V.max_index(tpos[:, i, 8:16], tops[:, i, 8:16], cand2[:, i]))
                if i % 4 == 3:
                    stream()
            tg = sel[:, 2].rearrange("p t (h k) -> p (t h) k", h=PH)
            st.wait()
            V.tensor_tensor(tg, tops[:], tops[:, :, 0:1].to_broadcast([P, 16, TOPK]), ALU.subtract
                            ).then_inc(gate_in, 1)
            tp = tpos[:].rearrange("p i k -> p (i k)")
            st.step(V.tensor_scalar(tab[:, 0], tp, 4, None, ALU.logical_shift_right))
            st.link(V.tensor_scalar(tab[:, 1], tp, 15, None, ALU.bitwise_and))
            st.link(V.tensor_copy(tabf[:], tab[:]))
            for q in range(2):
                for t in range(TT):
                    sl = tabf[:, q, 128 * t:128 * t + 128].rearrange("p (h k) -> p h k", h=PH)
                    st.link(V.tensor_tensor(eq[:], sl.unsqueeze(3).to_broadcast([P, PH, TOPK, TOPK]),
                                            iota[:, 0:TOPK].unsqueeze(1).unsqueeze(1).to_broadcast([P, PH, TOPK, TOPK]),
                                            ALU.is_equal))
                    st.link(V.tensor_tensor(eq[:], eq[:],
                                            f5[:, t, :, q].unsqueeze(2).to_broadcast([P, PH, TOPK, TOPK]), ALU.mult))
                    stream()
                    stream()
                    st.link(V.tensor_reduce(sel[:, q, t].rearrange("p (h k) -> p h k", h=PH), eq[:], AX, ALU.add))
                    stream()
            while early[0] < BASE["peer"] + 2 + CHOICE * TC:
                stream()
            dve.wait_ge(gate_exp, 1)
            st.link(V.tensor_reduce(stat[:, 80:96], tg, AX, ALU.add))
            st.link(V.reciprocal(stat[:, 96:112], stat[:, 80:96]))
            V.tensor_tensor(tg, tg, stat[:, 96:112].unsqueeze(2).to_broadcast([P, 16, TOPK]), ALU.mult
                            ).then_inc(sel_ok, 1)
            dve.wait_ge(selT_ok, 3)
            n0 = BASE["peer"]
            with dve.Fori(0, 2) as it:
                for e in range(2):
                    for g in range(GQ // GT4):
                        b = g % 2
                        c0 = GQ * e + GT4 * g
                        dve.wait_ge(g_ps[b], it * 16 + (8 * e + g // 2))
                        V.tensor_tensor(oh1[:, b], iota[:, 0:P].unsqueeze(1).to_broadcast([P, GT4, P]),
                                        selT[:, 0, bass.ds(it * (2 * GQ) + c0, GT4)].unsqueeze(2)
                                        .to_broadcast([P, GT4, P]), ALU.is_equal).then_inc(oh_ready[b], 1)
                        for k in range(GT4):
                            V.tensor_scalar(oh2[:, b, k], iota[:, 0:P],
                                            selT[:, 1, bass.ds(it * (2 * GQ) + (c0 + k), 1)],
                                            selT[:, 2, bass.ds(it * (2 * GQ) + (c0 + k), 1)],
                                            ALU.is_equal, ALU.mult).then_inc(oh_ready[b], 1)
                        if b:
                            split(n0 + (CHOICE + e) * TC + 2 + g // 2, it * (2 * TC))
            for j in range((AHEAD - CHOICE - GATES) * TC + 2):
                split(n0 + (CHOICE + GATES) * TC + 2 + j)

            n0 = BASE["peer"] + AHEAD * TC
            dve.wait_ge(csil, 1)

            def mod_unit(u, rr):
                dve.wait_ge(mod_in[u % 4], rr * 64 + 16 * (u // 4 + 1))
                if u == 0:
                    dve.wait_ge(mod_ps, rr)
                    V.tensor_scalar(macc[:], mraw[:, 0], stat[:, 64:65], None, ALU.mult).then_inc(mod_used, 1)
                    return
                dve.wait_ge(mod_used, rr * KD + u)
                V.scalar_tensor_tensor(macc[:], mraw[:, u % 4], stat[:, 64 + u:65 + u], macc[:],
                                       ALU.mult, ALU.add).then_inc(mod_used, 1)

            def gate(v, q, loads):
                dve.wait_ge(a_T, v + 1)
                dve.wait_ge(g_in[q], loads)
                if not isinstance(v, int) or v >= 2:
                    dve.wait_ge(ph_ok, v - 1)
                    dve.wait_ge(pl_ok, v - 1)
                for k in range(2):
                    V.tensor_tensor(P32[:, q, 2 * k:2 * k + 2].rearrange("p k (c n) -> p k c n", c=S // GQ),
                                    ps[:, 2 + k].rearrange("p (k c n) -> p k c n", k=2, c=S // GQ),
                                    Gb[:, q, :, 2 * k:2 * k + 2].rearrange("p c k n -> p k c n"), ALU.mult
                                    ).then_inc(gated, 1)

            def low(v, q):
                dve.wait_ge(ph_ok, v + 1)
                dve.wait_ge(gated, v * 2 + 2)
                V.tensor_tensor(Pl[:, q], P32[:, q], Ph[:, q].bitcast(F32), ALU.subtract).then_inc(pl_ok, 1)

            def v_add(v, c, n):
                dve.wait_ge(tile_used, n)
                if not isinstance(v, int) or v:
                    dve.wait_ge(v_out, v * 8)
                for t in range(TT):
                    xs = X[:, t, c * CH:(c + 1) * CH]
                    V.tensor_tensor(xs, xs, ps[:, 4 + 2 * (c % 2) + t], ALU.add).then_inc(v_out, 1)

            gate(0, 0, 16)
            low(0, 0)
            with dve.Fori(0, MAIN // 4) as rr:
                for i in range(4):
                    n, off, v = n0 + 16 * i, rr * 64, rr * 4 + i
                    for j in range(4):
                        split(n + 4 + 2 * j, off)
                        split(n + 5 + 2 * j, off)
                        mod_unit(4 * i + j, rr)
                    split(n + 12, off)
                    gate(v + 1, (i + 1) % 2, rr * 32 + 16 * ((i + 1) // 2 + 1))
                    split(n + 13, off)
                    v_add(v, 0, off + (n + 10))
                    low(v + 1, (i + 1) % 2)
                    for c in range(1, 4):
                        split(n + 12 + 2 * c, off)
                        split(n + 13 + 2 * c, off)
                        v_add(v, c, off + (n + 10 + 2 * c))
                dve.wait_ge(mod_ps, rr + 1)
                V.tensor_tensor(mcol[:, bass.ds(rr, 1)].rearrange("p a k -> p (a k)"), ps[:, 0, 0:KD],
                                cols[:, bass.ds(rr * KD + COFF["bmod"], KD)], ALU.add).then_inc(mod_col, 1)
            n0 += 16 * MAIN

            dve.wait_ge(mod_ps, 4)
            st.link(V.memset(macc[:], 0.0))

            def dve_tail(v, q, n, off, loads, mods):
                last = isinstance(v, int) and v == NBLK - 1
                if not last:
                    gate(v + 1, 1 - q, loads)
                split(n + 4, off)
                split(n + 5, off)
                v_add(v, 0, off + (n + 2))
                if not last:
                    low(v + 1, 1 - q)
                for c in range(1, 4):
                    split(n + 4 + 2 * c, off)
                    split(n + 5 + 2 * c, off)
                    v_add(v, c, off + (n + 2 + 2 * c))
                    if c == 1:
                        dve.wait_ge(mod_in[q], mods)
                        dve.wait_ge(mod_used, v + (4 * KD - MAIN))
                        k = v + (64 - MAIN)
                        V.scalar_tensor_tensor(macc[:], mraw[:, q], stat[:, k:k + 1] if isinstance(k, int) else
                                               stat[:, bass.ds(k, 1)], macc[:], ALU.mult, ALU.add
                                               ).then_inc(mod_used, 1)

            with dve.Fori(0, AHEAD // 2 - 1) as it:
                for e in range(2):
                    dve_tail(it * 2 + (MAIN + e), e, n0 + 8 * e, it * 16,
                             it * 16 + 16 * ((MAIN + e + 1) // 2 + 1), it * 16 + (16 * KD + 16))
            dve_tail(NBLK - 2, 0, n0 + 8 * AHEAD - 16, 0, 16 * (NBLK // 2), 16 * KD + 8 * AHEAD)
            dve_tail(NBLK - 1, 1, n0 + 8 * AHEAD - 8, 0, None, 16 * KD + 8 * AHEAD)
            dve.wait_ge(v_out, 8 * NBLK)
            mean_sq(2, D, 2)
            dve.wait_ge(gfin_in, 16)
            for t in range(TT):
                V.scalar_tensor_tensor(X[:, t], X[:, t], stat[:, 2 + t:3 + t], gfin[:], ALU.mult, ALU.mult
                                       ).then_inc(normed, 1)
            dve.wait_ge(mod_ps, 5)
            V.tensor_tensor(mcol[:, 4], ps[:, 0, 0:KD], C("bmod", 4 * KD, KD), ALU.add).then_inc(mod_col, 1)
            dve.wait_ge(mod_col, 4)
            V.scalar_tensor_tensor(mcol[:, 1], mcol[:, 1], 1.0, C("g3", 0, KD), ALU.add, ALU.mult).then_inc(mcol_ok, 1)
            dve.wait_ge(normed, 10)
            mean_sq(2, D, 2)
            for t in range(TT):
                V.tensor_scalar(N3[:, t], X[:, t], stat[:, 2 + t:3 + t], None, ALU.mult).then_inc(normed, 1)
            dve.wait_ge(mcol_ok, 1)
            turn("h3", 8, xh, xl, scale=lambda k: mcol[:, 1, k:k + 1], bias=lambda k: mcol[:, 0, k:k + 1], tmp=t3)
            st.link(V.memset(macc2[:], 0.0))

            def qkvu(it, between):
                for u in range(4):
                    splits(BASE["in2"] + 4 * u, 4, it * (2 * TC))
                    dve.wait_ge(mod2_in, it * 64 + (16 * u + 16))
                    dve.wait_ge(mod2_used, it * 4 + u)
                    V.scalar_tensor_tensor(macc2[:], mraw2[:], stat[:, bass.ds(it * 4 + (64 + u), 1)], macc2[:],
                                           ALU.mult, ALU.add).then_inc(mod2_used, 1)
                    between(u)

            with dve.Fori(0, 2) as it:
                qkvu(it, lambda u: None)

            def qk_sums(u):
                if u in (1, 3):
                    t = u // 2
                    dve.wait_ge(qk_sq, t + 1)
                    st.step(V.tensor_reduce(stat[:, 112 + 16 * t:128 + 16 * t], heads_rows(sq2[:, t], 16, AD), AX, ALU.add))

            def qk_norm(u):
                t = u // 2
                v = QKVU[:, t, 0:2 * AW]
                if u % 2 == 0:
                    v3 = heads_rows(v, 16, AD)
                    st.step(V.tensor_tensor(v3, v3, stat[:, 32 + 16 * t:48 + 16 * t].unsqueeze(2)
                                            .to_broadcast([P, 16, AD]), ALU.mult))
                else:
                    st.wait()
                    v4 = v.rearrange("p (a h w) -> p a h w", a=2, h=AH)
                    st.step(V.tensor_tensor(v4, v4, gqk[:].unsqueeze(2).to_broadcast([P, 2, AH, AD]), ALU.mult))

            qkvu(2, lambda u: qk_sums(u) if u == 1 else None)
            splits(BASE["in2"], 4, 6 * TC)
            qk_sums(3)
            st.wait()
            nroot[0] += 1
            V.tensor_scalar(stat[:, 0:32], stat[:, 112:144], 1.0 / AD, EPS, ALU.mult, ALU.add).then_inc(var_ready, 1)
            dve.wait_ge(gfin_in, 48)

            def qkvu_last():
                for u in range(4):
                    if u:
                        splits(BASE["in2"] + 4 * u, 4, 6 * TC)
                    else:
                        dve.wait_ge(rstd_ready, nroot[0])
                    dve.wait_ge(mod2_in, 16 * (13 + u))
                    dve.wait_ge(mod2_used, 12 + u)
                    V.scalar_tensor_tensor(macc2[:], mraw2[:], stat[:, 76 + u:77 + u], macc2[:],
                                           ALU.mult, ALU.add).then_inc(mod2_used, 1)
                    qk_norm(u)

            qkvu_last()
            st.wait()

            def rope64(h):
                x = QKVU[:, :, 0:2 * AW].rearrange("p t (a c) -> p t a c", a=2)
                x1, x2 = (x[:, :, :, bass.ds(h * AD + 64 * b, 64)] for b in range(2))
                sn, cn = (trig[:, i, 64:192].rearrange("p (t w) -> p t w", t=TT).unsqueeze(2)
                          .to_broadcast([P, TT, 2, 64]) for i in range(2))
                ta, tb = (rt[:, i].rearrange("p (t a w) -> p t a w", t=TT, a=2) for i in range(2))
                st.step(V.tensor_tensor(ta, x1, cn, ALU.mult))
                st.link(V.tensor_tensor(tb, x2, sn, ALU.mult))
                dve.wait_ge(qk_tr, h)
                st.link(V.tensor_tensor(rqk[:, :, :, 0:64], ta, tb, ALU.subtract))
                st.step(V.tensor_tensor(ta, x1, sn, ALU.mult))
                st.link(V.tensor_tensor(tb, x2, cn, ALU.mult))
                V.tensor_tensor(rqk[:, :, :, 64:128], ta, tb, ALU.add).then_inc(qk_rope, 1)
                dve.wait_ge(qk_rope, h + 1)

            dve.wait_ge(mod2_ps, 1)
            V.tensor_tensor(mcol[:, 5], ps[:, 4, 0:KD], C("bmod", 5 * KD, KD), ALU.add).then_inc(mod_col, 1)
            with dve.Fori(0, 4) as it:
                st.enter(18, it)
                for ab in range(2):
                    h, n = 16 + ab, BASE["in2"] + (8 + ab) * TC
                    rope64(it * 2 + ab)
                    splits(n, 4, it * (2 * TC))
                    soft_in(h, sc2, 4, float(AD) ** -0.5, it * 2)
                    splits(n + 4, 4, it * (2 * TC))
                    soft_out(h, 6, lambda t: QKVU[:, t, bass.ds(it * (2 * AD) + ab * AD, AD)], None, it * 2)
                st.leave(18, 4)
            dve.wait_ge(o_out, 48)
            dve.wait_ge(ut_ok, 4)
            V.memset(sv[:, 0], math.e).then_inc(sv_a, 1)
            st.link(V.memset(bM[:], 0.0))
            st.link(V.memset(cM[:], 0.0))
            dve.wait_ge(sv_p, 1)
            st.step(V.tensor_tensor(sv[:, 2], C("lim", 0, STT), sv[:, 1], ALU.mult))
            V.tensor_tensor(sv[:, 3], C("lre", 0, STT), sv[:, 1], ALU.mult).then_inc(sv_a, 1)
            st.wait()
            st.step(V.tensor_scalar(sv[:, 10], sv[:, 2], INV_2PI, None, ALU.mult))
            st.link(V.tensor_scalar(sv[:, 11], sv[:, 2], INV_2PI, 0.25, ALU.mult, ALU.add))
            st.link(V.tensor_scalar(sv[:, 10:12], sv[:, 10:12], MAGIC, None, ALU.add))
            st.link(V.tensor_scalar(sv[:, 10:12], sv[:, 10:12], MAGIC, None, ALU.subtract))
            both = sv[:, 2:3].to_broadcast([P, 2, STT])
            st.link(V.scalar_tensor_tensor(sv[:, 6:8], sv[:, 10:12], -C1, both, ALU.mult, ALU.add))
            st.link(V.scalar_tensor_tensor(sv[:, 6:8], sv[:, 10:12], -C2, sv[:, 6:8], ALU.mult, ALU.add))
            st.link(V.scalar_tensor_tensor(sv[:, 6:8], sv[:, 10:12], -C3, sv[:, 6:8], ALU.mult, ALU.add))
            st.step(V.tensor_scalar(sv[:, 5], sv[:, 6], INV_2PI, None, ALU.mult))
            st.link(V.tensor_scalar(sv[:, 7], sv[:, 7], math.pi / 2, None, ALU.add))
            V.tensor_scalar(sv[:, 6:8], sv[:, 6:8], PI_IN, -PI_IN, ALU.min, ALU.max).then_inc(sv_a, 1)
            st.step(V.tensor_tensor(sv[:, 12], C("lre", 0, STT), C("lre", 0, STT), ALU.mult))
            st.link(V.tensor_tensor(sv[:, 13], C("lim", 0, STT), C("lim", 0, STT), ALU.mult))
            st.link(V.tensor_tensor(sv[:, 12], sv[:, 12], sv[:, 13], ALU.add))
            st.link(V.reciprocal(sv[:, 12], sv[:, 12]))
            dve.wait_ge(sv_s, 1)
            dve.wait_ge(sv_p, 2)
            st.step(V.tensor_tensor(sv[:, 14], sv[:, 4], sv[:, 9], ALU.mult))
            st.link(V.tensor_tensor(sv[:, 15], sv[:, 4], sv[:, 8], ALU.mult))
            st.link(V.tensor_scalar(sv[:, 14], sv[:, 14], -1.0, None, ALU.add))
            st.step(V.tensor_tensor(sv[:, 16], sv[:, 14], C("lre", 0, STT), ALU.mult))
            st.step(V.tensor_tensor(sv[:, 17], sv[:, 15], C("lim", 0, STT), ALU.mult))
            st.step(V.tensor_tensor(sv[:, 18], sv[:, 15], C("lre", 0, STT), ALU.mult))
            st.link(V.tensor_tensor(sv[:, 19], sv[:, 14], C("lim", 0, STT), ALU.mult))
            st.step(V.tensor_tensor(sv[:, 16], sv[:, 16], sv[:, 17], ALU.add))
            st.link(V.tensor_tensor(sv[:, 18], sv[:, 18], sv[:, 19], ALU.subtract))
            st.step(V.tensor_tensor(sv[:, 16], sv[:, 16], sv[:, 12], ALU.mult))
            st.link(V.tensor_tensor(sv[:, 18], sv[:, 18], sv[:, 12], ALU.mult))
            cr = sv[:, 16].unsqueeze(2).to_broadcast([P, STT, GH])
            ci = sv[:, 18].unsqueeze(2).to_broadcast([P, STT, GH])
            tmp = rb[:, 0].rearrange("p s t -> p (s t)").rearrange("p (s h) -> p s h", s=STT)
            dve.wait_ge(ssm_in, 64)
            st.step(V.tensor_tensor(cB[:, 0], ssmB[:, 0], cr, ALU.mult))
            st.link(V.tensor_tensor(tmp, ssmB[:, 1], ci, ALU.mult))
            st.link(V.tensor_tensor(cB[:, 0], cB[:, 0], tmp, ALU.subtract))
            st.step(V.tensor_tensor(cB[:, 1], ssmB[:, 1], cr, ALU.mult))
            st.link(V.tensor_tensor(tmp, ssmB[:, 0], ci, ALU.mult))
            V.tensor_tensor(cB[:, 1], cB[:, 1], tmp, ALU.add).then_inc(sv_s, 1)
            dve.wait_ge(sv_s, 2)

            def remainder(q):
                dve.wait_ge(ph_x, q * 4 + 4)
                V.scalar_tensor_tensor(pr_[:], pr_[:], MAGIC, px[:], ALU.subtract, ALU.subtract).then_inc(ph_arg, 1)

            def states(e, q, col):
                sn, cn, zr, zi = cs[:, e, 0], cs[:, e, 1], rz[:, e, 0], rz[:, e, 1]
                dve.wait_ge(cs_ok, q * 3 + 3)
                dve.wait_ge(bu_ps, q + 1)
                if not isinstance(q, int) or q >= 2:
                    dve.wait_ge(y_ps, q - 1)
                bre, bim = (ps[:, 2 * e + i].rearrange("p (s t) -> p s t", s=2) for i in range(2))
                st.step(V.tensor_tensor(rb[:, 0], bre, cn, ALU.mult))
                st.step(V.tensor_tensor(zr, bim, sn, ALU.mult))
                st.step(V.tensor_tensor(rb[:, 1], bim, cn, ALU.mult))
                st.link(V.tensor_tensor(zi, bre, sn, ALU.mult))
                V.tensor_tensor(rb[:, 0], rb[:, 0], zr, ALU.add).then_inc(rot_ok, 1)
                V.tensor_tensor(rb[:, 1], rb[:, 1], zi, ALU.subtract).then_inc(rot_ok, 1)
                dve.wait_ge(rot_ok, q * 2 + 2)
                for i in range(2):
                    decay = sv[:, 4, bass.ds(col + i, 1)] if not isinstance(col, int) else sv[:, 4, col + i:col + i + 1]
                    for part in range(2):
                        st.step(V.tensor_tensor_scan(rz[:, e, part, i], decay.to_broadcast([P, S]), rb[:, part, i],
                                                     0.0, ALU.mult, ALU.add))
                st.wait()
                st.step(V.tensor_tensor(fw[:, e, 0], zr, cn, ALU.mult))
                st.link(V.scalar_tensor_tensor(fw[:, e, 1], zi, -1.0, sn, ALU.mult, ALU.mult))
                V.tensor_tensor(zr, zr, sn, ALU.mult).then_inc(fw_ok, 1)
                V.tensor_tensor(zi, zi, cn, ALU.mult).then_inc(fw_ok, 1)

            def y_add(it):
                dve.wait_ge(y_ps, it * 2 + 2)
                if isinstance(it, int):
                    y, u, d = yT[:, it], uT[:, it], C("dskip", it)
                else:
                    y, u = (a[:, bass.ds(it, 1)].rearrange("p a t -> p (a t)") for a in (yT, uT))
                    d = cols[:, bass.ds(it + COFF["dskip"], 1)]
                V.scalar_tensor_tensor(y, u, d, ps[:, 4, 0:S], ALU.mult, ALU.add).then_inc(y_sum, 1)

            remainder(0)
            remainder(1)
            states(0, 0, 0)
            remainder(2)
            states(1, 1, 2)
            with dve.Fori(1, 7) as it:
                st.enter(20, it - 1)
                remainder(it * 2 + 1)
                states(0, it * 2, it * SB)
                y_add(it - 1)
                remainder(it * 2 + 2)
                states(1, it * 2 + 1, it * SB + 2)
                st.leave(20, 6)
            remainder(15)
            states(0, 14, 28)
            y_add(6)
            states(1, 15, 30)
            y_add(7)

            def diagonals(dg, row):
                for k in range(KD):
                    V.tensor_scalar(dg[:, k], ident, mcol[:, row, k:k + 1], None, ALU.mult).then_inc(dg_ok, 1)

            dve.wait_ge(y_sum, 8)
            dve.wait_ge(mod_col, 5)
            diagonals(dg1, 4)
            dve.wait_ge(yspl_h, 1)
            V.tensor_tensor(yl[:], yT[:], yh[:].bitcast(F32), ALU.subtract).then_inc(yspl_l, 1)
            splits(BASE["glu"], 2 * TA)
            for g in range(4):
                dve.wait_ge(sg_T, g + 1)
                if g:
                    dve.wait_ge(yg_l, g)
                V.tensor_tensor(Y32[:], ps[:, 4 + g % 2].rearrange("p (k t) -> p k t", k=2),
                                yT[:, 2 * g:2 * g + 2], ALU.mult).then_inc(y32_ok, 1)
                dve.wait_ge(yg_h, g + 1)
                V.tensor_tensor(yl[:, 2 * g:2 * g + 2], Y32[:], yh[:, 2 * g:2 * g + 2].bitcast(F32), ALU.subtract
                                ).then_inc(yg_l, 1)
            turn("ya", 4, yah, yal)
            for br, name in enumerate(("abr", "sbr")):
                for pair in range(2):
                    for ab in range(2):
                        n = BASE[name] + (2 * pair + ab) * TA
                        splits(n, TA)
                        dve.wait_ge(tile_used, n + TA)
                        for t in range(TT):
                            c0 = 1024 * pair + 512 * ab
                            g = G2[:, t, br * D + c0:br * D + c0 + CH]
                            m = M2[:, t, c0:c0 + CH]
                            if br == 0:
                                V.tensor_tensor(m, ps[:, 2 * ab + t], g, ALU.mult).then_inc(acc_free[ab], 1)
                            else:
                                V.tensor_tensor(btmp[:, t], ps[:, 2 * ab + t], g, ALU.mult).then_inc(acc_free[ab], 1)
                                dve.wait_ge(acc_free[ab], 2 * (PB[name] + pair) + t + 1)
                                V.tensor_tensor(m, m, btmp[:, t], ALU.add).then_inc(br_out, 1)
            turn("merged2", 8, xh, xl)
            dve.wait_ge(spread_out, 4)
            for pair in range(2):
                for ab in range(2):
                    n = BASE["out2"] + (2 * pair + ab) * TC
                    splits(n, TC)
                    dve.wait_ge(tile_used, n + TC)
                    for t in range(TT):
                        c0 = 1024 * pair + 512 * ab
                        st.link(V.tensor_tensor(btmp[:, t], ps[:, 2 * ab + t], g1b[:, c0:c0 + CH], ALU.mult))
                        xs = X[:, t, c0:c0 + CH]
                        V.tensor_tensor(xs, xs, btmp[:, t], ALU.add).then_inc(acc_free[ab], 1)
            dve.wait_ge(acc_free[0], 2 * (PB["out2"] + 2))
            dve.wait_ge(acc_free[1], 2 * (PB["out2"] + 2))
            mean_sq(2, D, 2)
            V.scalar_tensor_tensor(mcol[:, 3], mcol[:, 3], 1.0, C("g4", 0, KD), ALU.add, ALU.mult).then_inc(mcol_ok, 1)
            for t in range(TT):
                V.tensor_scalar(N4[:, t], X[:, t], stat[:, 2 + t:3 + t], None, ALU.mult).then_inc(normed, 1)
            dve.wait_ge(mcol_ok, 2)
            turn("h4", 8, xh, xl, scale=lambda k: mcol[:, 3, k:k + 1], bias=lambda k: mcol[:, 2, k:k + 1], tmp=t4)

            st.link(V.memset(Y[:], 0.0))
            n0 = BASE["ffn"]

            def conv(b, half):
                for tap in range(2):
                    if tap == 0:
                        dve.wait_ge(cv_base, b * 8 + (4 * half + 4))
                    else:
                        st.wait()
                    for f in range(4):
                        q = 16 * half + 4 * f
                        d = 1 + tap
                        src = ps[:, 4 + 2 * half + f // 2, S * (f % 2):S * (f % 2) + S - d]
                        dst = cv[:, half, f, d:S]
                        ins = V.scalar_tensor_tensor(dst, src, ccol[:, q + 1 - tap:q + 2 - tap], dst,
                                                     ALU.mult, ALU.add)
                        if tap and f == 3:
                            ins.then_inc(cv_ok, 1)
                        else:
                            st.step(ins)

            def conv_cols(b):
                V.tensor_copy(ccol[:], cols[:, bass.ds(b * 32 + COFF["conv"], 32)] if not isinstance(b, int)
                              else C("conv", 32 * b, 32)).then_inc(cc_ok, 1)
                dve.wait_ge(cc_ok, b + 1)

            def product(b):
                dve.wait_ge(sil_ok, b + 1)
                dve.wait_ge(cv_ok, b * 2 + 2)
                V.tensor_tensor(F32t[:], cv[:, 0], sil[:], ALU.mult).then_inc(f32_ok, 1)

            def flow(b):
                dve.wait_ge(fh_ok, b + 1)
                dve.wait_ge(f32_ok, b + 1)
                V.tensor_tensor(Fl[:], F32t[:], Fh[:].bitcast(F32), ALU.subtract).then_inc(fl_ok, 1)

            def y_add(b, c, n):
                dve.wait_ge(tile_used, n)
                if not isinstance(b, int) or b:
                    dve.wait_ge(dn_out, b * 8)
                for t in range(TT):
                    ys = Y[:, t, c * CH:(c + 1) * CH]
                    V.tensor_tensor(ys, ys, ps[:, 4 + 2 * (c % 2) + t], ALU.add).then_inc(dn_out, 1)

            def hidden(b, rest):
                conv_cols(b)
                rest(2)
                conv(b, 0)
                rest(2)
                conv(b, 1)
                rest(2)
                product(b)
                rest(2)
                flow(b)

            diagonals(dg2, 5)
            splits(n0, 2 * TC)
            with dve.Fori(1, FB) as b:
                st.enter(14, b - 1)
                off = b * 24 - 24
                local = [n0 + 16 + SPL]

                def rest(k):
                    for _ in range(k):
                        split(local[0], off)
                        local[0] += 1

                hidden(b - 1, rest)
                rest(8)
                for c in range(4):
                    rest(2)
                    y_add(b - 1, c, off + (n0 + 34 + 2 * c))
                st.leave(14, FB - 1)
            hidden(FB - 1, lambda k: None)
            splits(TOTAL - 8, 4)
            for c in range(4):
                y_add(FB - 1, c, TOTAL - 6 + 2 * c)
            dve.wait_ge(dn_out, 8 * FB)
            dve.wait_ge(spread_out, 8)
            for t in range(TT):
                st.link(V.tensor_tensor(Y[:, t], Y[:, t], g2b[:], ALU.mult))
                V.tensor_tensor(Y[:, t], Y[:, t], X[:, t], ALU.add).then_inc(y_done, 1)

        @block.tensor
        def _(pe):
            def tile(n0, off, xhi, xlo, k0, banks, start, stop_, w=CH):
                pe.wait_ge(lo_ready, n0 + 1 + off)
                for k in range(SL):
                    H = hi[:, n0 % SPL, k * w:(k + 1) * w]
                    L = lo[:, n0 % SPL, k * w:(k + 1) * w]
                    for t in range(TT):
                        acc = ps[:, banks + t, 0:w]
                        xs = slice(t * P, (t + 1) * P)
                        s0 = start and k == 0
                        s1 = stop_ and k == SL - 1
                        PE_.matmul(acc, xhi[:, k0 + k, xs], H, start=s0, stop=False)
                        PE_.matmul(acc, xhi[:, k0 + k, xs], L, start=False, stop=False)
                        mm = PE_.matmul(acc, xlo[:, k0 + k, xs], H, start=False, stop=s1)
                mm.then_inc(tile_used, 1)

            def chunk(n0, off, tiles, ab, pair, xhi, xlo, bias=None):
                if not isinstance(pair, int) or pair:
                    pe.wait_ge(acc_free[ab], pair * 2)
                if bias is not None:
                    for t in range(TT):
                        mm = PE_.matmul(ps[:, 2 * ab + t], ones[0:1, :], bias, start=True, stop=False)
                    if ab:
                        mm.then_inc(bias_used, 1)
                for j in range(tiles):
                    tile(n0 + j, off, xhi, xlo, SL * j, 2 * ab, bias is None and j == 0, j == tiles - 1)

            def turn(name, rounds, src):
                for r in range(rounds):
                    g = TBASE[name] + r
                    if g >= 2:
                        pe.wait_ge(turn_lo, g - 1)
                    for k in range(2):
                        for t in range(TT):
                            c0 = (2 * r + k) * P
                            mm = PE_.transpose(ps[:, 4 + g % 2, k * S + t * P:k * S + (t + 1) * P],
                                               src[:, t, c0:c0 + P], ident)
                    mm.then_inc(turned, 1)

            pe.wait_ge(small_in, 64)
            pe.wait_ge(normed, 2)
            turn("h1", 8, N1)
            pe.wait_ge(turn_lo, 8)
            for ab in range(2):
                chunk(TC * ab, 0, TC, ab, 0, xh, xl)
            with pe.Fori(0, 4) as it:
                for ab in range(2):
                    chunk((2 + ab) * TC, it * (2 * TC), TC, ab, it + 1, xh, xl)
            with pe.Fori(0, 4) as it:
                pe.wait_ge(bias_in, it * 16 + 16)
                for ab in range(2):
                    chunk((10 + ab) * TC, it * (2 * TC), TC, ab, it + 5, xh, xl, bias=brow[0:1, ab * CH:(ab + 1) * CH])
            n0 = BASE["kpe"]
            pe.wait_ge(lo_ready, n0 + 1)
            pe.wait_ge(acc_free[0], 18)
            for t in range(TT):
                for k in range(KD):
                    H = hi[:, n0 % SPL, k * ROPE:(k + 1) * ROPE]
                    L = lo[:, n0 % SPL, k * ROPE:(k + 1) * ROPE]
                    xs = slice(t * P, (t + 1) * P)
                    acc = ps[:, t, 0:ROPE]
                    PE_.matmul(acc, xh[:, k, xs], H, start=k == 0, stop=False)
                    PE_.matmul(acc, xh[:, k, xs], L, start=False, stop=False)
                    mm = PE_.matmul(acc, xl[:, k, xs], H, start=False, stop=k == KD - 1)
            mm.then_inc(tile_used, 1)
            pe.wait_ge(kpe_out, 2)
            pe.wait_ge(acc_free[0], 18)
            pe.wait_ge(acc_free[1], 18)
            for t in range(TT):
                pe.wait_ge(ln_done, t + 1)
                for g in range(SGU_G):
                    bank = ((4, 5, 6, 7), (0, 1, 2, 3))[t][g // 2]
                    mm = PE_.matmul(ps[:, bank, SGU_W * (g % 2):SGU_W * (g % 2) + SGU_W], wsp[:, g],
                                    Z[:, t, D + g * SGU_W:D + (g + 1) * SGU_W], start=True, stop=True)
                    if g % 2:
                        mm.then_inc(mixed, 1)
            pe.wait_ge(normed, 6)
            pe.wait_ge(mixed_out, 8)
            turn("cq", 2, CQ)
            turn("ckv", 2, CKV)
            pe.wait_ge(kpr_ok, 2)
            for t in range(TT):
                mm = PE_.transpose(ps[:, 6, t * P:(t + 1) * P], KPR[:, t], ident)
            mm.then_inc(kpt_ps, 1)

            def scores(h, bank, parts, off=0, banks=2):
                if h >= 2 or not isinstance(off, int):
                    pe.wait_ge(s_max, max(h + 1 - banks, 0) + off)
                for q, (c0, w) in enumerate(((0, P), (P, S))):
                    for i, (l, r) in enumerate(parts):
                        mm = PE_.matmul(ps[:, bank, c0:c0 + w], l[:, q * P:(q + 1) * P], r[:, 0:w],
                                        start=i == 0, stop=i == len(parts) - 1)
                mm.then_inc(s_ready, 1)

            def probsT(h, src, bank, off=0):
                pe.wait_ge(p_ready, 2 * h + 2 + off * 2)
                if h >= 2 or not isinstance(off, int):
                    pe.wait_ge(pt_ok, max(h - 1, 0) + off)
                for j in range(3):
                    mm = PE_.transpose(ps[:, bank, j * P:(j + 1) * P], src[:, h % 2, j * P:(j + 1) * P], ident)
                mm.then_inc(pt_ps, 1)

            def values(h, src, bank, v, off=0, banks=2):
                pe.wait_ge(pt_ok, h + 1 + off)
                if h >= 2 or not isinstance(off, int):
                    pe.wait_ge(o_out, 2 * max(h + 1 - banks, 0) + off * 2)
                b = h % 2
                PE_.matmul(ps[:, bank, 0:P], src[:, b, 0:P], v(0), start=True, stop=True)
                PE_.matmul(ps[:, bank, P:S], src[:, b, P:2 * P], v(0), start=True, stop=False)
                PE_.matmul(ps[:, bank, P:S], src[:, b, 2 * P:3 * P], v(1), start=False, stop=True
                           ).then_inc(o_ready, 1)

            pe.wait_ge(turn_lo, TBASE["merged"])
            pe.wait_ge(mixed_out, 16)
            pe.wait_ge(kpt_ok, 1)
            with pe.Fori(0, 4) as it:
                n0 = BASE["mla"]
                for j, (l_h, l_l, w) in enumerate(((cqh, cql, CH), (cqh, cql, GROUP * ROPE),
                                                   (ckh, ckl, CH), (ckh, ckl, CH))):
                    if j == 0:
                        pe.wait_ge(o_out, it * 8)
                    for i in range(TL):
                        tile(n0 + TL * j + i, it * (4 * TL), l_h, l_l, SL * i, 2 * j, i == 0, i == TL - 1, w)
                pe.wait_ge(m_evac, it * 8 + 2)
                for h in range(GROUP):
                    for t in range(TT):
                        mm = PE_.transpose(ps[:, h // 2, (h % 2) * S + t * P:(h % 2) * S + (t + 1) * P],
                                           qn[:, t, h * P:(h + 1) * P], ident)
                mm.then_inc(m_tr, 1)
                pe.wait_ge(m_evac, it * 8 + 6)
                for h in range(GROUP):
                    for t in range(TT):
                        mm = PE_.transpose(ps[:, 2 + h // 2, (h % 2) * S + t * P:(h % 2) * S + (t + 1) * P],
                                           kn[:, t, h * P:(h + 1) * P], ident)
                mm.then_inc(m_tr, 1)
                pe.wait_ge(m_rope, it * 2 + 2)
                for h in range(GROUP // 2):
                    for t in range(TT):
                        mm = PE_.transpose(ps[:, 4, h * S + t * P:h * S + (t + 1) * P],
                                           qrr[:, t, h * P:(h + 1) * P], ident)
                mm.then_inc(m_tr, 1)
                pe.wait_ge(m_ta, it * 2 + 2)
                pe.wait_ge(m_tv, it + 1)
                pe.wait_ge(m_evac, it * 8 + 8)
                for h in range(GROUP + 2):
                    if h < GROUP:
                        r0 = 64 * (h % 2)
                        scores(h, 5 + h % 2, ((qT[:, h], kT[:, h]),
                                              (qrT[r0:r0 + 64, h // 2], KPT[r0:r0 + 64])), it * 4)
                    if 1 <= h <= GROUP:
                        probsT(h - 1, pr, (4, 7)[(h - 1) % 2], it * 4)
                    if h >= 2:
                        g = h - 2
                        values(g, pT, g % 2, lambda t: vv[:, t, g * VH:(g + 1) * VH], it * 4)
            pe.wait_ge(merged_ok, 2)
            pe.wait_ge(pt_ok, 16)
            turn("merged", 8, GT)
            pe.wait_ge(turn_lo, TBASE["merged"] + 8)
            for pair in range(2):
                for ab in range(2):
                    chunk(BASE["out"] + (2 * pair + ab) * TC, 0, TC, ab, PB["out"] + pair, xh, xl)
            pe.wait_ge(normed, 8)
            turn("h2", 8, N2)
            pe.wait_ge(turn_lo, TBASE["h2"] + 8)
            for pair in range(2):
                for ab in range(2):
                    chunk(BASE["pq"] + (2 * pair + ab) * TC, 0, TC, ab, PB["pq"] + pair, xh, xl)
            pe.wait_ge(acc_free[0], 2 * (PB["pq"] + 2))
            pe.wait_ge(acc_free[1], 2 * (PB["pq"] + 2))
            for g in range(8):
                if g >= 2:
                    pe.wait_ge(qt_ok, g - 1)
                for k in range(2):
                    for t in range(TT):
                        c0 = (2 * g + k) * P
                        mm = PE_.transpose(ps[:, 4 + g % 2, k * S + t * P:k * S + (t + 1) * P], Q[:, t, c0:c0 + P],
                                           ident)
                mm.then_inc(qt_ps, 1)
            pe.wait_ge(keys_in, 16)
            pe.wait_ge(qt_ok, 8)
            for g in range(8):
                if g >= 4:
                    pe.wait_ge(sub_ok, g - 3)
                for j in range(4):
                    hp, t = 2 * g + j // 2, j % 2
                    mm = PE_.matmul(ps[:, 4 + g % 4, j * P:(j + 1) * P], QT[:, hp, t * P:(t + 1) * P], keys[:, hp],
                                    start=True, stop=True)
                mm.then_inc(sub_ps, 1)
            n0 = BASE["peer"]

            def u_block(n, off=0, bank=0):
                for j in range(TC):
                    tile(n + j, off, xh, xl, SL * j, bank, j == 0, j == TC - 1)

            for b in range(CHOICE):
                if b >= 2:
                    pe.wait_ge(a_ok, b * 2 - 2)
                u_block(n0 + b * TC, 0, 2 * (b % 2))
            pe.wait_ge(sel_ok, 1)
            pe.wait_ge(sub_ok, 8)
            for i in range(3):
                for t in range(TT):
                    mm = PE_.transpose(ps[:, 4 + i, t * P:(t + 1) * P], sel[:, i, t], ident)
            mm.then_inc(selT_ps, 1)
            pe.wait_ge(selT_ok, 3)
            with pe.Fori(0, 2) as it:
                for e in range(2):
                    for g in range(GQ // GT4):
                        b = g % 2
                        pe.wait_ge(g_out[b], it * 16 + (8 * e + g // 2))
                        pe.wait_ge(oh_ready[b], it * 80 + 5 * (8 * e + g // 2 + 1))
                        for k in range(GT4):
                            mm = PE_.matmul(ps[:, 4 + b, k * P:(k + 1) * P], oh1[:, b, k], oh2[:, b, k],
                                            start=True, stop=True)
                        mm.then_inc(g_ps[b], 1)
                        if b:
                            if g == 1:
                                pe.wait_ge(a_ok, it * 4 + 2 * (CHOICE + e))
                            j = g // 2
                            tile(n0 + (CHOICE + e) * TC + j, it * (2 * TC), xh, xl, SL * j, 0, j == 0, j == TC - 1)

            n0 = BASE["peer"] + AHEAD * TC

            def mod_sum(parts, bank):
                for k in range(KD):
                    mm = PE_.matmul(ps[:, bank, k:k + 1], parts[:, k * P:(k + 1) * P], ones[:, 0:1],
                                    start=True, stop=True)
                mm.then_inc(mod_ps, 1)

            def a_turn(v, q, loads):
                pe.wait_ge(a_in[q], loads)
                if not isinstance(v, int) or v:
                    pe.wait_ge(gated, v * 2)
                for k in range(JB):
                    for t in range(TT):
                        mm = PE_.transpose(ps[:, 2 + k // 2, (k % 2) * S + t * P:(k % 2) * S + (t + 1) * P],
                                           Ain[:, q, t, k * P:(k + 1) * P], ident)
                mm.then_inc(a_T, 1)

            def v_block(v, q, n, off=0, first=False):
                pe.wait_ge(pl_ok, v + 1)
                for c in range(4):
                    pe.wait_ge(v_out, v * 8 + max(2 * c - 2, 0 if first else -2))
                    for j in range(TL):
                        tile(n + TL * c + j, off, Ph[:, q], Pl[:, q], SL * j, 4 + 2 * (c % 2), j == 0, j == TL - 1)

            for b in range(CHOICE + GATES, AHEAD):
                pe.wait_ge(a_ok, 2 * b)
                u_block(n0 - (AHEAD - b) * TC)
            for b in range(2):
                pe.wait_ge(g_out[b], 32)
            a_turn(0, 0, 16)
            with pe.Fori(0, MAIN // 4) as rr:
                pe.wait_ge(mod_col, rr)
                for i in range(4):
                    n, off, v = n0 + 16 * i, rr * 64, rr * 4 + i
                    pe.wait_ge(a_ok, rr * 8 + 2 * (AHEAD + i))
                    u_block(n, off)
                    a_turn(v + 1, (i + 1) % 2, rr * 32 + 16 * ((i + 1) // 2 + 1))
                    v_block(v, i % 2, n + 8, off, first=i == 0)
                pe.wait_ge(mod_used, rr * KD + KD)
                pe.wait_ge(a_ok, rr * 8 + 2 * (AHEAD + 4))
                mod_sum(macc, 0)
            n0 += 16 * MAIN
            with pe.Fori(0, AHEAD // 2 - 1) as it:
                for e in range(2):
                    v = it * 2 + (MAIN + e)
                    a_turn(v + 1, 1 - e, it * 16 + 16 * ((MAIN + e + 1) // 2 + 1))
                    v_block(v, e, n0 + 8 * e, it * 16)
            a_turn(NBLK - 1, 1, 16 * (NBLK // 2))
            v_block(NBLK - 2, 0, n0 + 8 * AHEAD - 16)
            v_block(NBLK - 1, 1, n0 + 8 * AHEAD - 8)
            pe.wait_ge(mod_col, 4)
            pe.wait_ge(mod_used, 5 * KD)
            mod_sum(macc, 0)

            def spread_vector(dg, n):
                pe.wait_ge(dg_ok, n * KD)
                for k in range(KD):
                    mm = PE_.matmul(ps[:, 4 + k // 4, (k % 4) * P:(k % 4 + 1) * P], ones[:], dg[:, k],
                                    start=True, stop=True)
                    if k % 4 == 3:
                        mm.then_inc(spread, 1)

            pe.wait_ge(v_out, 8 * NBLK)
            pe.wait_ge(normed, 12)
            turn("h3", 8, N3)
            pe.wait_ge(turn_lo, TBASE["h3"] + 8)
            with pe.Fori(0, 4) as it:
                for ab in range(2):
                    chunk(BASE["in2"] + ab * TC, it * (2 * TC), TC, ab, it + PB["in2"], xh, xl)
            pe.wait_ge(mod2_used, KD)
            for k in range(KD):
                mm = PE_.matmul(ps[:, 4, k:k + 1], macc2[:, k * P:(k + 1) * P], ones[:, 0:1], start=True, stop=True)
            mm.then_inc(mod2_ps, 1)
            pe.wait_ge(mod_col, 6)
            with pe.Fori(0, 4) as it:
                for ab in range(2):
                    h, n = 16 + ab, BASE["in2"] + (8 + ab) * TC

                    def gates(j):
                        for i in range(j, j + 2):
                            tile(n + i, it * (2 * TC), xh, xl, SL * i, 2 * ab, i == 0, i == TC - 1)

                    pe.wait_ge(acc_free[ab], it * 2 + 2 * (PB["in2"] + 4))
                    gates(0)
                    pe.wait_ge(qk_rope, it * 2 + (ab + 1))
                    pe.wait_ge(qk_out, it * 2 + ab)
                    for a in range(2):
                        for t in range(TT):
                            mm = PE_.transpose(ps[:, 7, a * S + t * P:a * S + (t + 1) * P], rqk[:, t, a], ident)
                    mm.then_inc(qk_tr, 1)
                    gates(2)
                    pe.wait_ge(qk_out, it * 2 + (ab + 1))
                    scores(h, 4, ((qkT[:, 0], qkT[:, 1]),), it * 2, banks=1)
                    gates(4)
                    probsT(h, pr2, 5, it * 2)
                    gates(6)
                    values(h, pT2, 6, lambda t: QKVU[:, t, bass.ds(it * (2 * AD) + (2 * AW + ab * AD), AD)], it * 2,
                           banks=1)
            pe.wait_ge(acc_free[0], 2 * (PB["in2"] + 8))
            pe.wait_ge(acc_free[1], 2 * (PB["in2"] + 8))
            pe.wait_ge(pt_ok, 24)
            for g in range(4):
                if g >= 2:
                    pe.wait_ge(ut_ok, g - 1)
                for k in range(2):
                    for t in range(TT):
                        c0 = 3 * AW + (2 * g + k) * P
                        mm = PE_.transpose(ps[:, 4 + g % 2, k * S + t * P:k * S + (t + 1) * P],
                                           QKVU[:, t, c0:c0 + P], ident)
                mm.then_inc(ut_ps, 1)
            pe.wait_ge(ut_ok, 4)
            def b_turn(it):
                pe.wait_ge(bm_ok, it * 4 + 4)
                pe.wait_ge(bl_ok, it * 2)
                for i in range(2):
                    for k in range(SB):
                        mm = PE_.transpose(ps[:, 6 + i, k * P:(k + 1) * P], bM[:, i, k], ident)
                    mm.then_inc(bl_ps, 1)

            def b_inputs(it, e):
                pe.wait_ge(bl_ok, it * 2 + 2)
                q = it * 2 + e
                if not isinstance(q, int) or q >= 2:
                    pe.wait_ge(rot_ok, q * 2 - 2)
                u = uT[:, it] if isinstance(it, int) else uT[:, bass.ds(it, 1)].rearrange("p a t -> p (a t)")
                for i in range(2):
                    for k in range(2):
                        mm = PE_.matmul(ps[:, 2 * e + i, k * S:k * S + S], bL[:, i, 2 * e + k], u,
                                        start=True, stop=True)
                mm.then_inc(bu_ps, 1)

            def outputs(it, e):
                pe.wait_ge(fw_ok, it * 4 + (2 * e + 2))
                if e == 0:
                    pe.wait_ge(cm_ok, it * 4 + 4)
                    pe.wait_ge(y_sum, it)
                parts = ((0, fw[:, e, 0]), (0, fw[:, e, 1]), (1, rz[:, e, 0]), (1, rz[:, e, 1]))
                for n, (i, x) in enumerate(parts):
                    for k in range(2):
                        mm = PE_.matmul(ps[:, 4, 0:S], cM[:, i, 2 * e + k], x[:, k], start=e + n + k == 0,
                                        stop=e == 1 and n == 3 and k == 1)
                mm.then_inc(y_ps, 1)

            def round_(it):
                b_inputs(it, 1)
                b_turn(it + 1)
                outputs(it, 0)
                b_inputs(it + 1, 0)
                outputs(it, 1)

            b_turn(0)
            b_inputs(0, 0)
            round_(0)
            with pe.Fori(1, 7) as it:
                round_(it)
            b_inputs(7, 1)
            outputs(7, 0)
            outputs(7, 1)
            spread_vector(dg1, 1)
            pe.wait_ge(yspl_l, 1)
            pe.wait_ge(bglu_in, 16)
            for ab in range(2):
                chunk(BASE["glu"] + ab * TA, 0, TA, ab, PB["glu"], yh, yl, bias=bglu[0:1, ab * CH:(ab + 1) * CH])
            pe.wait_ge(y_sum, 8)
            pe.wait_ge(acc_free[1], 2 * (PB["glu"] + 1))
            pe.wait_ge(spread_out, 4)
            for g in range(4):
                pe.wait_ge(acc_free[g // 2], 2 * (PB["glu"] + 1))
                if g >= 2:
                    pe.wait_ge(y32_ok, g - 1)
                for k in range(2):
                    for t in range(TT):
                        c0 = (2 * g + k) * P
                        mm = PE_.transpose(ps[:, 4 + g % 2, k * S + t * P:k * S + (t + 1) * P], SG[:, t, c0:c0 + P],
                                           ident)
                mm.then_inc(sg_T, 1)
            pe.wait_ge(y32_ok, 4)
            turn("ya", 4, YA)
            pe.wait_ge(turn_lo, TBASE["ya"] + 4)
            for pair in range(2):
                for ab in range(2):
                    chunk(BASE["abr"] + (2 * pair + ab) * TA, 0, TA, ab, PB["abr"] + pair, yah, yal)
            pe.wait_ge(yg_l, 4)
            for pair in range(2):
                for ab in range(2):
                    chunk(BASE["sbr"] + (2 * pair + ab) * TA, 0, TA, ab, PB["sbr"] + pair, yh, yl)
            pe.wait_ge(br_out, 8)
            turn("merged2", 8, M2)
            pe.wait_ge(turn_lo, TBASE["merged2"] + 8)
            for pair in range(2):
                for ab in range(2):
                    chunk(BASE["out2"] + (2 * pair + ab) * TC, 0, TC, ab, PB["out2"] + pair, xh, xl)
            pe.wait_ge(normed, 14)
            turn("h4", 8, N4)
            pe.wait_ge(turn_lo, TBASE["h4"] + 8)
            spread_vector(dg2, 2)
            pe.wait_ge(spread_out, 8)
            n0 = BASE["ffn"]

            def up_block(b, n, off=0):
                for half in range(2):
                    if not isinstance(b, int) or b:
                        pe.wait_ge(up_out, b * 4 + (2 * half - 2))
                    for j in range(TC):
                        tile(n + TC * half + j, off, xh, xl, SL * j, 2 * half, j == 0, j == TC - 1)

            def up_turn(b):
                for half in range(2):
                    pe.wait_ge(up_out, b * 4 + (2 * half + 2))
                    if not isinstance(b, int) or b:
                        pe.wait_ge(dn_out, b * 8 - (2, 0)[half])
                    for f in range(4):
                        for t in range(TT):
                            mm = PE_.transpose(ps[:, 4 + 2 * half + f // 2, (f % 2) * S + t * P:(f % 2) * S + (t + 1) * P],
                                               UP[:, half, t, f * P:(f + 1) * P], ident)
                    mm.then_inc(up_T, 1)

            def down_block(b, n, off=0):
                pe.wait_ge(fl_ok, b + 1)
                for c in range(4):
                    if c >= 2:
                        pe.wait_ge(dn_out, b * 8 + (2 * c - 2))
                    for j in range(TL):
                        tile(n + TL * c + j, off, Fh, Fl, SL * j, 4 + 2 * (c % 2), j == 0, j == TL - 1)

            pe.wait_ge(acc_free[0], 2 * (PB["out2"] + 2))
            pe.wait_ge(acc_free[1], 2 * (PB["out2"] + 2))
            up_block(0, n0)
            up_turn(0)
            with pe.Fori(1, FB) as b:
                up_block(b, n0 + 16, b * 24 - 24)
                down_block(b - 1, n0 + 32, b * 24 - 24)
                up_turn(b)
            down_block(FB - 1, n0 + 24 * FB - 8)


def constants():
    c = np.zeros((P, NCONST), np.float32)

    def put(name, a):
        c[:, KOFF[name]:KOFF[name] + a.shape[-1]] = a

    put("ident", np.eye(P, dtype=np.float32))
    put("ones", np.ones((P, P), np.float32))
    causal = np.where(np.arange(P)[:, None] >= np.arange(P)[None], 0.0, NEG).astype(np.float32)
    put("mask", np.concatenate([causal, np.zeros((P, P), np.float32), causal], 1))
    put("triu", np.triu(np.ones((P, P), np.float32)))
    put("halfpi", np.full((P, 1), math.pi / 2, np.float32))
    put("magic", np.full((P, 1), MAGIC, np.float32))
    put("iota", np.arange(2 * P, dtype=np.float32)[None].repeat(P, 0))
    f = np.float32(10000.0) ** (-np.arange(0, 64, 2, dtype=np.float32) / np.float32(64))
    put("freq", f.astype(np.float32)[None].repeat(P, 0))
    f = np.float32(10000.0) ** (-np.arange(64, dtype=np.float32) / np.float32(64))
    put("freq2", f.astype(np.float32)[None].repeat(P, 0))
    return c


MODS = [0, 1, 3, 4, 2, 5]


def weight_tiles(w):
    k, n = w.shape
    return np.ascontiguousarray(
        w.reshape(k // (SL * P), SL, P, n // CH, CH).transpose(3, 0, 2, 1, 4).reshape(-1, P, TW))


def columns(v):
    return v.reshape(-1, P).T


def prepare(i):
    g = {k: np.asarray(v) for k, v in i.items()}
    a = {}
    a["const"] = constants()
    a["x"] = np.ascontiguousarray(g["x"][0].reshape(TT, P, D).transpose(1, 0, 2))
    a["pos"] = np.ascontiguousarray(np.concatenate([g["positions"].reshape(TT, P).T,
                                                    g["positions_2"].reshape(TT, P).T], 1))
    w = g["w_in"][0]
    o = 2 * LORA
    order = np.concatenate([w[:, 0:o], w[:, o + ROPE:]], 1)
    a["w_in"] = weight_tiles(order)
    a["kpe"] = np.ascontiguousarray(w[:, o:o + ROPE].reshape(KD, P, ROPE).transpose(1, 0, 2).reshape(P, KD * ROPE))
    a["b_gate"] = np.ascontiguousarray(g["b_gate"][0].reshape(4, 2 * CH))
    uq, ukv = g["w_uq"][0], g["w_ukv"][0]
    parts = []
    for r in range(HEADS // GROUP):
        hs = slice(r * GROUP, (r + 1) * GROUP)
        for m in (uq[:, hs, :NOPE], ukv[:, hs, :NOPE], ukv[:, hs, NOPE:]):
            parts.append(weight_tiles(m.reshape(LORA, CH)))
    a["mla"] = np.concatenate(parts)
    a["mla_r"] = np.ascontiguousarray(
        uq[:, :, NOPE:].reshape(TL, SL, P, HEADS // GROUP, GROUP * ROPE).transpose(3, 0, 2, 1, 4)
        .reshape(HEADS // GROUP * TL, P, TW // 2))
    a["w_spatial"] = np.ascontiguousarray(g["w_spatial"][0].transpose(2, 0, 1))
    a["sgu_ln_g"], a["sgu_ln_b"] = g["sgu_ln_g"][0], g["sgu_ln_b"][0]
    a["out"] = weight_tiles(g["w_out"][0])
    a["pq"] = weight_tiles(g["w_peer_q"][0].reshape(D, D))
    a["peer_keys"] = np.ascontiguousarray(g["peer_keys"][0].reshape(16, NKEY, P).transpose(2, 0, 1))
    u = g["peer_u"][0].reshape(P, NBLK, JB, KD, P)
    a["peer_u"] = np.ascontiguousarray(u.transpose(1, 3, 4, 2, 0).reshape(NBLK, TC, SL, P, EB)
                                       .transpose(0, 1, 3, 2, 4).reshape(NBLK * TC, P, TW))
    v = g["peer_v"][0].reshape(P, NBLK, TL, SL, 4, CH)
    a["peer_v"] = np.ascontiguousarray(v.transpose(1, 4, 2, 0, 3, 5).reshape(NBLK * 4 * TL, P, TW))
    a["w_mod"] = np.ascontiguousarray(g["w_mod_2"][0].reshape(KD, P, 6, D).transpose(2, 0, 1, 3)[MODS]
                                      .reshape(6 * KD, P, D))
    a["g_final"] = g["g_final"]
    a["q_norm_g"], a["k_norm_g"] = g["q_norm_g_2"][0], g["k_norm_g_2"][0]
    a["in2"] = weight_tiles(g["w_in_2"][0])
    a["glu"] = weight_tiles(g["w_glu_2"][0])
    a["b_glu"] = np.ascontiguousarray(g["b_glu_2"][0].reshape(1, AW))
    a["abr"] = weight_tiles(g["w_attn_br_2"][0])
    a["sbr"] = weight_tiles(g["w_ssm_br_2"][0])
    a["out2"] = weight_tiles(g["w_out_2"][0])
    wu = weight_tiles(g["w_up_2"][0]).reshape(2, FB, TC, P, TW)
    a["w_up"] = np.ascontiguousarray(wu.transpose(1, 0, 2, 3, 4).reshape(FB * 2 * TC, P, TW))
    wd = g["w_down_2"][0].reshape(FB, TL, SL, P, 4, CH)
    a["w_down"] = np.ascontiguousarray(wd.transpose(0, 4, 1, 3, 2, 5).reshape(FB * 4 * TL, P, TW))

    def states(v):
        return v.reshape(STT, P, *v.shape[2:]).swapaxes(0, 1)

    for n in ("re", "im"):
        a[f"ssm_b_{n}"] = np.ascontiguousarray(states(g[f"ssm_b_{n}_2"][0]))
        a[f"ssm_c_{n}"] = np.ascontiguousarray(states(g[f"ssm_c_{n}_2"][0].swapaxes(1, 2)))
    cols = np.zeros((P, NCOLS), np.float32)

    def put(name, m):
        cols[:, COFF[name]:COFF[name] + m.shape[1]] = m

    put("bmod", columns(g["b_mod_2"][0].reshape(6, D)[MODS].reshape(-1)))
    put("g1", columns(g["g_norm1"][0]))
    put("gqa", columns(g["g_q_a"][0]))
    put("gkva", columns(g["g_kv_a"][0]))
    put("g2", columns(g["g_norm2"][0]))
    put("g3", columns(g["norm1_g_2"][0]))
    put("g4", columns(g["norm2_g_2"][0]))
    put("bsp", g["b_spatial"][0].T)
    put("c", columns(g["c_2"][0]))
    put("dskip", columns(g["ssm_d_2"][0]))
    put("lre", states(g["ssm_lambda_re_2"][0]))
    put("lim", states(g["ssm_lambda_im_2"][0]))
    put("ldt", states(np.broadcast_to(g["ssm_log_dt_2"][0][:, None], (NG, NST))))
    taps = np.concatenate([g["conv_w_2"][0], g["conv_b_2"]], 0)
    taps = taps.reshape(4, 2, FB, 4, P).transpose(4, 2, 1, 3, 0)
    put("conv", taps.reshape(P, FB * 32))
    a["cols"] = cols
    return a


def kernel(**inputs):
    import numpy as _np
    import concourse.bacc as _bacc
    from concourse import mybir as _mybir
    from concourse.bass_utils import run_bass_kernel_spmd as _run

    arrays = prepare(inputs)
    nc = _bacc.Bacc("TRN2", target_bir_lowering=False, num_devices=1)
    aps = {}
    for name, v in arrays.items():
        aps[name] = nc.dram_tensor(f"in_{name}", v.shape, _mybir.dt.from_np(v.dtype), kind="ExternalInput").ap()
    out = nc.dram_tensor("out_0", (S, D), F32, kind="ExternalOutput").ap()
    build(nc, aps, out)
    r = _run(nc, [{f"in_{k}": v for k, v in arrays.items()}], core_ids=[0])
    return _np.asarray(r.results[0]["out_0"]).reshape(1, S, D)
```

```python
import math
from contextlib import ExitStack

import numpy as np

import concourse.bass as bass
from concourse import mybir

F32 = mybir.dt.float32
F32R = mybir.dt.float32r
I32 = mybir.dt.int32
U32 = mybir.dt.uint32
ALU = mybir.AluOpType
ACT = mybir.ActivationFunctionType
AX = mybir.AxisListType.X

P = 128
S, TT = 256, 2
D, KD = 2048, 16
CH = 512
SL = 2
TW = SL * CH
TC, TA, TL = KD // SL, 8 // SL, 4 // SL
RAW, SPL = 8, 4
EPS = 1e-6
HEADS, NOPE, ROPE, VH = 16, 128, 64, 128
LORA, KL = 512, 4
GROUP = 4
SGU_G, SGU_W = 8, 256
PH, NKEY, TOPK = 8, 128, 16
HK = PH * TOPK
NEXP = NKEY * NKEY
EB = CH
NBLK = NEXP // EB
JB = EB // NKEY
AHEAD, CHOICE = 16, 11
GATES = 4
MAIN = NBLK - AHEAD
GT4, GQ = 4, 64
AH, AD, AW = 8, 128, 1024
NG, GH, NST = 64, 16, 64
STT = NG * NST // P
SB = 4
FFN = 5632
FB = FFN // CH
NEG = -1e30

STREAM = [("w_in", 10 * TC), ("kpe", 1), ("gate", 8 * TC), ("mla", 4 * 4 * TL), ("out", 4 * TC), ("pq", 4 * TC),
          ("peer", (TC + 4 * TL) * NBLK), ("in2", 16 * TC), ("glu", 2 * TA), ("abr", 4 * TA),
          ("sbr", 4 * TA), ("out2", 4 * TC), ("ffn", (2 * TC + 4 * TL) * FB)]
BASE, _n = {}, 0
for _name, _count in STREAM:
    BASE[_name] = _n
    _n += _count
TOTAL = _n

TURNS = [("h1", 8), ("cq", 2), ("ckv", 2), ("merged", 8), ("h2", 8), ("h3", 8), ("ya", 4),
         ("merged2", 8), ("h4", 8)]
TBASE, _n = {}, 0
for _name, _count in TURNS:
    TBASE[_name] = _n
    _n += _count

COLS = [("bmod", 96), ("g1", 16), ("gqa", 4), ("gkva", 4), ("g2", 16), ("g3", 16), ("g4", 16), ("bsp", 8),
        ("c", 16), ("dskip", 8), ("lre", 32), ("lim", 32), ("ldt", 32), ("conv", FB * 32)]
COFF, _n = {}, 0
for _name, _count in COLS:
    COFF[_name] = _n
    _n += _count
NCOLS = _n

CONST = [("ident", 128), ("ones", 128), ("mask", 384), ("triu", 128), ("iota", 256),
         ("freq", 32), ("freq2", 64), ("halfpi", 1), ("magic", 1)]
KOFF, _n = {}, 0
for _name, _count in CONST:
    KOFF[_name] = _n
    _n += _count
NCONST = _n

TWO_PI = 2.0 * math.pi
INV_2PI = 1.0 / TWO_PI
C1 = 6.28125
C2 = float(np.float32(0.0019350051879882812))
C3 = TWO_PI - C1 - C2
MAGIC = 12582912.0
PI_IN = 3.1415925
TURN = 6.283185


MOD_SIX = (((0, 3), (1, 3), (2, 2)), ((3, 3), (4, 3), (5, 2)))
MOD_FOUR = (((0, 4), (1, 4)), ((2, 4), (3, 4)))
MOD_NONE = (((None, 4), (None, 4)), ((None, 4), (None, 4)))


class Steps:

    def __init__(self, eng, sem):
        self.eng, self.sem, self.base, self.k = eng, sem, 0, 0

    def step(self, ins):
        ins.then_inc(self.sem, 1)
        self.k += 1

    def wait(self):
        self.eng.wait_ge(self.sem, self.base + self.k)

    def link(self, ins):
        self.step(ins)
        self.wait()

    def enter(self, per, it):
        self.outer = self.base + self.k
        self.base, self.k = per * it + self.outer, 0

    def leave(self, per, count):
        assert self.k == per, (self.k, per)
        self.base, self.k = self.outer + per * count, 0


def build(nc, A, out):
    V, SC, PE_, GP = nc.vector, nc.scalar, nc.tensor, nc.gpsimd
    ctx = ExitStack()
    with ctx:
        base0 = 16512

        def at(name, shape, kb, dt=F32):
            return nc.alloc_sbuf_tensor_at(name, shape, dt, offset=base0 + int(kb * 1024)).ap()

        def sem(name):
            return ctx.enter_context(nc.semaphore(name))

        raw = at("raw", [P, RAW, TW], 0)
        hi = at("hi", [P, SPL, TW], 32, F32R)
        lo = at("lo", [P, SPL, TW], 48, F32R)
        xh = at("xh", [P, KD, S], 64, F32R)
        xl = at("xl", [P, KD, S], 80, F32R)
        X = at("X", [P, TT, D], 96)
        const = at("const", [P, NCONST], 112)
        cols = at("cols", [P, NCOLS], 112 + 4.5)
        stat = at("stat", [P, 256], 112 + 4.5 + 2.75)
        trig = at("trig", [P, 2, 192], 112 + 4.5 + 3.75)
        W0 = 112 + 4.5 + 3.75 + 1.5

        def K(name):
            return const[:, KOFF[name]:KOFF[name] + dict(CONST)[name]]

        def C(name, i, n=1):
            return cols[:, COFF[name] + i:COFF[name] + i + n]

        ident, ones, iota = K("ident"), K("ones"), K("iota")

        Z = at("Z", [P, TT, 2 * D], W0)
        GT = at("GT", [P, TT, 2 * D], W0 + 32)
        CQ = at("CQ", [P, TT, LORA], W0 + 64)
        CKV = at("CKV", [P, TT, LORA], W0 + 68)
        KPE = at("KPE", [P, TT, ROPE], W0 + 72)
        brow = at("brow", [1, 2 * CH], W0 + 73)
        wsp = at("wsp", [P, SGU_G, P], W0 + 77)
        KPR = at("KPR", [P, TT, P], W0 + 81)
        KPT = at("KPT", [P, S], W0 + 82)
        ktmp = at("ktmp", [P, TT, 64], W0 + 83)
        N1 = at("N1", [P, TT, D], W0)
        ang = at("ang", [P, 6, 192], W0 + 16)
        posi = at("posi", [P, 4], W0 + 22, I32)
        posf = at("posf", [P, 4], W0 + 22.25)
        junk = at("junk", [P, D], W0 + 24)
        lng = at("lng", [P, D], W0 + 40)
        lnb = at("lnb", [P, D], W0 + 56)
        cqh = at("cqh", [P, KL, S], 64, F32R)
        cql = at("cql", [P, KL, S], 68, F32R)
        ckh = at("ckh", [P, KL, S], 72, F32R)
        ckl = at("ckl", [P, KL, S], 76, F32R)
        junk2 = at("junk2", [P, D], 64)
        qn = at("qn", [P, TT, CH], W0)
        kn = at("kn", [P, TT, CH], W0 + 4)
        vv = at("vv", [P, TT, CH], W0 + 8)
        qr = at("qr", [P, TT, GROUP * ROPE], W0 + 12)
        qrr = at("qrr", [P, TT, GROUP * ROPE], W0 + 14)
        qtmp = at("qtmp", [P, TT, GROUP * 32], W0 + 16)
        qT = at("qT", [P, GROUP, S], W0 + 17)
        kT = at("kT", [P, GROUP, S], W0 + 21)
        qrT = at("qrT", [P, GROUP // 2, S], W0 + 25)
        sc = at("sc", [P, 2, 384], W0 + 73)
        pr = at("pr", [P, 2, 384], W0 + 76)
        pT = at("pT", [P, 2, 384], W0 + 27)
        N2 = at("N2", [P, TT, D], W0)
        Q = at("Q", [P, TT, D], W0)
        QT = at("QT", [P, 16, S], W0 + 16)
        keys = at("keys", [P, 16, NKEY], W0 + 32)
        sub = at("sub", [P, 32, NKEY], W0 + 40)
        sub2 = at("sub2", [P, 32, NKEY], W0 + 56)
        vals = at("vals", [P, 32, TOPK], W0 + 72)
        vidx = at("vidx", [P, 32, TOPK], W0 + 74, U32)
        vidf = at("vidf", [P, 32, TOPK], W0 + 76)
        cand = at("cand", [P, 16, 256], W0 + 56)
        cand2 = at("cand2", [P, 16, 256], W0 + 40)
        tops = at("tops", [P, 16, TOPK], W0 + 78)
        tpos = at("tpos", [P, 16, TOPK], W0 + 79, U32)
        tab = at("tab", [P, 2, 16 * TOPK], W0 + 80, U32)
        tabf = at("tabf", [P, 2, 16 * TOPK], W0 + 82)
        eq = at("eq", [P, 8, TOPK, TOPK], W0 + 40)
        sel = at("sel", [P, 3, TT, HK], W0 + 48)
        selT = at("selT", [P, 3, S], W0 + 81)
        oh1 = at("oh1", [P, 2, GT4, P], W0 + 8)
        oh2 = at("oh2", [P, 2, GT4, P], W0 + 12)
        gst = at("gst", [P, 2, NKEY, GQ], W0 + 16)
        Ab = at("Ab", [P, TT, EB], W0)
        Ain = at("Ain", [P, 2, TT, EB], W0 + 4)
        Gb = at("Gb", [P, 2, S // GQ, JB, GQ], W0 + 12)
        P32 = at("P32", [P, 2, JB, S], W0 + 20)
        Ph = at("Ph", [P, 2, JB, S], W0 + 28, F32R)
        Pl = at("Pl", [P, 2, JB, S], W0 + 36, F32R)
        macc = at("macc", [P, D], W0 + 44)
        mraw = at("mraw", [P, 4, D], W0 + 52)
        macc2 = at("macc2", [P, D], W0 + 48)
        mraw2 = at("mraw2", [P, D], W0 + 56)
        gfin = at("gfin", [P, D], W0 + 68)
        N3 = at("N3", [P, TT, D], W0)
        mcol = at("mcol", [P, 6, KD], W0 + 84)
        t3 = at("t3", [P, 2, S], W0 + 16)
        QKVU = at("QKVU", [P, TT, 4 * AW], W0)
        G2 = at("G2", [P, TT, 2 * D], W0 + 32)
        gqk = at("gqk", [P, 2, AD], W0 + 85)
        neghalf = at("neghalf", [P, 32], W0 + 84.5)
        sq2 = at("sq2", [P, TT, 2 * AW], W0 + 32)
        sc2 = at("sc2", [P, 2, 384], W0 + 64)
        pr2 = at("pr2", [P, 2, 384], W0 + 67)
        pT2 = at("pT2", [P, 2, 384], W0 + 70)
        rqk = at("rqk", [P, TT, 2, AD], W0 + 73)
        rt = at("rt", [P, 2, TT * 2 * AD // 2], W0 + 75)
        qkT = at("qkT", [P, 2, S], W0 + 77)
        YA = QKVU[:, :, 0:AW]
        uT = at("uT", [P, 8, S], W0 + 64)
        ssmB = at("ssmB", [P, 2, STT, GH], W0 + 4)
        ssmC = at("ssmC", [P, 2, STT, GH], W0 + 12)
        cB = at("cB", [P, 2, STT, GH], W0 + 8)
        sv = at("sv", [P, 24, STT], W0 + 80)
        bM = at("bM", [P, 2, SB, P], W0 + 20)
        bL = at("bL", [P, 2, SB, P], W0 + 24)
        cM = at("cM", [P, 2, SB, P], W0 + 28)
        px = at("px", [P, 2, S], 64)
        pr_ = at("pr_", [P, 2, S], 66)
        cs = at("cs", [P, 2, 2, 2, S], 68)
        rb = at("rb", [P, 2, 2, S], 76)
        rz = at("rz", [P, 2, 2, 2, S], 80)
        fw = at("fw", [P, 2, 2, 2, S], 88)
        yT = at("yT", [P, 8, S], W0 + 72)
        yh = at("yh", [P, 8, S], 64, F32R)
        yl = at("yl", [P, 8, S], 72, F32R)
        SG = at("SG", [P, TT, AW], W0 + 64)
        bglu = at("bglu", [1, AW], W0 + 12)
        Y32 = at("Y32", [P, 2, S], W0 + 28)
        yah = at("yah", [P, 8, S], 80, F32R)
        yal = at("yal", [P, 8, S], 88, F32R)
        M2 = at("M2", [P, TT, D], W0)
        btmp = at("btmp", [P, 2, CH], W0 + 16)
        g1b = at("g1b", [P, D], W0 + 20)
        dg1 = at("dg1", [P, KD, P], W0 + 72)
        dg2 = at("dg2", [P, KD, P], W0 + 50)
        N4 = at("N4", [P, TT, D], W0 + 32)
        t4 = at("t4", [P, 2, S], W0 + 29)
        Y = at("Y", [P, TT, D], W0)
        g2b = at("g2b", [P, D], W0 + 74)
        UP = at("UP", [P, 2, TT, CH], W0 + 32)
        cv = at("cv", [P, 2, 4, S], W0 + 40)
        ccol = at("ccol", [P, 32], W0 + 48)
        sil = at("sil", [P, 4, S], W0 + 50)
        F32t = at("F32t", [P, 4, S], W0 + 54)
        Fh = at("Fh", [P, 4, S], W0 + 58, F32R)
        Fl = at("Fl", [P, 4, S], W0 + 62, F32R)
        Fh2 = at("Fh2", [P, 4, S], W0 + 66, F32R)
        Fl2 = at("Fl2", [P, 4, S], W0 + 70, F32R)

        ps = ctx.enter_context(nc.psum_tensor("ps", [P, 8, CH], F32)).ap()

        gdram = nc.dram_tensor("gate_scratch", [S // GQ, P, NKEY, GQ], F32, kind="Internal").ap()
        adram = nc.dram_tensor("act_scratch", [NBLK, P, TT * EB], F32, kind="Internal").ap()

        raw_ready = [sem(f"raw_ready{i}") for i in range(RAW)]
        hi_ready = sem("hi_ready")
        lo_ready = sem("lo_ready")
        tile_used = sem("tile_used")
        acc_free = [sem("accA_free"), sem("accB_free")]
        turned = sem("turned")
        turn_hi = sem("turn_hi")
        turn_lo = sem("turn_lo")
        x_in = [sem(f"x_in{t}") for t in range(TT)]
        small_in, pos_in = sem("small_in"), sem("pos_in")
        var_ready = sem("var_ready")
        rstd_ready = sem("rstd_ready")
        sq_ready = sem("sq_ready")
        normed = sem("normed")
        act_step, dve_step = sem("act_step"), sem("dve_step")
        trig_arg, trig_ok = sem("trig_arg"), sem("trig_ok")
        bias_in, bias_used = sem("bias_in"), sem("bias_used")
        kpe_T, kpe_ps, kpe_out = sem("kpe_T"), sem("kpe_ps"), sem("kpe_out")
        ln_in, keys_in = sem("ln_in"), sem("keys_in")
        ln_sum, ln_mu = sem("ln_sum"), sem("ln_mu")
        ln_done, mixed, mixed_out = sem("ln_done"), sem("mixed"), sem("mixed_out")
        sgu_ok = sem("sgu_ok")
        kpr_ok, kpt_ps, kpt_ok = sem("kpr_ok"), sem("kpt_ps"), sem("kpt_ok")
        m_evac, m_rope, m_tr = sem("m_evac"), sem("m_rope"), sem("m_tr")
        m_ta, m_tv = sem("m_ta"), sem("m_tv")
        s_ready, s_max, p_ready = sem("s_ready"), sem("s_max"), sem("p_ready")
        pt_ps, pt_ok, o_ready, o_out = sem("pt_ps"), sem("pt_ok"), sem("o_ready"), sem("o_out")
        merged_ok = sem("merged_ok")
        qt_ps, qt_ok = sem("qt_ps"), sem("qt_ok")
        sub_ps, sub_ok = sem("sub_ps"), sem("sub_ok")
        gate_in, gate_exp = sem("gate_in"), sem("gate_exp")
        sel_ok, selT_ps, selT_ok = sem("sel_ok"), sem("selT_ps"), sem("selT_ok")
        oh_ready, g_ps, g_out = ([sem(f"{n}{b}") for b in range(2)] for n in ("oh_ready", "g_ps", "g_out"))
        g_st = [sem(f"g_st{b}") for b in range(2)]
        g_in, a_in = ([sem(f"{n}{b}") for b in range(2)] for n in ("g_in", "a_in"))
        gated, a_st = sem("gated"), sem("a_st")
        a_ok, a_T, ph_ok, pl_ok = sem("a_ok"), sem("a_T"), sem("ph_ok"), sem("pl_ok")
        v_out = sem("v_out")
        mod_in = [sem(f"mod_in{i}") for i in range(4)]
        mod_used, pow_ok = sem("mod_used"), sem("pow_ok")
        mod2_in, mod2_used, mod2_ps = sem("mod2_in"), sem("mod2_used"), sem("mod2_ps")
        csil, mod_ps = sem("csil"), sem("mod_ps")
        dg_ok, spread, spread_out = sem("dg_ok"), sem("spread"), sem("spread_out")
        gfin_in, mod_col = sem("gfin_in"), sem("mod_col")
        mcol_ok = sem("mcol_ok")
        qk_sq, qk_rope, qk_tr, qk_out = sem("qk_sq"), sem("qk_rope"), sem("qk_tr"), sem("qk_out")
        ut_ps, ut_ok = sem("ut_ps"), sem("ut_ok")
        ssm_in, sv_arg, sv_sin, sv_ok = sem("ssm_in"), sem("sv_arg"), sem("sv_sin"), sem("sv_ok")
        cb_ok, blocks_zero, scan_ok, fw_p = sem("cb_ok"), sem("blocks_zero"), sem("scan_ok"), sem("fw_p")
        pool_step, ssmc_in, gqk_in = sem("pool_step"), sem("ssmc_in"), sem("gqk_in")
        bm_ok, bl_ps, bl_ok, bu_ps = sem("bm_ok"), sem("bl_ps"), sem("bl_ok"), sem("bu_ps")
        ph_x, ph_arg, cs_ok, rot_ok, fw_ok, y_ps, y_ok = (
            sem(n) for n in ("ph_x", "ph_arg", "cs_ok", "rot_ok", "fw_ok", "y_ps", "y_ok"))
        y_sum, cm_ok = sem("y_sum"), sem("cm_ok")
        yspl_h, yspl_l = sem("yspl_h"), sem("yspl_l")
        sg_T, y32_ok, yg_h, yg_l = (sem(n) for n in ("sg_T", "y32_ok", "yg_h", "yg_l"))
        br_out, bglu_in = sem("br_out"), sem("bglu_in")
        up_out, up_T, cv_base, cv_ok, sil_ok, f32_ok, fh_ok, fl_ok, dn_out = (
            sem(n) for n in ("up_out", "up_T", "cv_base", "cv_ok", "sil_ok", "f32_ok", "fh_ok",
                             "fl_ok", "dn_out"))
        cc_ok = sem("cc_ok")
        y_zero = sem("y_zero")
        y_done, o_st = sem("y_done"), sem("o_st")

        PAIRS = [("w_in", 9), ("out", 2), ("pq", 2), ("in2", 8), ("glu", 1), ("abr", 2),
                 ("sbr", 2), ("out2", 2)]
        PB, n = {}, 0
        for name, count in PAIRS:
            PB[name] = n
            n += count

        def heads_rows(ap, h, w):
            return ap.rearrange("p (h w) -> p h w", h=h, w=w)

        block = ctx.enter_context(nc.Block())

        @block.sync
        def _(sp):
            def load(src, n0, off=0, w=TW):
                if n0 >= RAW:
                    sp.wait_ge(lo_ready, n0 - RAW + 1 + off)
                sp.dma_start(raw[:, n0 % RAW, 0:w], src).then_inc(raw_ready[n0 % RAW], 16)

            def tile(name, i):
                if isinstance(i, int):
                    return A[name][i]
                return A[name][bass.ds(i, 1)].rearrange("a p n -> p (a n)")

            def section(name, count):
                n0 = BASE[name]
                with sp.Fori(0, count // RAW) as it:
                    for j in range(RAW):
                        load(tile(name, it * RAW + j), n0 + j, it * RAW)

            for t in range(TT):
                sp.dma_start(X[:, t], A["x"][:, t]).then_inc(x_in[t], 16)
            for j in range(RAW):
                load(tile("w_in", j), j)
            with sp.Fori(1, 10) as it:
                for j in range(TC):
                    load(tile("w_in", it * TC + j), j + TC, it * TC - TC)
            load(A["kpe"], BASE["kpe"], w=KD * ROPE)
            with sp.Fori(0, 4) as it:
                sp.wait_ge(bias_used, it)
                sp.dma_start(brow[:], A["b_gate"][bass.ds(it, 1), :]).then_inc(bias_in, 16)
                for j in range(2 * TC):
                    load(tile("w_in", it * (2 * TC) + (10 * TC + j)), BASE["gate"] + j, it * (2 * TC))
            with sp.Fori(0, 4) as it:
                for j in range(4 * TL):
                    n0 = BASE["mla"] + j
                    if j // TL == 1:
                        load(A["mla_r"][bass.ds(it * TL + j % TL, 1)].rearrange("a p n -> p (a n)"), n0,
                             it * (4 * TL), TW // 2)
                    else:
                        load(tile("mla", it * (3 * TL) + (j if j < TL else j - TL)), n0, it * (4 * TL))
            section("out", 4 * TC)
            section("pq", 4 * TC)
            n0 = BASE["peer"]

            def up(b, n, off=0):
                for j in range(TC):
                    load(tile("peer_u", b * TC + j), n + j, off)

            def down(b, n, off=0):
                for j in range(4 * TL):
                    load(tile("peer_v", b * (4 * TL) + j), n + j, off)

            with sp.Fori(0, AHEAD) as b:
                up(b, n0, b * TC)
            with sp.Fori(0, MAIN) as b:
                up(b + AHEAD, n0 + AHEAD * TC, b * 16)
                down(b, n0 + AHEAD * TC + 8, b * 16)
            with sp.Fori(0, AHEAD) as b:
                down(b + MAIN, n0 + AHEAD * TC + 16 * MAIN, b * 8)
            section("in2", 16 * TC)
            section("glu", 2 * TA)
            section("abr", 4 * TA)
            section("sbr", 4 * TA)
            section("out2", 4 * TC)
            n0 = BASE["ffn"]

            def ups(b, n, off=0):
                for j in range(2 * TC):
                    load(tile("w_up", b * (2 * TC) + j), n + j, off)

            def downs(b, n, off=0):
                for j in range(4 * TL):
                    load(tile("w_down", b * (4 * TL) + j), n + j, off)

            ups(0, n0)
            with sp.Fori(1, FB) as b:
                ups(b, n0 + 16, b * 24 - 24)
                downs(b - 1, n0 + 32, b * 24 - 24)
            downs(FB - 1, n0 + 24 * FB - 8)

        @block.gpsimd
        def _(pool):
            pool.dma_start(const[:], A["const"]).then_inc(small_in, 16)
            pool.dma_start(cols[:], A["cols"]).then_inc(small_in, 16)
            pool.dma_start(posi[:], A["pos"]).then_inc(pos_in, 16)
            pool.dma_start(wsp[:], A["w_spatial"]).then_inc(pos_in, 16)
            pool.dma_start(lng[:], A["sgu_ln_g"].partition_broadcast(P)).then_inc(ln_in, 16)
            pool.dma_start(lnb[:], A["sgu_ln_b"].partition_broadcast(P)).then_inc(ln_in, 16)
            GP.memset(neghalf[:], -0.5).then_inc(pow_ok, 1)
            count = [0]
            pool.wait_ge(pow_ok, 1)

            def inverse_root(off, n):
                count[0] += 1
                pool.wait_ge(var_ready, count[0])
                GP.tensor_tensor(stat[:, off + n:off + 2 * n], stat[:, off:off + n], neghalf[:, 0:n],
                                 ALU.pow).then_inc(rstd_ready, 1)

            inverse_root(0, 2)
            inverse_root(0, 2)
            inverse_root(0, 4)
            pool.wait_ge(turn_lo, TBASE["merged"] + 8)
            pool.dma_start(keys[:], A["peer_keys"]).then_inc(keys_in, 16)
            inverse_root(0, 2)
            def a_store(b):
                pool.wait_ge(a_ok, b * 2 + 2)
                pool.dma_start(adram[b] if isinstance(b, int) else adram[bass.ds(b, 1)].rearrange("a p n -> p (a n)"),
                               Ab[:].rearrange("p t n -> p (t n)")).then_inc(a_st, 16)

            def expert_in(v, q):
                if not isinstance(v, int) or v >= 2:
                    pool.wait_ge(a_T, v - 1)
                    pool.wait_ge(gated, v * 2 - 2)
                pool.wait_ge(a_st, v * 16 + 16)
                pool.dma_start(Ain[:, q].rearrange("p t n -> p (t n)"),
                               adram[v] if isinstance(v, int) else adram[bass.ds(v, 1)].rearrange("a p n -> p (a n)")
                               ).then_inc(a_in[q], 16)
                pool.dma_start(Gb[:, q], gdram[:, :, slice(v * JB, v * JB + JB) if isinstance(v, int)
                                               else bass.ds(v * JB, JB)].rearrange("c i j t -> i c j t")
                               ).then_inc(g_in[q], 16)

            for b in range(CHOICE):
                a_store(b)
            with pool.Fori(0, 2) as it:
                for e in range(2):
                    for b in range(2):
                        pool.wait_ge(g_out[b], it * 16 + (8 * e + 8))
                    pool.dma_start(gdram[bass.ds(it * 2 + e, 1)].rearrange("c i j t -> i (c j t)"),
                                   gst[:, e].rearrange("p j t -> p (j t)")).then_inc(g_st[e], 16)
                    a_store(it * 2 + (CHOICE + e))
            for b in range(CHOICE + GATES, AHEAD):
                a_store(b)
            for e in range(2):
                pool.wait_ge(g_st[e], 32)
            expert_in(0, 0)
            with pool.Fori(0, MAIN // 2) as it:
                for e in range(2):
                    expert_in(it * 2 + (e + 1), (e + 1) % 2)
                    a_store(it * 2 + (AHEAD + e))
            pool.wait_ge(mod_used, 4 * KD)
            pool.dma_start(gfin[:], A["g_final"].partition_broadcast(P)).then_inc(gfin_in, 16)
            for v in range(MAIN + 1, NBLK):
                expert_in(v, v % 2)
            st = Steps(pool, pool_step)
            lre, lim = C("lre", 0, STT), C("lim", 0, STT)
            st.step(GP.memset(sv[:, 0], math.e))
            st.link(GP.memset(sv[:, 20], -1.0))
            st.link(GP.tensor_tensor(sv[:, 1], sv[:, 0], C("ldt", 0, STT), ALU.pow))
            st.step(GP.tensor_tensor(sv[:, 2], lim, sv[:, 1], ALU.mult))
            st.link(GP.tensor_tensor(sv[:, 3], lre, sv[:, 1], ALU.mult))
            st.step(GP.tensor_tensor(sv[:, 4], sv[:, 0], sv[:, 3], ALU.pow))
            st.step(GP.tensor_scalar(sv[:, 10], sv[:, 2], INV_2PI, None, ALU.mult))
            st.link(GP.tensor_scalar(sv[:, 11], sv[:, 2], INV_2PI, 0.25, ALU.mult, ALU.add))
            st.link(GP.tensor_scalar(sv[:, 10:12], sv[:, 10:12], MAGIC, None, ALU.add))
            st.link(GP.tensor_scalar(sv[:, 10:12], sv[:, 10:12], MAGIC, None, ALU.subtract))
            for i, part in enumerate((C1, C2, C3)):
                st.link(GP.tensor_scalar(sv[:, 12:14], sv[:, 10:12], -part, None, ALU.mult))
                for j in range(2):
                    st.step(GP.tensor_tensor(sv[:, 6 + j], sv[:, 2 if i == 0 else 6 + j], sv[:, 12 + j], ALU.add))
                st.wait()
            st.step(GP.tensor_scalar(sv[:, 5], sv[:, 6], INV_2PI, None, ALU.mult))
            st.link(GP.tensor_scalar(sv[:, 7], sv[:, 7], math.pi / 2, None, ALU.add))
            GP.tensor_scalar(sv[:, 6:8], sv[:, 6:8], PI_IN, -PI_IN, ALU.min, ALU.max).then_inc(sv_arg, 1)
            st.step(GP.tensor_tensor(sv[:, 12], lre, lre, ALU.mult))
            st.link(GP.tensor_tensor(sv[:, 13], lim, lim, ALU.mult))
            st.link(GP.tensor_tensor(sv[:, 12], sv[:, 12], sv[:, 13], ALU.add))
            st.link(GP.tensor_tensor(sv[:, 12], sv[:, 12], sv[:, 20], ALU.pow))
            inverse_root(0, 2)
            inverse_root(0, 2)
            pool.wait_ge(sv_sin, 1)
            st.step(GP.tensor_tensor(sv[:, 14], sv[:, 4], sv[:, 9], ALU.mult))
            st.link(GP.tensor_tensor(sv[:, 15], sv[:, 4], sv[:, 8], ALU.mult))
            st.link(GP.tensor_scalar(sv[:, 14], sv[:, 14], -1.0, None, ALU.add))
            st.step(GP.tensor_tensor(sv[:, 16], sv[:, 14], lre, ALU.mult))
            st.step(GP.tensor_tensor(sv[:, 17], sv[:, 15], lim, ALU.mult))
            st.step(GP.tensor_tensor(sv[:, 18], sv[:, 15], lre, ALU.mult))
            st.link(GP.tensor_tensor(sv[:, 19], sv[:, 14], lim, ALU.mult))
            st.step(GP.tensor_tensor(sv[:, 16], sv[:, 16], sv[:, 17], ALU.add))
            st.link(GP.tensor_tensor(sv[:, 18], sv[:, 18], sv[:, 19], ALU.subtract))
            GP.tensor_tensor(sv[:, 16], sv[:, 16], sv[:, 12], ALU.mult).then_inc(sv_ok, 1)
            GP.tensor_tensor(sv[:, 18], sv[:, 18], sv[:, 12], ALU.mult).then_inc(sv_ok, 1)
            pool.dma_start(gqk[:, 0], A["q_norm_g"].partition_broadcast(P)).then_inc(gqk_in, 16)
            pool.dma_start(gqk[:, 1], A["k_norm_g"].partition_broadcast(P)).then_inc(gqk_in, 16)
            inverse_root(0, 32)
            pool.wait_ge(qk_rope, 8)
            for i, n in enumerate(("ssm_b_re", "ssm_b_im")):
                pool.dma_start(ssmB[:, i], A[n]).then_inc(ssm_in, 16)
            pool.wait_ge(ut_ok, 4)
            for i, n in enumerate(("ssm_c_re", "ssm_c_im")):
                pool.dma_start(ssmC[:, i], A[n]).then_inc(ssmc_in, 16)
            GP.memset(bM[:], 0.0).then_inc(blocks_zero, 1)
            GP.memset(cM[:], 0.0).then_inc(blocks_zero, 1)
            def forward(e, q):
                pool.wait_ge(scan_ok, q * 4 + 4)
                zr, sn, cn = rz[:, e, 0], cs[:, e, 0], cs[:, e, 1]
                GP.tensor_tensor(fw[:, e, 0], zr, cn, ALU.mult).then_inc(fw_p, 1)
                pool.wait_ge(fw_p, q * 2 + 1)
                GP.tensor_tensor(zr, zr, sn, ALU.mult).then_inc(fw_p, 1)

            with pool.Fori(0, 8) as it:
                for e in range(2):
                    forward(e, it * 2 + e)
            pool.wait_ge(yspl_l, 1)
            pool.dma_start(bglu[:], A["b_glu"]).then_inc(bglu_in, 16)
            pool.wait_ge(turned, TBASE["merged2"] + 8)
            GP.memset(Y[:], 0.0).then_inc(y_zero, 1)
            inverse_root(0, 2)

        @block.scalar
        def _(act):
            st = Steps(act, act_step)

            def split(n0, off=0):
                if n0 >= TOTAL:
                    return
                act.wait_ge(raw_ready[n0 % RAW], 16 * (n0 // RAW + 1) + off * (16 // RAW))
                if n0 >= SPL:
                    act.wait_ge(tile_used, n0 - SPL + 1 + off)
                SC.copy(hi[:, n0 % SPL], raw[:, n0 % RAW]).then_inc(hi_ready, 1)

            def splits(n0, count, off=0):
                for j in range(count):
                    split(n0 + SPL + j, off)

            squares = [0]

            def sumsq(junk, src, accum, bias=0.0):
                if squares[0]:
                    act.wait_ge(sq_ready, squares[0])
                squares[0] += 1
                SC.activation(junk, src, ACT.Square, bias=bias, accum_out=accum).then_inc(sq_ready, 1)

            def turn(name, rounds, h, scale=None, bias=None, after=None):
                for r in range(rounds):
                    g = TBASE[name] + r
                    act.wait_ge(turned, g + 1)
                    bank = ps[:, 4 + g % 2].rearrange("p (k t) -> p k t", k=2)
                    if r == 0 and after is not None:
                        act.wait_ge(tile_used, after)
                    for k in range(2):
                        kk = 2 * r + k
                        if scale is None:
                            if k == 0:
                                SC.copy(h[:, kk:kk + 2], bank).then_inc(turn_hi, 2)
                        elif bias is None:
                            SC.activation(h[:, kk], bank[:, k], ACT.Copy, scale=scale(kk)).then_inc(turn_hi, 1)
                        else:
                            SC.activation(h[:, kk], bank[:, k], ACT.Identity, scale=scale(kk),
                                          bias=bias(kk)).then_inc(turn_hi, 1)

            for t in range(TT):
                act.wait_ge(x_in[t], 16)
                sumsq(junk[:], X[:, t], stat[:, 8 + t:9 + t])
            for j in range(SPL):
                split(j)
            act.wait_ge(small_in, 32)
            turn("h1", 8, xh, scale=lambda k: C("g1", k))
            act.wait_ge(trig_arg, 1)
            SC.activation(trig[:], ang[:, 4:6], ACT.Sin).then_inc(trig_ok, 1)
            def evac(pair, ab, dst, func, off=0, pinc=None):
                act.wait_ge(tile_used, pair)
                for t in range(TT):
                    SC.activation(dst(t), ps[:, 2 * ab + t], func).then_inc(acc_free[ab], 1)

            splits(0, TC)
            evac(TC, 0, lambda t: CQ[:, t], ACT.Copy)
            splits(TC, TC)
            evac(2 * TC, 1, lambda t: CKV[:, t], ACT.Copy)
            with act.Fori(0, 4) as it:
                for ab in range(2):
                    splits((2 + ab) * TC, TC, it * (2 * TC))
                    evac(it * (2 * TC) + (3 + ab) * TC, ab,
                         lambda t: Z[:, t, bass.ds(it * 1024 + 512 * ab, CH)], ACT.Gelu_apprx_tanh)
            split(BASE["kpe"] + SPL)
            act.wait_ge(tile_used, BASE["kpe"] + 1)
            SC.copy(KPT[0:ROPE], ps[0:ROPE, 4, 0:S]).then_inc(kpe_T, 1)
            unused = ps[:, 4:8].rearrange("p a n -> p (a n)")
            for c in range(8):
                for j in range(TC):
                    split(BASE["gate"] + c * TC + SPL + j)
                    t = j // 2
                    if c == 0 and j in (0, 2):
                        if t == 0:
                            act.wait_ge(kpe_ps, 1)
                            SC.copy(KPE[:], ps[:, 5, 0:TT * ROPE].rearrange("p (t n) -> p t n", t=TT)
                                    ).then_inc(kpe_out, 1)
                            act.wait_ge(kpe_out, 1)
                            for ab in range(2):
                                act.wait_ge(acc_free[ab], 10)
                        else:
                            act.wait_ge(ln_sum, 1)
                        SC.activation(unused, Z[:, t, D:2 * D], ACT.Copy, accum_out=stat[:, 16 + t:17 + t]
                                      ).then_inc(ln_sum, 1)
                    elif c == 1 and j in (0, 2):
                        if t == 0:
                            act.wait_ge(ln_sum, 2)
                            act.wait_ge(ln_mu, 1)
                        sumsq(unused, Z[:, t, D:2 * D], stat[:, 8 + t:9 + t], stat[:, 18 + t:19 + t])
                    elif c == 2 and j % 2 == 0:
                        src = (CQ, CKV)[t // 2][:, t % 2]
                        sumsq(unused[:, 0:LORA], src, stat[:, 10 + t:11 + t])
                if c == 4:
                    act.wait_ge(ln_done, 2)
                evac(BASE["gate"] + (c + 1) * TC, c % 2, lambda t: GT[:, t, c * CH:(c + 1) * CH], ACT.Sigmoid)
            turn("cq", 2, cqh, scale=lambda k: C("gqa", k), after=BASE["mla"])
            turn("ckv", 2, ckh, scale=lambda k: C("gkva", k))
            act.wait_ge(kpt_ps, 1)
            SC.copy(KPT[:], ps[:, 6, 0:S]).then_inc(kpt_ok, 1)

            def probs(h, s, p, stats, off=0):
                act.wait_ge(s_max, h + 1 + off)
                b, q = h % 2, h % 2 if h >= 16 else h % 4
                if h >= 2 or not isinstance(off, int):
                    act.wait_ge(pt_ps, max(h - 1, 0) + off)
                SC.activation(p[:, b, 0:P], s[:, b, 0:P], ACT.Exp, bias=stats(q, 0),
                              accum_out=stats(q, 2)).then_inc(p_ready, 1)
                SC.activation(p[:, b, P:384], s[:, b, P:384], ACT.Exp, bias=stats(q, 1),
                              accum_out=stats(q, 3)).then_inc(p_ready, 1)

            def probsT(h, dst, bank, off=0):
                act.wait_ge(pt_ps, h + 1 + off)
                if h >= 2 or not isinstance(off, int):
                    act.wait_ge(o_ready, max(h - 1, 0) + off)
                SC.copy(dst[:, h % 2], ps[:, bank, 0:384]).then_inc(pt_ok, 1)

            def stat_col(q, i):
                return stat[:, 32 + 4 * q + i:33 + 4 * q + i]

            act.wait_ge(sgu_ok, 2)
            with act.Fori(0, 4) as it:
                n0 = BASE["mla"]
                for j, (dst, w) in enumerate(((qn, CH), (qr, GROUP * ROPE), (kn, CH), (vv, CH))):
                    splits(n0 + TL * j, TL, it * (4 * TL))
                    act.wait_ge(tile_used, it * (4 * TL) + (n0 + TL * j + TL))
                    if j == 0:
                        act.wait_ge(m_tr, it * 3)
                    if j == 3:
                        act.wait_ge(o_ready, it * 4)
                    for t in range(TT):
                        SC.copy(dst[:, t], ps[:, 2 * j + t, 0:w]).then_inc(m_evac, 1)
                act.wait_ge(m_tr, it * 3 + 1)
                act.wait_ge(s_ready, it * 4)
                SC.copy(qT[:].rearrange("p h t -> p (h t)"), ps[:, 0:2].rearrange("p a n -> p (a n)")
                        ).then_inc(m_ta, 1)
                act.wait_ge(m_tr, it * 3 + 3)
                SC.copy(qrT[:].rearrange("p h t -> p (h t)"), ps[:, 4]).then_inc(m_ta, 1)
                for h in range(GROUP + 1):
                    if h < GROUP:
                        probs(h, sc, pr, stat_col, it * 4)
                    if h >= 1:
                        probsT(h - 1, pT, (4, 7)[(h - 1) % 2], it * 4)
            turn("merged", 8, xh, after=BASE["out"])
            splits(BASE["out"], 4 * TC)
            act.wait_ge(acc_free[1], 22)
            for t in range(TT):
                sumsq(junk2[:], X[:, t], stat[:, 8 + t:9 + t])
            turn("h2", 8, xh, scale=lambda k: C("g2", k), after=BASE["pq"])
            for pair in range(2):
                for ab in range(2):
                    splits(BASE["pq"] + (2 * pair + ab) * TC, TC)
                    evac(BASE["pq"] + (2 * pair + ab + 1) * TC, ab,
                         lambda t: Q[:, t, 1024 * pair + 512 * ab:1024 * pair + 512 * ab + CH], ACT.Copy)
            for g in range(8):
                act.wait_ge(qt_ps, g + 1)
                SC.copy(QT[:, 2 * g:2 * g + 2], ps[:, 4 + g % 2].rearrange("p (k t) -> p k t", k=2)
                        ).then_inc(qt_ok, 1)
            for g in range(8):
                act.wait_ge(sub_ps, g + 1)
                SC.copy(sub[:, 4 * g:4 * g + 4].rearrange("p a n -> p (a n)"), ps[:, 4 + g % 4]
                        ).then_inc(sub_ok, 1)
            act.wait_ge(small_in, 32)
            SC.activation(stat[:, 64:80], C("c", 0, KD), ACT.Silu).then_inc(csil, 1)
            n0 = BASE["peer"]

            def gelu(b, n, bank=0):
                act.wait_ge(tile_used, n)
                if not isinstance(b, int) or b:
                    act.wait_ge(a_st, b * 16)
                for t in range(TT):
                    SC.activation(Ab[:, t], ps[:, bank + t], ACT.Gelu_apprx_tanh).then_inc(a_ok, 1)

            for b in range(CHOICE):
                splits(n0 + b * TC, TC)
                gelu(b, n0 + b * TC + TC, 2 * (b % 2))
            act.wait_ge(gate_in, 1)
            SC.activation(sel[:, 2], sel[:, 2], ACT.Exp).then_inc(gate_exp, 1)
            act.wait_ge(selT_ps, 1)
            act.wait_ge(sel_ok, 1)
            for i in range(3):
                SC.copy(selT[:, i], ps[:, 4 + i, 0:S]).then_inc(selT_ok, 1)
            with act.Fori(0, 2) as it:
                for e in range(2):
                    act.wait_ge(g_st[e], it * 16)
                    for g in range(GQ // GT4):
                        act.wait_ge(g_ps[g % 2], it * 16 + (8 * e + g // 2 + 1))
                        SC.copy(gst[:, e, :, GT4 * g:GT4 * g + GT4],
                                ps[:, 4 + g % 2].rearrange("p (k j) -> p j k", k=GT4)).then_inc(g_out[g % 2], 1)
                        if g % 2:
                            split(n0 + (CHOICE + e) * TC + SPL + g // 2, it * (2 * TC))
                    gelu(it * 2 + (CHOICE + e), it * (2 * TC) + (n0 + (CHOICE + e + 1) * TC))
            for b in range(CHOICE + GATES, AHEAD):
                splits(n0 + b * TC, TC)
                gelu(b, n0 + b * TC + TC)

            n0 = BASE["peer"] + AHEAD * TC

            def act_high(v, q, used):
                act.wait_ge(gated, v * 2 + 2)
                if used is not None:
                    act.wait_ge(tile_used, used)
                SC.copy(Ph[:, q], P32[:, q]).then_inc(ph_ok, 1)

            def mod_load(u, rr):
                act.dma_start(mraw[:, u % 4], A["w_mod"][bass.ds(rr * KD + u, 1)].rearrange("a p n -> p (a n)")
                              ).then_inc(mod_in[u % 4], 16)

            act_high(0, 0, None)
            with act.Fori(0, MAIN // 4) as rr:
                act.wait_ge(mod_used, rr * KD)
                for u in range(3):
                    mod_load(u, rr)
                for i in range(4):
                    n, off = n0 + 16 * i, rr * 64
                    for j in range(4):
                        split(n + 4 + 2 * j, off)
                        split(n + 5 + 2 * j, off)
                        u = 4 * i + j
                        if u + 3 < KD:
                            act.wait_ge(mod_used, rr * KD + u)
                            mod_load(u + 3, rr)
                    gelu(rr * 4 + (AHEAD + i), off + (n + 8))
                    split(n + 12, off)
                    split(n + 13, off)
                    act_high(rr * 4 + (i + 1), (i + 1) % 2, off + n)
                    for j in range(14, 20):
                        split(n + j, off)
            n0 += 16 * MAIN

            def act_tail(v, q, n, off):
                act.wait_ge(mod_used, v + (4 * KD - MAIN))
                act.dma_start(mraw[:, q], A["w_mod"][v + (4 * KD - MAIN)] if isinstance(v, int) else
                              A["w_mod"][bass.ds(v + (4 * KD - MAIN), 1)].rearrange("a p n -> p (a n)")
                              ).then_inc(mod_in[q], 16)
                split(n + 4, off)
                split(n + 5, off)
                if not isinstance(v, int) or v < NBLK - 1:
                    act_high(v + 1, 1 - q, off + n)
                for j in range(6, 12):
                    split(n + j, off)

            with act.Fori(0, AHEAD // 2 - 1) as it:
                for e in range(2):
                    act_tail(it * 2 + (MAIN + e), e, n0 + 8 * e, it * 16)
            act_tail(NBLK - 2, 0, n0 + 8 * AHEAD - 16, 0)
            act_tail(NBLK - 1, 1, n0 + 8 * AHEAD - 8, 0)
            act.wait_ge(v_out, 8 * NBLK)
            for t in range(TT):
                sumsq(junk2[:], X[:, t], stat[:, 8 + t:9 + t])
            for t in range(TT):
                act.wait_ge(normed, 9 + t)
                sumsq(junk2[:], X[:, t], stat[:, 8 + t:9 + t])
            act.wait_ge(sv_arg, 1)
            SC.activation(sv[:, 8:10], sv[:, 6:8], ACT.Sin).then_inc(sv_sin, 1)
            act.wait_ge(mcol_ok, 1)
            turn("h3", 8, xh, scale=lambda k: mcol[:, 1, k:k + 1], bias=lambda k: mcol[:, 0, k:k + 1],
                 after=BASE["in2"])
            def qkvu(it, units):
                for ab in range(2):
                    n, off = BASE["in2"] + ab * TC, it * (2 * TC)
                    for u, k in units[ab]:
                        split(n + SPL, off)
                        if u is not None:
                            act.wait_ge(mod2_used, it * 6 + u)
                            act.dma_start(mraw2[:], A["w_mod"][bass.ds(it * 6 + (5 * KD + u), 1)]
                                          .rearrange("a p n -> p (a n)")).then_inc(mod2_in, 16)
                        splits(n + 1, k - 1, off)
                        n += k
                    evac(off + (BASE["in2"] + (1 + ab) * TC), ab,
                         lambda t: QKVU[:, t, bass.ds(it * 1024 + 512 * ab, CH)], ACT.Copy)

            with act.Fori(0, 2) as it:
                qkvu(it, MOD_SIX)
            for ab in range(2):
                act.wait_ge(acc_free[ab], 2 * (PB["in2"] + 2))
            for t in range(TT):
                SC.activation(sq2[:, t], QKVU[:, t, 0:2 * AW], ACT.Square).then_inc(qk_sq, 1)
                qkvu(2 + t, (MOD_FOUR, MOD_NONE)[t])
            act.wait_ge(mod2_ps, 1)
            with act.Fori(0, 4) as it:
                for ab in range(2):
                    h, n = 16 + ab, BASE["in2"] + (8 + ab) * TC
                    splits(n, 2, it * (2 * TC))
                    act.wait_ge(qk_tr, it * 2 + (ab + 1))
                    SC.copy(qkT[:].rearrange("p a t -> p (a t)"), ps[:, 7]).then_inc(qk_out, 1)
                    splits(n + 2, 2, it * (2 * TC))
                    probs(h, sc2, pr2, stat_col, it * 2)
                    splits(n + 4, 2, it * (2 * TC))
                    probsT(h, pT2, 5, it * 2)
                    splits(n + 6, 2, it * (2 * TC))
                    evac(it * (2 * TC) + (n + TC), ab,
                         lambda t: G2[:, t, bass.ds(it * 1024 + 512 * ab, CH)], ACT.Sigmoid)
            for g in range(4):
                act.wait_ge(ut_ps, g + 1)
                SC.copy(uT[:, 2 * g:2 * g + 2], ps[:, 4 + g % 2].rearrange("p (k t) -> p k t", k=2)
                        ).then_inc(ut_ok, 1)
            def turns_of(q, col):
                act.wait_ge(cs_ok, q * 3)
                act.wait_ge(ph_arg, q)
                for i in range(2):
                    turns = sv[:, 5, bass.ds(col + i, 1)] if not isinstance(col, int) else sv[:, 5, col + i:col + i + 1]
                    SC.activation(px[:, i], iota, ACT.Copy, scale=turns).then_inc(ph_x, 1)
                    SC.activation(pr_[:, i], iota, ACT.Identity, scale=turns, bias=K("magic")).then_inc(ph_x, 1)

            def sines(e, q):
                act.wait_ge(ph_arg, q + 1)
                if not isinstance(q, int) or q >= 2:
                    act.wait_ge(fw_ok, q * 2 - 2)
                    act.wait_ge(fw_p, q * 2 - 2)
                SC.activation(cs[:, e, 0], pr_[:], ACT.Sin, scale=-TURN).then_inc(cs_ok, 1)
                act.wait_ge(cs_ok, q * 3 + 1)
                SC.activation(pr_[:], pr_[:], ACT.Abs).then_inc(cs_ok, 1)
                act.wait_ge(cs_ok, q * 3 + 2)
                SC.activation(cs[:, e, 1], pr_[:], ACT.Sin, scale=-TURN, bias=K("halfpi")).then_inc(cs_ok, 1)

            def b_copy(it):
                for i in range(2):
                    act.wait_ge(bl_ps, it * 2 + (i + 1))
                    SC.copy(bL[:, i].rearrange("p s n -> p (s n)"), ps[:, 6 + i]).then_inc(bl_ok, 1)

            def y_gelu(it):
                act.wait_ge(y_sum, it + 1)
                y = (yT[:, it] if isinstance(it, int) else yT[:, bass.ds(it, 1)].rearrange("p a t -> p (a t)"))
                SC.activation(y, y, ACT.Gelu_apprx_tanh).then_inc(y_ok, 1)

            def diagonal(m, src, it, sign, done):
                for half in range(2):
                    p0 = 64 * half
                    flat = m.rearrange("p s n -> p (s n)")[p0:p0 + 64]
                    dst = bass.AP(flat.tensor, flat.offset + GH * half,
                                  [list(flat.ap[0]), [P + 2 * GH, SB], [1, GH]])
                    block = src[p0:p0 + 64, it * SB:it * SB + SB] if isinstance(it, int) else \
                        src[p0:p0 + 64, bass.ds(it * SB, SB)]
                    SC.activation(dst, block, ACT.Copy, scale=sign).then_inc(done, 1)

            def b_blocks(it):
                act.wait_ge(bl_ps, it * 2)
                for i in range(2):
                    diagonal(bM[:, i], cB[:, i], it, 1.0, bm_ok)

            def c_blocks(it):
                act.wait_ge(y_ps, it * 2)
                for i in range(2):
                    diagonal(cM[:, i], ssmC[:, i], it, (1.0, -1.0)[i], cm_ok)

            act.wait_ge(sv_ok, 2)
            turns_of(0, 0)
            sines(0, 0)
            turns_of(1, 2)
            act.wait_ge(cb_ok, 1)
            act.wait_ge(blocks_zero, 2)
            act.wait_ge(ssmc_in, 32)
            b_blocks(0)
            b_copy(0)
            sines(1, 1)
            turns_of(2, 4)
            c_blocks(0)
            b_blocks(1)
            b_copy(1)
            sines(0, 2)
            turns_of(3, 6)
            with act.Fori(1, 7) as it:
                sines(1, it * 2 + 1)
                turns_of(it * 2 + 2, it * SB + SB)
                c_blocks(it)
                b_blocks(it + 1)
                b_copy(it + 1)
                y_gelu(it - 1)
                sines(0, it * 2 + 2)
                turns_of(it * 2 + 3, it * SB + (SB + 2))
            sines(1, 15)
            c_blocks(7)
            y_gelu(6)
            y_gelu(7)

            def spread_vector(dst, n):
                for q in range(4):
                    act.wait_ge(spread, 4 * n - 3 + q)
                    SC.copy(dst[:, CH * q:CH * q + CH], ps[:, 4 + q]).then_inc(spread_out, 1)

            act.wait_ge(y_ok, 8)
            SC.copy(yh[:], yT[:]).then_inc(yspl_h, 1)
            splits(BASE["glu"], TA)
            evac(BASE["glu"] + TA, 0, lambda t: SG[:, t, 0:CH], ACT.Sigmoid)
            splits(BASE["glu"] + TA, TA)
            evac(BASE["glu"] + 2 * TA, 1, lambda t: SG[:, t, CH:2 * CH], ACT.Sigmoid)
            for g in range(4):
                act.wait_ge(y32_ok, g + 1)
                SC.copy(yh[:, 2 * g:2 * g + 2], Y32[:]).then_inc(yg_h, 1)
            turn("ya", 4, yah, after=BASE["abr"])
            splits(BASE["abr"], 4 * TA)
            splits(BASE["sbr"], 4 * TA)
            spread_vector(g1b, 1)
            turn("merged2", 8, xh, after=BASE["out2"])
            splits(BASE["out2"], 4 * TC)
            act.wait_ge(acc_free[1], 2 * (PB["out2"] + 2))
            for t in range(TT):
                sumsq(junk2[:], X[:, t], stat[:, 8 + t:9 + t])
            spread_vector(g2b, 2)
            act.wait_ge(mcol_ok, 2)
            turn("h4", 8, xh, scale=lambda k: mcol[:, 3, k:k + 1], bias=lambda k: mcol[:, 2, k:k + 1],
                 after=BASE["ffn"])

            n0 = BASE["ffn"]

            def up_evac(b, half, n):
                act.wait_ge(tile_used, n)
                if half == 0 and (not isinstance(b, int) or b):
                    act.wait_ge(up_T, b * 2)
                for t in range(TT):
                    SC.copy(UP[:, half, t], ps[:, 2 * half + t]).then_inc(up_out, 1)

            def conv_base(b, half):
                act.wait_ge(cc_ok, b + 1)
                act.wait_ge(up_T, b * 2 + (half + 1))
                for f in range(4):
                    q = 16 * half + 4 * f
                    SC.activation(cv[:, half, f], ps[:, 4 + 2 * half + f // 2, S * (f % 2):S * (f % 2) + S],
                                  ACT.Identity, scale=ccol[:, q + 2:q + 3], bias=ccol[:, q + 3:q + 4]
                                  ).then_inc(cv_base, 1)

            def silu(b):
                act.wait_ge(cv_ok, b * 2 + 2)
                SC.activation(sil[:], cv[:, 1], ACT.Silu).then_inc(sil_ok, 1)

            def act_high(b):
                act.wait_ge(f32_ok, b + 1)
                if not isinstance(b, int) or 0 < b < FB - 1:
                    act.wait_ge(tile_used, b * 24 + n0)
                last = isinstance(b, int) and b == FB - 1
                SC.copy((Fh2 if last else Fh)[:], F32t[:]).then_inc(fh_ok, 1)

            def hidden(b, rest):
                rest(2)
                conv_base(b, 0)
                rest(1)
                conv_base(b, 1)
                rest(2)
                silu(b)
                rest(2)
                act_high(b)

            def rest(k):
                for _ in range(k):
                    split(local[0], off)
                    local[0] += 1

            splits(n0, TC)
            up_evac(0, 0, n0 + TC)
            splits(n0 + TC, TC)
            up_evac(0, 1, n0 + 2 * TC)
            with act.Fori(1, FB - 1) as b:
                off = b * 24 - 24
                local = [n0 + 16 + SPL]

                hidden(b - 1, rest)
                rest(1)
                up_evac(b, 0, off + (n0 + 24))
                rest(8)
                up_evac(b, 1, off + (n0 + 32))
                rest(8)
            local, off = [TOTAL - 32 + SPL], 0
            hidden(FB - 2, rest)
            rest(1)
            up_evac(FB - 1, 0, TOTAL - 24)
            rest(8)
            up_evac(FB - 1, 1, TOTAL - 16)
            hidden(FB - 1, rest)
            rest(5)
            for c in range(0, 4, 2):
                for t in range(TT):
                    act.wait_ge(y_done, (c + 1) * TT + t + 1)
                    act.dma_start(out[t * P:(t + 1) * P, c * CH:(c + 2) * CH], Y[:, t, c * CH:(c + 2) * CH]
                                  ).then_inc(o_st, 16)
            act.wait_ge(o_st, 64)

        @block.vector
        def _(dve):
            st = Steps(dve, dve_step)

            def split(n0, off=0):
                if n0 >= TOTAL:
                    return
                dve.wait_ge(hi_ready, n0 + 1 + off)
                V.tensor_tensor(lo[:, n0 % SPL], raw[:, n0 % RAW], hi[:, n0 % SPL].bitcast(F32),
                                ALU.subtract).then_inc(lo_ready, 1)

            def splits(n0, count, off=0):
                for j in range(count):
                    split(n0 + SPL + j, off)

            nroot = [0]
            nsq = [0]

            def mean_sq(n, width, sqs):
                nsq[0] += sqs
                dve.wait_ge(sq_ready, nsq[0])
                nroot[0] += 1
                V.tensor_scalar(stat[:, 0:n], stat[:, 8:8 + n], 1.0 / width, EPS, ALU.mult, ALU.add
                                ).then_inc(var_ready, 1)
                dve.wait_ge(rstd_ready, nroot[0])

            def turn(name, rounds, h, l, scale=None, bias=None, tmp=None):
                for r in range(rounds):
                    g = TBASE[name] + r
                    dve.wait_ge(turn_hi, 2 * g + 2)
                    bank = ps[:, 4 + g % 2].rearrange("p (k t) -> p k t", k=2)
                    kk = 2 * r
                    if scale is None:
                        V.tensor_tensor(l[:, kk:kk + 2], bank, h[:, kk:kk + 2].bitcast(F32), ALU.subtract
                                        ).then_inc(turn_lo, 1)
                        continue
                    if bias is not None:
                        if r:
                            dve.wait_ge(turn_lo, g)
                        for k in range(2):
                            st.step(V.tensor_scalar(tmp[:, k], bank[:, k], scale(kk + k), bias(kk + k),
                                                    ALU.mult, ALU.add))
                        st.wait()
                        V.tensor_tensor(l[:, kk:kk + 2], tmp[:], h[:, kk:kk + 2].bitcast(F32), ALU.subtract
                                        ).then_inc(turn_lo, 1)
                        continue
                    st.step(V.scalar_tensor_tensor(l[:, kk], bank[:, 0], scale(kk), h[:, kk].bitcast(F32),
                                                   ALU.mult, ALU.subtract))
                    V.scalar_tensor_tensor(l[:, kk + 1], bank[:, 1], scale(kk + 1), h[:, kk + 1].bitcast(F32),
                                           ALU.mult, ALU.subtract).then_inc(turn_lo, 1)

            mean_sq(2, D, 2)
            for t in range(TT):
                V.tensor_scalar(N1[:, t], X[:, t], stat[:, 2 + t:3 + t], None, ALU.mult).then_inc(normed, 1)
            for j in range(SPL):
                split(j)
            dve.wait_ge(small_in, 32)
            turn("h1", 8, xh, xl, scale=lambda k: C("g1", k))
            dve.wait_ge(pos_in, 32)
            st.link(V.tensor_copy(posf[:], posi[:]))
            for t in range(TT):
                st.step(V.tensor_scalar(ang[:, 0, 32 * t:32 * t + 32], K("freq"), posf[:, t:t + 1], None, ALU.mult))
                st.step(V.tensor_scalar(ang[:, 0, 64 + 64 * t:128 + 64 * t], K("freq2"), posf[:, 2 + t:3 + t],
                                        None, ALU.mult))
            st.wait()
            st.step(V.tensor_scalar(ang[:, 2], ang[:, 0], INV_2PI, None, ALU.mult))
            st.link(V.tensor_scalar(ang[:, 3], ang[:, 0], INV_2PI, 0.25, ALU.mult, ALU.add))
            st.link(V.tensor_scalar(ang[:, 2:4], ang[:, 2:4], MAGIC, None, ALU.add))
            st.link(V.tensor_scalar(ang[:, 2:4], ang[:, 2:4], MAGIC, None, ALU.subtract))
            both = ang[:, 0:1].to_broadcast([P, 2, 192])
            st.link(V.scalar_tensor_tensor(ang[:, 4:6], ang[:, 2:4], -C1, both, ALU.mult, ALU.add))
            st.link(V.scalar_tensor_tensor(ang[:, 4:6], ang[:, 2:4], -C2, ang[:, 4:6], ALU.mult, ALU.add))
            st.link(V.scalar_tensor_tensor(ang[:, 4:6], ang[:, 2:4], -C3, ang[:, 4:6], ALU.mult, ALU.add))
            st.link(V.tensor_scalar(ang[:, 5], ang[:, 5], math.pi / 2, None, ALU.add))
            V.tensor_scalar(ang[:, 4:6], ang[:, 4:6], PI_IN, -PI_IN, ALU.min, ALU.max).then_inc(trig_arg, 1)
            splits(0, 2 * TC)
            st.link(V.tensor_tensor(wsp[:], wsp[:], K("triu").unsqueeze(1).to_broadcast([P, SGU_G, P]), ALU.mult))
            with dve.Fori(0, 4) as it:
                splits(2 * TC, 2 * TC, it * (2 * TC))

            def mixed_in(t, g):
                dve.wait_ge(mixed, t * 4 + g // 2 + 1)
                u = Z[:, t, g * SGU_W:(g + 1) * SGU_W]
                V.scalar_tensor_tensor(u, ps[:, 4 + g // 2, SGU_W * (g % 2):SGU_W * (g % 2) + SGU_W],
                                       C("bsp", g), u, ALU.add, ALU.mult).then_inc(mixed_out, 1)

            def rope32(dst, src, tmp, nh, done=None):
                for t in range(TT):
                    sn = trig[:, 0, 32 * t:32 * t + 32].unsqueeze(1).to_broadcast([P, nh, 32])
                    cn = trig[:, 1, 32 * t:32 * t + 32].unsqueeze(1).to_broadcast([P, nh, 32])
                    s4 = src[:, t].rearrange("p (h b w) -> p h b w", h=nh, b=2)
                    d4 = dst(t)
                    t4_ = tmp[:, t].rearrange("p (h w) -> p h w", h=nh)
                    st.step(V.tensor_tensor(d4[:, :, 0], s4[:, :, 0], cn, ALU.mult))
                    st.link(V.tensor_tensor(t4_, s4[:, :, 1], sn, ALU.mult))
                    st.link(V.tensor_tensor(d4[:, :, 0], d4[:, :, 0], t4_, ALU.subtract))
                    st.step(V.tensor_tensor(d4[:, :, 1], s4[:, :, 0], sn, ALU.mult))
                    st.link(V.tensor_tensor(t4_, s4[:, :, 1], cn, ALU.mult))
                    last = V.tensor_tensor(d4[:, :, 1], d4[:, :, 1], t4_, ALU.add)
                    if done is None:
                        st.link(last)
                    else:
                        last.then_inc(done, 1)

            def gated_half(half):
                for ab in range(2):
                    dve.wait_ge(acc_free[ab], 16 + 2 * half)
                dve.wait_ge(mixed_out, 12 + 4 * half)
                h = slice(half * D // 2, (half + 1) * D // 2)
                g = GT[:, :, D:2 * D][:, :, h]
                V.tensor_tensor(g, g, Z[:, :, h], ALU.mult).then_inc(sgu_ok, 1)

            split(BASE["kpe"] + SPL)
            for c in range(8):
                for j in range(TC):
                    split(BASE["gate"] + c * TC + SPL + j)
                    if c == 0 and j == 7:
                        dve.wait_ge(ln_sum, 2)
                        V.tensor_scalar(stat[:, 18:20], stat[:, 16:18], -1.0 / D, None, ALU.mult).then_inc(ln_mu, 1)
                    elif c == 1 and j == 7:
                        mean_sq(2, D, 2)
                        dve.wait_ge(ln_in, 32)
                    elif c in (2, 3):
                        t, v = c - 2, Z[:, c - 2, D:2 * D]
                        if j == 0:
                            st.step(V.tensor_scalar(v, v, stat[:, 18 + t:19 + t], stat[:, 2 + t:3 + t],
                                                    ALU.add, ALU.mult))
                        elif j == 2:
                            st.wait()
                            st.step(V.tensor_tensor(v, v, lng[:], ALU.mult))
                        elif j == 4:
                            st.wait()
                            V.tensor_tensor(v, v, lnb[:], ALU.add).then_inc(ln_done, 1)
                        elif j == 7 and t == 1:
                            nsq[0] += 4
                            dve.wait_ge(sq_ready, nsq[0])
                            V.tensor_scalar(stat[:, 0:4], stat[:, 10:14], 1.0 / LORA, EPS, ALU.mult, ALU.add
                                            ).then_inc(var_ready, 1)
                    elif c == 4 and j % 2 == 0:
                        if j == 0:
                            nroot[0] += 1
                            dve.wait_ge(rstd_ready, nroot[0])
                        i = j // 2
                        src = (CQ, CKV)[i // 2][:, i % 2]
                        V.tensor_scalar(src, src, stat[:, 4 + i:5 + i], None, ALU.mult).then_inc(normed, 1)
                    elif c == 6 and j == 2:
                        dve.wait_ge(kpe_out, 1)
                        dve.wait_ge(trig_ok, 1)
                        rope32(lambda t: KPR[:, t, 0:64].rearrange("p (h b w) -> p h b w", h=1, b=2), KPE,
                               ktmp[:, :, 0:32], 1)
                        for t in range(TT):
                            V.tensor_copy(KPR[:, t, 64:128], KPR[:, t, 0:64]).then_inc(kpr_ok, 1)
                    elif c in (5, 7):
                        mixed_in((c - 5) // 2, j)
                        if c == 7 and j == 5:
                            gated_half(0)
            turn("cq", 2, cqh, cql, scale=lambda k: C("gqa", k))
            turn("ckv", 2, ckh, ckl, scale=lambda k: C("gkva", k))
            gated_half(1)
            dve.wait_ge(sgu_ok, 2)

            def soft_in(h, s, bank, scale, off=0):
                b, q = h % 2, h % 2 if h >= 16 else h % 4
                dve.wait_ge(s_ready, h + 1 + off)
                if h >= 2 or not isinstance(off, int):
                    dve.wait_ge(p_ready, 2 * max(h - 1, 0) + off * 2)
                st.link(V.scalar_tensor_tensor(s[:, b], ps[:, bank, 0:384], scale, K("mask"), ALU.mult, ALU.add))
                st.step(V.tensor_reduce(stat[:, 144 + 2 * b:145 + 2 * b], s[:, b, 0:P], AX, ALU.max))
                st.link(V.tensor_reduce(stat[:, 145 + 2 * b:146 + 2 * b], s[:, b, P:384], AX, ALU.max))
                V.tensor_scalar(stat[:, 32 + 4 * q:34 + 4 * q], stat[:, 144 + 2 * b:146 + 2 * b], -1.0, None, ALU.mult
                                ).then_inc(s_max, 1)

            def soft_out(h, bank, dst, other, off=0):
                b, q = h % 2, h % 2 if h >= 16 else h % 4
                dve.wait_ge(p_ready, 2 * h + 2 + off * 2)
                st.link(V.reciprocal(stat[:, 148 + 2 * b:150 + 2 * b], stat[:, 34 + 4 * q:36 + 4 * q]))
                dve.wait_ge(o_ready, h + 1 + off)
                for t in range(TT):
                    o = ps[:, bank, P * t:P * t + P]
                    r = stat[:, 148 + 2 * b + t:149 + 2 * b + t]
                    if other is None:
                        V.tensor_scalar(dst(t), o, r, None, ALU.mult).then_inc(o_out, 1)
                    else:
                        V.scalar_tensor_tensor(dst(t), o, r, other(t), ALU.mult, ALU.mult).then_inc(o_out, 1)

            PER = 10 + 16
            with dve.Fori(0, 4) as it:
                st.enter(PER, it)
                n0 = BASE["mla"]
                splits(n0, 2 * TL + 1, it * (4 * TL))
                dve.wait_ge(m_evac, it * 8 + 4)
                dve.wait_ge(m_tr, it * 3)
                rope32(lambda t: qrr[:, t].rearrange("p (h b w) -> p h b w", h=GROUP, b=2), qr, qtmp, GROUP, m_rope)
                splits(n0 + 2 * TL + 1, 2 * TL - 1, it * (4 * TL))
                dve.wait_ge(m_tr, it * 3 + 2)
                dve.wait_ge(s_ready, it * 4)
                V.tensor_copy(kT[:].rearrange("p h t -> p (h t)"), ps[:, 2:4].rearrange("p a n -> p (a n)")
                              ).then_inc(m_tv, 1)
                for h in range(GROUP + 2):
                    if h < GROUP:
                        soft_in(h, sc, 5 + h % 2, float(NOPE + ROPE) ** -0.5, it * 4)
                    if h >= 2:
                        g = h - 2
                        dst = lambda t: GT[:, t, bass.ds(it * CH + g * VH, VH)]
                        soft_out(g, g % 2, dst, dst, it * 4)
                st.leave(PER, 4)
            dve.wait_ge(o_out, 32)
            for t in range(TT):
                V.tensor_tensor(GT[:, t, 0:D], GT[:, t, 0:D], GT[:, t, D:2 * D], ALU.add).then_inc(merged_ok, 1)
            turn("merged", 8, xh, xl)
            for pair in range(2):
                for ab in range(2):
                    n = BASE["out"] + (2 * pair + ab) * TC
                    splits(n, TC)
                    dve.wait_ge(tile_used, n + TC)
                    for t in range(TT):
                        xs = X[:, t, 1024 * pair + 512 * ab:1024 * pair + 512 * ab + CH]
                        V.tensor_tensor(xs, xs, ps[:, 2 * ab + t], ALU.add).then_inc(acc_free[ab], 1)
            dve.wait_ge(acc_free[0], 22)
            dve.wait_ge(acc_free[1], 22)
            mean_sq(2, D, 2)
            for t in range(TT):
                V.tensor_scalar(N2[:, t], X[:, t], stat[:, 2 + t:3 + t], None, ALU.mult).then_inc(normed, 1)
            turn("h2", 8, xh, xl, scale=lambda k: C("g2", k))
            splits(BASE["pq"], 4 * TC)

            early = [BASE["peer"] + SPL]

            def stream():
                split(early[0])
                early[0] += 1

            dve.wait_ge(sub_ok, 8)
            for i in range(32):
                st.step(V.max(vals[:, i, 0:8], sub[:, i]))
                if i % 4 == 3:
                    stream()
            st.wait()
            for i in range(32):
                st.step(V.max_index(vidx[:, i, 0:8], vals[:, i, 0:8], sub[:, i]))
                st.step(V.match_replace(sub2[:, i], vals[:, i, 0:8], sub[:, i], -3e38))
                if i % 2 == 1:
                    stream()
            st.wait()
            for i in range(32):
                st.step(V.max(vals[:, i, 8:16], sub2[:, i]))
                if i % 4 == 3:
                    stream()
            st.wait()
            for i in range(32):
                st.step(V.max_index(vidx[:, i, 8:16], vals[:, i, 8:16], sub2[:, i]))
                if i % 4 == 3:
                    stream()
            st.wait()
            v5 = vals[:].rearrange("p (h q t) k -> p t h q k", h=PH, q=2, t=TT)
            f5 = vidf[:].rearrange("p (h q t) k -> p t h q k", h=PH, q=2, t=TT)
            st.step(V.tensor_copy(vidf[:], vidx[:]))
            for t in range(TT):
                st.step(V.tensor_tensor(
                    cand[:, 8 * t:8 * t + 8].rearrange("p h (a b) -> p h a b", a=TOPK),
                    v5[:, t, :, 0].unsqueeze(3).to_broadcast([P, PH, TOPK, TOPK]),
                    v5[:, t, :, 1].unsqueeze(2).to_broadcast([P, PH, TOPK, TOPK]), ALU.add))
                stream()
            st.wait()
            for i in range(16):
                st.step(V.max(tops[:, i, 0:8], cand[:, i]))
                if i % 4 == 3:
                    stream()
            st.wait()
            for i in range(16):
                st.step(V.max_index(tpos[:, i, 0:8], tops[:, i, 0:8], cand[:, i]))
                st.step(V.match_replace(cand2[:, i], tops[:, i, 0:8], cand[:, i], -3e38))
                if i % 2 == 1:
                    stream()
            st.wait()
            for i in range(16):
                st.step(V.max(tops[:, i, 8:16], cand2[:, i]))
                if i % 4 == 3:
                    stream()
            st.wait()
            for i in range(16):
                st.step(V.max_index(tpos[:, i, 8:16], tops[:, i, 8:16], cand2[:, i]))
                if i % 4 == 3:
                    stream()
            tg = sel[:, 2].rearrange("p t (h k) -> p (t h) k", h=PH)
            st.wait()
            V.tensor_tensor(tg, tops[:], tops[:, :, 0:1].to_broadcast([P, 16, TOPK]), ALU.subtract
                            ).then_inc(gate_in, 1)
            tp = tpos[:].rearrange("p i k -> p (i k)")
            st.step(V.tensor_scalar(tab[:, 0], tp, 4, None, ALU.logical_shift_right))
            st.link(V.tensor_scalar(tab[:, 1], tp, 15, None, ALU.bitwise_and))
            st.link(V.tensor_copy(tabf[:], tab[:]))
            for q in range(2):
                for t in range(TT):
                    sl = tabf[:, q, 128 * t:128 * t + 128].rearrange("p (h k) -> p h k", h=PH)
                    st.link(V.tensor_tensor(eq[:], sl.unsqueeze(3).to_broadcast([P, PH, TOPK, TOPK]),
                                            iota[:, 0:TOPK].unsqueeze(1).unsqueeze(1).to_broadcast([P, PH, TOPK, TOPK]),
                                            ALU.is_equal))
                    st.link(V.tensor_tensor(eq[:], eq[:],
                                            f5[:, t, :, q].unsqueeze(2).to_broadcast([P, PH, TOPK, TOPK]), ALU.mult))
                    stream()
                    stream()
                    st.link(V.tensor_reduce(sel[:, q, t].rearrange("p (h k) -> p h k", h=PH), eq[:], AX, ALU.add))
                    stream()
            while early[0] < BASE["peer"] + 2 + CHOICE * TC:
                stream()
            dve.wait_ge(gate_exp, 1)
            st.link(V.tensor_reduce(stat[:, 80:96], tg, AX, ALU.add))
            st.link(V.reciprocal(stat[:, 96:112], stat[:, 80:96]))
            V.tensor_tensor(tg, tg, stat[:, 96:112].unsqueeze(2).to_broadcast([P, 16, TOPK]), ALU.mult
                            ).then_inc(sel_ok, 1)
            dve.wait_ge(selT_ok, 3)
            n0 = BASE["peer"]
            with dve.Fori(0, 2) as it:
                for e in range(2):
                    for g in range(GQ // GT4):
                        b = g % 2
                        c0 = GQ * e + GT4 * g
                        dve.wait_ge(g_ps[b], it * 16 + (8 * e + g // 2))
                        V.tensor_tensor(oh1[:, b], iota[:, 0:P].unsqueeze(1).to_broadcast([P, GT4, P]),
                                        selT[:, 0, bass.ds(it * (2 * GQ) + c0, GT4)].unsqueeze(2)
                                        .to_broadcast([P, GT4, P]), ALU.is_equal).then_inc(oh_ready[b], 1)
                        for k in range(GT4):
                            V.tensor_scalar(oh2[:, b, k], iota[:, 0:P],
                                            selT[:, 1, bass.ds(it * (2 * GQ) + (c0 + k), 1)],
                                            selT[:, 2, bass.ds(it * (2 * GQ) + (c0 + k), 1)],
                                            ALU.is_equal, ALU.mult).then_inc(oh_ready[b], 1)
                        if b:
                            split(n0 + (CHOICE + e) * TC + 2 + g // 2, it * (2 * TC))
            for j in range((AHEAD - CHOICE - GATES) * TC + 2):
                split(n0 + (CHOICE + GATES) * TC + 2 + j)

            n0 = BASE["peer"] + AHEAD * TC
            dve.wait_ge(csil, 1)

            def mod_unit(u, rr):
                dve.wait_ge(mod_in[u % 4], rr * 64 + 16 * (u // 4 + 1))
                if u == 0:
                    dve.wait_ge(mod_ps, rr)
                    V.tensor_scalar(macc[:], mraw[:, 0], stat[:, 64:65], None, ALU.mult).then_inc(mod_used, 1)
                    return
                dve.wait_ge(mod_used, rr * KD + u)
                V.scalar_tensor_tensor(macc[:], mraw[:, u % 4], stat[:, 64 + u:65 + u], macc[:],
                                       ALU.mult, ALU.add).then_inc(mod_used, 1)

            def gate(v, q, loads):
                dve.wait_ge(a_T, v + 1)
                dve.wait_ge(g_in[q], loads)
                if not isinstance(v, int) or v >= 2:
                    dve.wait_ge(ph_ok, v - 1)
                    dve.wait_ge(pl_ok, v - 1)
                for k in range(2):
                    V.tensor_tensor(P32[:, q, 2 * k:2 * k + 2].rearrange("p k (c n) -> p k c n", c=S // GQ),
                                    ps[:, 2 + k].rearrange("p (k c n) -> p k c n", k=2, c=S // GQ),
                                    Gb[:, q, :, 2 * k:2 * k + 2].rearrange("p c k n -> p k c n"), ALU.mult
                                    ).then_inc(gated, 1)

            def low(v, q):
                dve.wait_ge(ph_ok, v + 1)
                dve.wait_ge(gated, v * 2 + 2)
                V.tensor_tensor(Pl[:, q], P32[:, q], Ph[:, q].bitcast(F32), ALU.subtract).then_inc(pl_ok, 1)

            def v_add(v, c, n):
                dve.wait_ge(tile_used, n)
                if not isinstance(v, int) or v:
                    dve.wait_ge(v_out, v * 8)
                for t in range(TT):
                    xs = X[:, t, c * CH:(c + 1) * CH]
                    V.tensor_tensor(xs, xs, ps[:, 4 + 2 * (c % 2) + t], ALU.add).then_inc(v_out, 1)

            gate(0, 0, 16)
            low(0, 0)
            with dve.Fori(0, MAIN // 4) as rr:
                for i in range(4):
                    n, off, v = n0 + 16 * i, rr * 64, rr * 4 + i
                    for j in range(4):
                        split(n + 4 + 2 * j, off)
                        split(n + 5 + 2 * j, off)
                        mod_unit(4 * i + j, rr)
                    split(n + 12, off)
                    gate(v + 1, (i + 1) % 2, rr * 32 + 16 * ((i + 1) // 2 + 1))
                    split(n + 13, off)
                    v_add(v, 0, off + (n + 10))
                    low(v + 1, (i + 1) % 2)
                    for c in range(1, 4):
                        split(n + 12 + 2 * c, off)
                        split(n + 13 + 2 * c, off)
                        v_add(v, c, off + (n + 10 + 2 * c))
                dve.wait_ge(mod_ps, rr + 1)
                V.tensor_tensor(mcol[:, bass.ds(rr, 1)].rearrange("p a k -> p (a k)"), ps[:, 2, 0:KD],
                                cols[:, bass.ds(rr * KD + COFF["bmod"], KD)], ALU.add).then_inc(mod_col, 1)
            n0 += 16 * MAIN

            dve.wait_ge(mod_ps, 4)
            st.link(V.memset(macc[:], 0.0))

            def dve_tail(v, q, n, off, loads, mods):
                last = isinstance(v, int) and v == NBLK - 1
                if not last:
                    gate(v + 1, 1 - q, loads)
                split(n + 4, off)
                split(n + 5, off)
                v_add(v, 0, off + (n + 2))
                if not last:
                    low(v + 1, 1 - q)
                for c in range(1, 4):
                    split(n + 4 + 2 * c, off)
                    split(n + 5 + 2 * c, off)
                    v_add(v, c, off + (n + 2 + 2 * c))
                    if c == 1:
                        dve.wait_ge(mod_in[q], mods)
                        dve.wait_ge(mod_used, v + (4 * KD - MAIN))
                        k = v + (64 - MAIN)
                        V.scalar_tensor_tensor(macc[:], mraw[:, q], stat[:, k:k + 1] if isinstance(k, int) else
                                               stat[:, bass.ds(k, 1)], macc[:], ALU.mult, ALU.add
                                               ).then_inc(mod_used, 1)

            with dve.Fori(0, AHEAD // 2 - 1) as it:
                for e in range(2):
                    dve_tail(it * 2 + (MAIN + e), e, n0 + 8 * e, it * 16,
                             it * 16 + 16 * ((MAIN + e + 1) // 2 + 1), it * 16 + (16 * KD + 16))
            dve_tail(NBLK - 2, 0, n0 + 8 * AHEAD - 16, 0, 16 * (NBLK // 2), 16 * KD + 8 * AHEAD)
            dve_tail(NBLK - 1, 1, n0 + 8 * AHEAD - 8, 0, None, 16 * KD + 8 * AHEAD)
            dve.wait_ge(v_out, 8 * NBLK)
            mean_sq(2, D, 2)
            dve.wait_ge(gfin_in, 16)
            for t in range(TT):
                V.scalar_tensor_tensor(X[:, t], X[:, t], stat[:, 2 + t:3 + t], gfin[:], ALU.mult, ALU.mult
                                       ).then_inc(normed, 1)
            dve.wait_ge(mod_ps, 5)
            V.tensor_tensor(mcol[:, 4], ps[:, 0, 0:KD], C("bmod", 4 * KD, KD), ALU.add).then_inc(mod_col, 1)
            dve.wait_ge(mod_col, 4)
            V.scalar_tensor_tensor(mcol[:, 1], mcol[:, 1], 1.0, C("g3", 0, KD), ALU.add, ALU.mult).then_inc(mcol_ok, 1)
            dve.wait_ge(normed, 10)
            mean_sq(2, D, 2)
            for t in range(TT):
                V.tensor_scalar(N3[:, t], X[:, t], stat[:, 2 + t:3 + t], None, ALU.mult).then_inc(normed, 1)
            dve.wait_ge(mcol_ok, 1)
            turn("h3", 8, xh, xl, scale=lambda k: mcol[:, 1, k:k + 1], bias=lambda k: mcol[:, 0, k:k + 1], tmp=t3)
            st.link(V.memset(macc2[:], 0.0))

            def qkvu(it, units, between=()):
                n, off = BASE["in2"], it * (2 * TC)
                for i, (u, k) in enumerate(units[0] + units[1]):
                    splits(n, k, off)
                    n += k
                    if u is not None:
                        dve.wait_ge(mod2_in, it * 96 + (16 * u + 16))
                        dve.wait_ge(mod2_used, it * 6 + u)
                        V.scalar_tensor_tensor(macc2[:], mraw2[:], stat[:, bass.ds(it * 6 + (64 + u), 1)], macc2[:],
                                               ALU.mult, ALU.add).then_inc(mod2_used, 1)
                    if between:
                        between[i]()

            with dve.Fori(0, 2) as it:
                qkvu(it, MOD_SIX)

            def qk_sums(t):
                dve.wait_ge(qk_sq, t + 1)
                st.step(V.tensor_reduce(stat[:, 112 + 16 * t:128 + 16 * t], heads_rows(sq2[:, t], 16, AD), AX, ALU.add))

            def qk_mean():
                qk_sums(1)
                st.wait()
                nroot[0] += 1
                V.tensor_scalar(stat[:, 0:32], stat[:, 112:144], 1.0 / AD, EPS, ALU.mult, ALU.add).then_inc(var_ready, 1)

            def qk_norm(t):
                if t == 0:
                    dve.wait_ge(rstd_ready, nroot[0])
                    dve.wait_ge(gqk_in, 32)
                v = QKVU[:, t, 0:2 * AW]
                v3 = heads_rows(v, 16, AD)
                st.link(V.tensor_tensor(v3, v3, stat[:, 32 + 16 * t:48 + 16 * t].unsqueeze(2).to_broadcast([P, 16, AD]),
                                        ALU.mult))
                v4 = v.rearrange("p (a h w) -> p a h w", a=2, h=AH)
                st.step(V.tensor_tensor(v4, v4, gqk[:].unsqueeze(2).to_broadcast([P, 2, AH, AD]), ALU.mult))

            none = lambda: None
            qkvu(2, MOD_FOUR, (none, lambda: qk_sums(0), none, none))
            qkvu(3, MOD_NONE, (qk_mean, lambda: qk_norm(0), lambda: qk_norm(1), none))
            st.wait()

            def rope64(h):
                x = QKVU[:, :, 0:2 * AW].rearrange("p t (a c) -> p t a c", a=2)
                x1, x2 = (x[:, :, :, bass.ds(h * AD + 64 * b, 64)] for b in range(2))
                sn, cn = (trig[:, i, 64:192].rearrange("p (t w) -> p t w", t=TT).unsqueeze(2)
                          .to_broadcast([P, TT, 2, 64]) for i in range(2))
                ta, tb = (rt[:, i].rearrange("p (t a w) -> p t a w", t=TT, a=2) for i in range(2))
                st.step(V.tensor_tensor(ta, x1, cn, ALU.mult))
                st.link(V.tensor_tensor(tb, x2, sn, ALU.mult))
                dve.wait_ge(qk_tr, h)
                st.link(V.tensor_tensor(rqk[:, :, :, 0:64], ta, tb, ALU.subtract))
                st.step(V.tensor_tensor(ta, x1, sn, ALU.mult))
                st.link(V.tensor_tensor(tb, x2, cn, ALU.mult))
                V.tensor_tensor(rqk[:, :, :, 64:128], ta, tb, ALU.add).then_inc(qk_rope, 1)
                dve.wait_ge(qk_rope, h + 1)

            dve.wait_ge(mod2_ps, 1)
            V.tensor_tensor(mcol[:, 5], ps[:, 4, 0:KD], C("bmod", 5 * KD, KD), ALU.add).then_inc(mod_col, 1)
            with dve.Fori(0, 4) as it:
                st.enter(18, it)
                for ab in range(2):
                    h, n = 16 + ab, BASE["in2"] + (8 + ab) * TC
                    rope64(it * 2 + ab)
                    splits(n, 4, it * (2 * TC))
                    soft_in(h, sc2, 4, float(AD) ** -0.5, it * 2)
                    splits(n + 4, 4, it * (2 * TC))
                    soft_out(h, 6, lambda t: QKVU[:, t, bass.ds(it * (2 * AD) + ab * AD, AD)], None, it * 2)
                st.leave(18, 4)
            dve.wait_ge(ut_ok, 4)
            dve.wait_ge(sv_ok, 2)
            cr = sv[:, 16].unsqueeze(2).to_broadcast([P, STT, GH])
            ci = sv[:, 18].unsqueeze(2).to_broadcast([P, STT, GH])
            tmp = rb[:, 0].rearrange("p s t -> p (s t)").rearrange("p (s h) -> p s h", s=STT)
            dve.wait_ge(ssm_in, 32)
            st.step(V.tensor_tensor(cB[:, 0], ssmB[:, 0], cr, ALU.mult))
            st.link(V.tensor_tensor(tmp, ssmB[:, 1], ci, ALU.mult))
            st.link(V.tensor_tensor(cB[:, 0], cB[:, 0], tmp, ALU.subtract))
            st.step(V.tensor_tensor(cB[:, 1], ssmB[:, 1], cr, ALU.mult))
            st.link(V.tensor_tensor(tmp, ssmB[:, 0], ci, ALU.mult))
            V.tensor_tensor(cB[:, 1], cB[:, 1], tmp, ALU.add).then_inc(cb_ok, 1)
            dve.wait_ge(cb_ok, 1)

            def remainder(q):
                dve.wait_ge(ph_x, q * 4 + 4)
                V.scalar_tensor_tensor(pr_[:], pr_[:], MAGIC, px[:], ALU.subtract, ALU.subtract).then_inc(ph_arg, 1)

            def states(e, q, col):
                sn, cn, zr, zi = cs[:, e, 0], cs[:, e, 1], rz[:, e, 0], rz[:, e, 1]
                dve.wait_ge(cs_ok, q * 3 + 3)
                dve.wait_ge(bu_ps, q + 1)
                if not isinstance(q, int) or q >= 2:
                    dve.wait_ge(y_ps, q - 1)
                bre, bim = (ps[:, 2 * e + i].rearrange("p (s t) -> p s t", s=2) for i in range(2))
                st.step(V.tensor_tensor(rb[:, 0], bre, cn, ALU.mult))
                st.step(V.tensor_tensor(zr, bim, sn, ALU.mult))
                st.step(V.tensor_tensor(rb[:, 1], bim, cn, ALU.mult))
                st.link(V.tensor_tensor(zi, bre, sn, ALU.mult))
                V.tensor_tensor(rb[:, 0], rb[:, 0], zr, ALU.add).then_inc(rot_ok, 1)
                V.tensor_tensor(rb[:, 1], rb[:, 1], zi, ALU.subtract).then_inc(rot_ok, 1)
                dve.wait_ge(rot_ok, q * 2 + 2)
                for i in range(2):
                    decay = sv[:, 4, bass.ds(col + i, 1)] if not isinstance(col, int) else sv[:, 4, col + i:col + i + 1]
                    for part in range(2):
                        V.tensor_tensor_scan(rz[:, e, part, i], decay.to_broadcast([P, S]), rb[:, part, i],
                                             0.0, ALU.mult, ALU.add).then_inc(scan_ok, 1)
                dve.wait_ge(scan_ok, q * 4 + 4)
                V.scalar_tensor_tensor(fw[:, e, 1], zi, -1.0, sn, ALU.mult, ALU.mult).then_inc(fw_ok, 1)
                dve.wait_ge(fw_ok, q * 2 + 1)
                V.tensor_tensor(zi, zi, cn, ALU.mult).then_inc(fw_ok, 1)

            def y_add(it):
                dve.wait_ge(y_ps, it * 2 + 2)
                if isinstance(it, int):
                    y, u, d = yT[:, it], uT[:, it], C("dskip", it)
                else:
                    y, u = (a[:, bass.ds(it, 1)].rearrange("p a t -> p (a t)") for a in (yT, uT))
                    d = cols[:, bass.ds(it + COFF["dskip"], 1)]
                V.scalar_tensor_tensor(y, u, d, ps[:, 4, 0:S], ALU.mult, ALU.add).then_inc(y_sum, 1)

            remainder(0)
            remainder(1)
            states(0, 0, 0)
            remainder(2)
            states(1, 1, 2)
            with dve.Fori(1, 7) as it:
                st.enter(8, it - 1)
                remainder(it * 2 + 1)
                states(0, it * 2, it * SB)
                y_add(it - 1)
                remainder(it * 2 + 2)
                states(1, it * 2 + 1, it * SB + 2)
                st.leave(8, 6)
            remainder(15)
            states(0, 14, 28)
            y_add(6)
            states(1, 15, 30)
            y_add(7)

            def diagonals(dg, row):
                for k in range(KD):
                    V.tensor_scalar(dg[:, k], ident, mcol[:, row, k:k + 1], None, ALU.mult).then_inc(dg_ok, 1)

            dve.wait_ge(y_sum, 8)
            dve.wait_ge(yspl_h, 1)
            V.tensor_tensor(yl[:], yT[:], yh[:].bitcast(F32), ALU.subtract).then_inc(yspl_l, 1)
            splits(BASE["glu"], 2 * TA)
            for g in range(4):
                dve.wait_ge(sg_T, g + 1)
                if g:
                    dve.wait_ge(yg_l, g)
                V.tensor_tensor(Y32[:], ps[:, 4 + g % 2].rearrange("p (k t) -> p k t", k=2),
                                yT[:, 2 * g:2 * g + 2], ALU.mult).then_inc(y32_ok, 1)
                dve.wait_ge(yg_h, g + 1)
                V.tensor_tensor(yl[:, 2 * g:2 * g + 2], Y32[:], yh[:, 2 * g:2 * g + 2].bitcast(F32), ALU.subtract
                                ).then_inc(yg_l, 1)
            turn("ya", 4, yah, yal)
            for br, name in enumerate(("abr", "sbr")):
                for pair in range(2):
                    for ab in range(2):
                        n = BASE[name] + (2 * pair + ab) * TA
                        splits(n, TA)
                        if br == 0 and pair == 0 and ab == 0:
                            dve.wait_ge(mod_col, 5)
                            dve.wait_ge(y32_ok, 4)
                            diagonals(dg1, 4)
                        dve.wait_ge(tile_used, n + TA)
                        for t in range(TT):
                            c0 = 1024 * pair + 512 * ab
                            g = G2[:, t, br * D + c0:br * D + c0 + CH]
                            m = M2[:, t, c0:c0 + CH]
                            if br == 0:
                                V.tensor_tensor(m, ps[:, 2 * ab + t], g, ALU.mult).then_inc(acc_free[ab], 1)
                            else:
                                V.tensor_tensor(btmp[:, t], ps[:, 2 * ab + t], g, ALU.mult).then_inc(acc_free[ab], 1)
                                dve.wait_ge(acc_free[ab], 2 * (PB[name] + pair) + t + 1)
                                V.tensor_tensor(m, m, btmp[:, t], ALU.add).then_inc(br_out, 1)
            turn("merged2", 8, xh, xl)
            dve.wait_ge(spread_out, 4)
            for pair in range(2):
                for ab in range(2):
                    n = BASE["out2"] + (2 * pair + ab) * TC
                    splits(n, TC)
                    if pair == 0 and ab == 0:
                        dve.wait_ge(br_out, 8)
                        diagonals(dg2, 5)
                    dve.wait_ge(tile_used, n + TC)
                    for t in range(TT):
                        c0 = 1024 * pair + 512 * ab
                        st.link(V.tensor_tensor(btmp[:, t], ps[:, 2 * ab + t], g1b[:, c0:c0 + CH], ALU.mult))
                        xs = X[:, t, c0:c0 + CH]
                        V.tensor_tensor(xs, xs, btmp[:, t], ALU.add).then_inc(acc_free[ab], 1)
            dve.wait_ge(acc_free[0], 2 * (PB["out2"] + 2))
            dve.wait_ge(acc_free[1], 2 * (PB["out2"] + 2))
            mean_sq(2, D, 2)
            V.scalar_tensor_tensor(mcol[:, 3], mcol[:, 3], 1.0, C("g4", 0, KD), ALU.add, ALU.mult).then_inc(mcol_ok, 1)
            for t in range(TT):
                V.tensor_scalar(N4[:, t], X[:, t], stat[:, 2 + t:3 + t], None, ALU.mult).then_inc(normed, 1)
            dve.wait_ge(mcol_ok, 2)
            turn("h4", 8, xh, xl, scale=lambda k: mcol[:, 3, k:k + 1], bias=lambda k: mcol[:, 2, k:k + 1], tmp=t4)

            dve.wait_ge(y_zero, 1)
            n0 = BASE["ffn"]

            def conv(b, half):
                for tap in range(2):
                    if tap == 0:
                        dve.wait_ge(cv_base, b * 8 + (4 * half + 4))
                    else:
                        st.wait()
                    for f in range(4):
                        q = 16 * half + 4 * f
                        d = 1 + tap
                        src = ps[:, 4 + 2 * half + f // 2, S * (f % 2):S * (f % 2) + S - d]
                        dst = cv[:, half, f, d:S]
                        ins = V.scalar_tensor_tensor(dst, src, ccol[:, q + 1 - tap:q + 2 - tap], dst,
                                                     ALU.mult, ALU.add)
                        if tap and f == 3:
                            ins.then_inc(cv_ok, 1)
                        else:
                            st.step(ins)

            def conv_cols(b):
                V.tensor_copy(ccol[:], cols[:, bass.ds(b * 32 + COFF["conv"], 32)] if not isinstance(b, int)
                              else C("conv", 32 * b, 32)).then_inc(cc_ok, 1)
                dve.wait_ge(cc_ok, b + 1)

            def product(b):
                dve.wait_ge(sil_ok, b + 1)
                dve.wait_ge(cv_ok, b * 2 + 2)
                V.tensor_tensor(F32t[:], cv[:, 0], sil[:], ALU.mult).then_inc(f32_ok, 1)

            def flow(b):
                dve.wait_ge(fh_ok, b + 1)
                dve.wait_ge(f32_ok, b + 1)
                h, l = (Fh2, Fl2) if isinstance(b, int) and b == FB - 1 else (Fh, Fl)
                V.tensor_tensor(l[:], F32t[:], h[:].bitcast(F32), ALU.subtract).then_inc(fl_ok, 1)

            def y_add(b, c, n, bank=4):
                dve.wait_ge(tile_used, n)
                if not isinstance(b, int) or b:
                    dve.wait_ge(dn_out, b * 8)
                for t in range(TT):
                    ys = Y[:, t, c * CH:(c + 1) * CH]
                    V.tensor_tensor(ys, ys, ps[:, bank + 2 * (c % 2) + t], ALU.add).then_inc(dn_out, 1)

            def hidden(b, rest):
                conv_cols(b)
                rest(2)
                conv(b, 0)
                rest(2)
                conv(b, 1)
                rest(2)
                product(b)
                rest(2)
                flow(b)

            def rest(k):
                for _ in range(k):
                    split(local[0], off)
                    local[0] += 1

            splits(n0, 2 * TC)
            with dve.Fori(1, FB - 1) as b:
                st.enter(14, b - 1)
                off = b * 24 - 24
                local = [n0 + 16 + SPL]

                hidden(b - 1, rest)
                rest(8)
                for c in range(4):
                    rest(2)
                    y_add(b - 1, c, off + (n0 + 34 + 2 * c), 0)
                st.leave(14, FB - 2)
            local, off = [TOTAL - 32 + SPL], 0
            hidden(FB - 2, rest)
            rest(8)
            conv_cols(FB - 1)
            rest(2)
            conv(FB - 1, 0)
            y_add(FB - 2, 0, TOTAL - 14, 0)
            conv(FB - 1, 1)
            rest(2)
            y_add(FB - 2, 1, TOTAL - 12, 0)
            product(FB - 1)
            rest(2)
            flow(FB - 1)
            y_add(FB - 2, 2, TOTAL - 10, 0)
            rest(2)
            rest(2)
            y_add(FB - 2, 3, TOTAL - 8, 0)
            rest(2)
            dve.wait_ge(spread_out, 8)
            for c in range(4):
                y_add(FB - 1, c, TOTAL - 6 + 2 * c)
                for t in range(TT):
                    ys = Y[:, t, c * CH:(c + 1) * CH]
                    dve.wait_ge(dn_out, 8 * (FB - 1) + 2 * c + t + 1)
                    st.link(V.tensor_tensor(ys, ys, g2b[:, c * CH:(c + 1) * CH], ALU.mult))
                    V.tensor_tensor(ys, ys, X[:, t, c * CH:(c + 1) * CH], ALU.add).then_inc(y_done, 1)

        @block.tensor
        def _(pe):
            def tile(n0, off, xhi, xlo, k0, banks, start, stop_, w=CH):
                pe.wait_ge(lo_ready, n0 + 1 + off)
                for k in range(SL):
                    H = hi[:, n0 % SPL, k * w:(k + 1) * w]
                    L = lo[:, n0 % SPL, k * w:(k + 1) * w]
                    for t in range(TT):
                        acc = ps[:, banks + t, 0:w]
                        xs = slice(t * P, (t + 1) * P)
                        s0 = start and k == 0
                        s1 = stop_ and k == SL - 1
                        PE_.matmul(acc, xhi[:, k0 + k, xs], H, start=s0, stop=False)
                        PE_.matmul(acc, xhi[:, k0 + k, xs], L, start=False, stop=False)
                        mm = PE_.matmul(acc, xlo[:, k0 + k, xs], H, start=False, stop=s1)
                mm.then_inc(tile_used, 1)

            def chunk(n0, off, tiles, ab, pair, xhi, xlo, bias=None, meanwhile=None):
                if not isinstance(pair, int) or pair:
                    pe.wait_ge(acc_free[ab], pair * 2)
                if bias is not None:
                    for t in range(TT):
                        mm = PE_.matmul(ps[:, 2 * ab + t], ones[0:1, :], bias, start=True, stop=False)
                    if ab:
                        mm.then_inc(bias_used, 1)
                if meanwhile is not None:
                    meanwhile()
                for j in range(tiles):
                    tile(n0 + j, off, xhi, xlo, SL * j, 2 * ab, bias is None and j == 0, j == tiles - 1)

            def turn(name, rounds, src):
                for r in range(rounds):
                    g = TBASE[name] + r
                    if g >= 2:
                        pe.wait_ge(turn_lo, g - 1)
                    for k in range(2):
                        for t in range(TT):
                            c0 = (2 * r + k) * P
                            mm = PE_.transpose(ps[:, 4 + g % 2, k * S + t * P:k * S + (t + 1) * P],
                                               src[:, t, c0:c0 + P], ident)
                    mm.then_inc(turned, 1)

            pe.wait_ge(small_in, 32)
            pe.wait_ge(normed, 2)
            turn("h1", 8, N1)
            pe.wait_ge(turn_lo, 8)
            for ab in range(2):
                chunk(TC * ab, 0, TC, ab, 0, xh, xl)
            with pe.Fori(0, 4) as it:
                for ab in range(2):
                    chunk((2 + ab) * TC, it * (2 * TC), TC, ab, it + 1, xh, xl)

            def gates(i):
                pe.wait_ge(bias_in, 16 * i + 16)
                for ab in range(2):
                    chunk(BASE["gate"] + (2 * i + ab) * TC, 0, TC, ab, 5 + i, xh, xl,
                          brow[0:1, ab * CH:(ab + 1) * CH], key_back if i + ab == 0 else None)

            def mix(t):
                pe.wait_ge(ln_done, t + 1)
                if t:
                    pe.wait_ge(mixed_out, 8)
                for g in range(SGU_G):
                    mm = PE_.matmul(ps[:, 4 + g // 2, SGU_W * (g % 2):SGU_W * (g % 2) + SGU_W], wsp[:, g],
                                    Z[:, t, D + g * SGU_W:D + (g + 1) * SGU_W], start=True, stop=True)
                    if g % 2:
                        mm.then_inc(mixed, 1)

            n0 = BASE["kpe"]
            pe.wait_ge(lo_ready, n0 + 1)
            acc = ps[0:ROPE, 4, 0:S]
            for k in range(KD):
                H = hi[:, n0 % SPL, k * ROPE:(k + 1) * ROPE]
                L = lo[:, n0 % SPL, k * ROPE:(k + 1) * ROPE]
                PE_.matmul(acc, H, xh[:, k], start=k == 0, stop=False)
                PE_.matmul(acc, L, xh[:, k], start=False, stop=False)
                mm = PE_.matmul(acc, H, xl[:, k], start=False, stop=k == KD - 1)
            mm.then_inc(tile_used, 1)

            def key_back():
                pe.wait_ge(kpe_T, 1)
                for t in range(TT):
                    mm = PE_.transpose(ps[:, 5, t * ROPE:(t + 1) * ROPE], KPT[0:ROPE, t * P:(t + 1) * P],
                                       ident[0:ROPE, 0:ROPE])
                mm.then_inc(kpe_ps, 1)

            gates(0)
            gates(1)
            pe.wait_ge(sq_ready, 8)
            mix(0)
            gates(2)
            mix(1)
            gates(3)
            pe.wait_ge(normed, 6)
            pe.wait_ge(mixed_out, 16)
            turn("cq", 2, CQ)
            turn("ckv", 2, CKV)
            pe.wait_ge(kpr_ok, 2)
            for t in range(TT):
                mm = PE_.transpose(ps[:, 6, t * P:(t + 1) * P], KPR[:, t], ident)
            mm.then_inc(kpt_ps, 1)

            def scores(h, bank, parts, off=0, banks=2):
                if h >= 2 or not isinstance(off, int):
                    pe.wait_ge(s_max, max(h + 1 - banks, 0) + off)
                for q, (c0, w) in enumerate(((0, P), (P, S))):
                    for i, (l, r) in enumerate(parts):
                        mm = PE_.matmul(ps[:, bank, c0:c0 + w], l[:, q * P:(q + 1) * P], r[:, 0:w],
                                        start=i == 0, stop=i == len(parts) - 1)
                mm.then_inc(s_ready, 1)

            def probsT(h, src, bank, off=0):
                pe.wait_ge(p_ready, 2 * h + 2 + off * 2)
                if h >= 2 or not isinstance(off, int):
                    pe.wait_ge(pt_ok, max(h - 1, 0) + off)
                for j in range(3):
                    mm = PE_.transpose(ps[:, bank, j * P:(j + 1) * P], src[:, h % 2, j * P:(j + 1) * P], ident)
                mm.then_inc(pt_ps, 1)

            def values(h, src, bank, v, off=0, banks=2):
                pe.wait_ge(pt_ok, h + 1 + off)
                if h >= 2 or not isinstance(off, int):
                    pe.wait_ge(o_out, 2 * max(h + 1 - banks, 0) + off * 2)
                b = h % 2
                PE_.matmul(ps[:, bank, 0:P], src[:, b, 0:P], v(0), start=True, stop=True)
                PE_.matmul(ps[:, bank, P:S], src[:, b, P:2 * P], v(0), start=True, stop=False)
                PE_.matmul(ps[:, bank, P:S], src[:, b, 2 * P:3 * P], v(1), start=False, stop=True
                           ).then_inc(o_ready, 1)

            pe.wait_ge(turn_lo, TBASE["merged"])
            for ab in range(2):
                pe.wait_ge(acc_free[ab], 18)
            pe.wait_ge(kpt_ok, 1)
            with pe.Fori(0, 4) as it:
                n0 = BASE["mla"]
                for j, (l_h, l_l, w) in enumerate(((cqh, cql, CH), (cqh, cql, GROUP * ROPE),
                                                   (ckh, ckl, CH), (ckh, ckl, CH))):
                    if j == 0:
                        pe.wait_ge(o_out, it * 8)
                    for i in range(TL):
                        tile(n0 + TL * j + i, it * (4 * TL), l_h, l_l, SL * i, 2 * j, i == 0, i == TL - 1, w)
                pe.wait_ge(m_evac, it * 8 + 2)
                for h in range(GROUP):
                    for t in range(TT):
                        mm = PE_.transpose(ps[:, h // 2, (h % 2) * S + t * P:(h % 2) * S + (t + 1) * P],
                                           qn[:, t, h * P:(h + 1) * P], ident)
                mm.then_inc(m_tr, 1)
                pe.wait_ge(m_evac, it * 8 + 6)
                for h in range(GROUP):
                    for t in range(TT):
                        mm = PE_.transpose(ps[:, 2 + h // 2, (h % 2) * S + t * P:(h % 2) * S + (t + 1) * P],
                                           kn[:, t, h * P:(h + 1) * P], ident)
                mm.then_inc(m_tr, 1)
                pe.wait_ge(m_rope, it * 2 + 2)
                for h in range(GROUP // 2):
                    for t in range(TT):
                        mm = PE_.transpose(ps[:, 4, h * S + t * P:h * S + (t + 1) * P],
                                           qrr[:, t, h * P:(h + 1) * P], ident)
                mm.then_inc(m_tr, 1)
                pe.wait_ge(m_ta, it * 2 + 2)
                pe.wait_ge(m_tv, it + 1)
                pe.wait_ge(m_evac, it * 8 + 8)
                for h in range(GROUP + 2):
                    if h < GROUP:
                        r0 = 64 * (h % 2)
                        scores(h, 5 + h % 2, ((qT[:, h], kT[:, h]),
                                              (qrT[r0:r0 + 64, h // 2], KPT[r0:r0 + 64])), it * 4)
                    if 1 <= h <= GROUP:
                        probsT(h - 1, pr, (4, 7)[(h - 1) % 2], it * 4)
                    if h >= 2:
                        g = h - 2
                        values(g, pT, g % 2, lambda t: vv[:, t, g * VH:(g + 1) * VH], it * 4)
            pe.wait_ge(merged_ok, 2)
            pe.wait_ge(pt_ok, 16)
            turn("merged", 8, GT)
            pe.wait_ge(turn_lo, TBASE["merged"] + 8)
            for pair in range(2):
                for ab in range(2):
                    chunk(BASE["out"] + (2 * pair + ab) * TC, 0, TC, ab, PB["out"] + pair, xh, xl)
            pe.wait_ge(normed, 8)
            turn("h2", 8, N2)
            pe.wait_ge(turn_lo, TBASE["h2"] + 8)
            for pair in range(2):
                for ab in range(2):
                    chunk(BASE["pq"] + (2 * pair + ab) * TC, 0, TC, ab, PB["pq"] + pair, xh, xl)
            pe.wait_ge(acc_free[0], 2 * (PB["pq"] + 2))
            pe.wait_ge(acc_free[1], 2 * (PB["pq"] + 2))
            for g in range(8):
                if g >= 2:
                    pe.wait_ge(qt_ok, g - 1)
                for k in range(2):
                    for t in range(TT):
                        c0 = (2 * g + k) * P
                        mm = PE_.transpose(ps[:, 4 + g % 2, k * S + t * P:k * S + (t + 1) * P], Q[:, t, c0:c0 + P],
                                           ident)
                mm.then_inc(qt_ps, 1)
            pe.wait_ge(keys_in, 16)
            pe.wait_ge(qt_ok, 8)
            for g in range(8):
                if g >= 4:
                    pe.wait_ge(sub_ok, g - 3)
                for j in range(4):
                    hp, t = 2 * g + j // 2, j % 2
                    mm = PE_.matmul(ps[:, 4 + g % 4, j * P:(j + 1) * P], QT[:, hp, t * P:(t + 1) * P], keys[:, hp],
                                    start=True, stop=True)
                mm.then_inc(sub_ps, 1)
            n0 = BASE["peer"]

            def u_block(n, off=0, bank=0):
                for j in range(TC):
                    tile(n + j, off, xh, xl, SL * j, bank, j == 0, j == TC - 1)

            for b in range(CHOICE):
                if b >= 2:
                    pe.wait_ge(a_ok, b * 2 - 2)
                u_block(n0 + b * TC, 0, 2 * (b % 2))
            pe.wait_ge(sel_ok, 1)
            pe.wait_ge(sub_ok, 8)
            for i in range(3):
                for t in range(TT):
                    mm = PE_.transpose(ps[:, 4 + i, t * P:(t + 1) * P], sel[:, i, t], ident)
            mm.then_inc(selT_ps, 1)
            pe.wait_ge(selT_ok, 3)
            with pe.Fori(0, 2) as it:
                for e in range(2):
                    for g in range(GQ // GT4):
                        b = g % 2
                        pe.wait_ge(g_out[b], it * 16 + (8 * e + g // 2))
                        pe.wait_ge(oh_ready[b], it * 80 + 5 * (8 * e + g // 2 + 1))
                        for k in range(GT4):
                            mm = PE_.matmul(ps[:, 4 + b, k * P:(k + 1) * P], oh1[:, b, k], oh2[:, b, k],
                                            start=True, stop=True)
                        mm.then_inc(g_ps[b], 1)
                        if b:
                            if g == 1:
                                pe.wait_ge(a_ok, it * 4 + 2 * (CHOICE + e))
                            j = g // 2
                            tile(n0 + (CHOICE + e) * TC + j, it * (2 * TC), xh, xl, SL * j, 0, j == 0, j == TC - 1)

            n0 = BASE["peer"] + AHEAD * TC

            def mod_sum(parts, bank):
                for k in range(KD):
                    mm = PE_.matmul(ps[:, bank, k:k + 1], parts[:, k * P:(k + 1) * P], ones[:, 0:1],
                                    start=True, stop=True)
                mm.then_inc(mod_ps, 1)

            def a_turn(v, q, loads):
                pe.wait_ge(a_in[q], loads)
                if not isinstance(v, int) or v:
                    pe.wait_ge(gated, v * 2)
                for k in range(JB):
                    for t in range(TT):
                        mm = PE_.transpose(ps[:, 2 + k // 2, (k % 2) * S + t * P:(k % 2) * S + (t + 1) * P],
                                           Ain[:, q, t, k * P:(k + 1) * P], ident)
                mm.then_inc(a_T, 1)

            def v_block(v, q, n, off=0, first=False):
                pe.wait_ge(pl_ok, v + 1)
                for c in range(4):
                    pe.wait_ge(v_out, v * 8 + max(2 * c - 2, 0 if first else -2))
                    for j in range(TL):
                        tile(n + TL * c + j, off, Ph[:, q], Pl[:, q], SL * j, 4 + 2 * (c % 2), j == 0, j == TL - 1)

            for b in range(CHOICE + GATES, AHEAD):
                pe.wait_ge(a_ok, 2 * b)
                u_block(n0 - (AHEAD - b) * TC)
            for b in range(2):
                pe.wait_ge(g_out[b], 32)
            a_turn(0, 0, 16)
            with pe.Fori(0, MAIN // 4) as rr:
                for i in range(4):
                    n, off, v = n0 + 16 * i, rr * 64, rr * 4 + i
                    pe.wait_ge(a_ok, rr * 8 + 2 * (AHEAD + i))
                    u_block(n, off)
                    if i == 0:
                        pe.wait_ge(mod_col, rr)
                    a_turn(v + 1, (i + 1) % 2, rr * 32 + 16 * ((i + 1) // 2 + 1))
                    v_block(v, i % 2, n + 8, off, first=i == 0)
                pe.wait_ge(mod_used, rr * KD + KD)
                pe.wait_ge(gated, rr * 8 + 10)
                mod_sum(macc, 2)
            n0 += 16 * MAIN
            pe.wait_ge(mod_col, MAIN // 4)
            with pe.Fori(0, AHEAD // 2 - 1) as it:
                for e in range(2):
                    v = it * 2 + (MAIN + e)
                    a_turn(v + 1, 1 - e, it * 16 + 16 * ((MAIN + e + 1) // 2 + 1))
                    v_block(v, e, n0 + 8 * e, it * 16)
            a_turn(NBLK - 1, 1, 16 * (NBLK // 2))
            v_block(NBLK - 2, 0, n0 + 8 * AHEAD - 16)
            v_block(NBLK - 1, 1, n0 + 8 * AHEAD - 8)
            pe.wait_ge(mod_used, 5 * KD)
            mod_sum(macc, 0)

            def spread_vector(dg, n):
                pe.wait_ge(dg_ok, n * KD)
                for k in range(KD):
                    mm = PE_.matmul(ps[:, 4 + k // 4, (k % 4) * P:(k % 4 + 1) * P], ones[:], dg[:, k],
                                    start=True, stop=True)
                    if k % 4 == 3:
                        mm.then_inc(spread, 1)

            pe.wait_ge(v_out, 8 * NBLK)
            pe.wait_ge(normed, 12)
            turn("h3", 8, N3)
            pe.wait_ge(turn_lo, TBASE["h3"] + 8)
            with pe.Fori(0, 3) as it:
                for ab in range(2):
                    chunk(BASE["in2"] + ab * TC, it * (2 * TC), TC, ab, it + PB["in2"], xh, xl)
            for ab in range(2):
                chunk(BASE["in2"] + (6 + ab) * TC, 0, TC, ab, PB["in2"] + 3, xh, xl)
            pe.wait_ge(mod2_used, KD)
            for k in range(KD):
                mm = PE_.matmul(ps[:, 4, k:k + 1], macc2[:, k * P:(k + 1) * P], ones[:, 0:1], start=True, stop=True)
            mm.then_inc(mod2_ps, 1)
            pe.wait_ge(mod_col, 6)
            with pe.Fori(0, 4) as it:
                for ab in range(2):
                    h, n = 16 + ab, BASE["in2"] + (8 + ab) * TC

                    def gates(j):
                        for i in range(j, j + 2):
                            tile(n + i, it * (2 * TC), xh, xl, SL * i, 2 * ab, i == 0, i == TC - 1)

                    pe.wait_ge(acc_free[ab], it * 2 + 2 * (PB["in2"] + 4))
                    gates(0)
                    pe.wait_ge(qk_rope, it * 2 + (ab + 1))
                    pe.wait_ge(qk_out, it * 2 + ab)
                    for a in range(2):
                        for t in range(TT):
                            mm = PE_.transpose(ps[:, 7, a * S + t * P:a * S + (t + 1) * P], rqk[:, t, a], ident)
                    mm.then_inc(qk_tr, 1)
                    gates(2)
                    pe.wait_ge(qk_out, it * 2 + (ab + 1))
                    scores(h, 4, ((qkT[:, 0], qkT[:, 1]),), it * 2, banks=1)
                    gates(4)
                    probsT(h, pr2, 5, it * 2)
                    gates(6)
                    values(h, pT2, 6, lambda t: QKVU[:, t, bass.ds(it * (2 * AD) + (2 * AW + ab * AD), AD)], it * 2,
                           banks=1)
            pe.wait_ge(acc_free[0], 2 * (PB["in2"] + 8))
            pe.wait_ge(acc_free[1], 2 * (PB["in2"] + 8))
            pe.wait_ge(pt_ok, 24)
            for g in range(4):
                if g >= 2:
                    pe.wait_ge(ut_ok, g - 1)
                for k in range(2):
                    for t in range(TT):
                        c0 = 3 * AW + (2 * g + k) * P
                        mm = PE_.transpose(ps[:, 4 + g % 2, k * S + t * P:k * S + (t + 1) * P],
                                           QKVU[:, t, c0:c0 + P], ident)
                mm.then_inc(ut_ps, 1)
            pe.wait_ge(ut_ok, 4)
            def b_turn(it):
                pe.wait_ge(bm_ok, it * 4 + 4)
                pe.wait_ge(bl_ok, it * 2)
                for i in range(2):
                    for k in range(SB):
                        mm = PE_.transpose(ps[:, 6 + i, k * P:(k + 1) * P], bM[:, i, k], ident)
                    mm.then_inc(bl_ps, 1)

            def b_inputs(it, e):
                pe.wait_ge(bl_ok, it * 2 + 2)
                q = it * 2 + e
                if not isinstance(q, int) or q >= 2:
                    pe.wait_ge(rot_ok, q * 2 - 2)
                u = uT[:, it] if isinstance(it, int) else uT[:, bass.ds(it, 1)].rearrange("p a t -> p (a t)")
                for i in range(2):
                    for k in range(2):
                        mm = PE_.matmul(ps[:, 2 * e + i, k * S:k * S + S], bL[:, i, 2 * e + k], u,
                                        start=True, stop=True)
                mm.then_inc(bu_ps, 1)

            def outputs(it, e):
                pe.wait_ge(fw_ok, it * 4 + (2 * e + 2))
                pe.wait_ge(fw_p, it * 4 + (2 * e + 2))
                if e == 0:
                    pe.wait_ge(cm_ok, it * 4 + 4)
                    pe.wait_ge(y_sum, it)
                parts = ((0, fw[:, e, 0]), (0, fw[:, e, 1]), (1, rz[:, e, 0]), (1, rz[:, e, 1]))
                for n, (i, x) in enumerate(parts):
                    for k in range(2):
                        mm = PE_.matmul(ps[:, 4, 0:S], cM[:, i, 2 * e + k], x[:, k], start=e + n + k == 0,
                                        stop=e == 1 and n == 3 and k == 1)
                mm.then_inc(y_ps, 1)

            def round_(it):
                b_inputs(it, 1)
                b_turn(it + 1)
                outputs(it, 0)
                b_inputs(it + 1, 0)
                outputs(it, 1)

            b_turn(0)
            b_inputs(0, 0)
            round_(0)
            with pe.Fori(1, 7) as it:
                round_(it)
            b_inputs(7, 1)
            outputs(7, 0)
            outputs(7, 1)
            pe.wait_ge(yspl_l, 1)
            pe.wait_ge(bglu_in, 16)
            for ab in range(2):
                chunk(BASE["glu"] + ab * TA, 0, TA, ab, PB["glu"], yh, yl, bias=bglu[0:1, ab * CH:(ab + 1) * CH])
            pe.wait_ge(y_sum, 8)
            pe.wait_ge(acc_free[1], 2 * (PB["glu"] + 1))
            for g in range(4):
                pe.wait_ge(acc_free[g // 2], 2 * (PB["glu"] + 1))
                if g >= 2:
                    pe.wait_ge(y32_ok, g - 1)
                for k in range(2):
                    for t in range(TT):
                        c0 = (2 * g + k) * P
                        mm = PE_.transpose(ps[:, 4 + g % 2, k * S + t * P:k * S + (t + 1) * P], SG[:, t, c0:c0 + P],
                                           ident)
                mm.then_inc(sg_T, 1)
            pe.wait_ge(y32_ok, 4)
            turn("ya", 4, YA)
            pe.wait_ge(turn_lo, TBASE["ya"] + 4)
            for pair in range(2):
                for ab in range(2):
                    chunk(BASE["abr"] + (2 * pair + ab) * TA, 0, TA, ab, PB["abr"] + pair, yah, yal)
            pe.wait_ge(yg_l, 4)
            for pair in range(2):
                for ab in range(2):
                    chunk(BASE["sbr"] + (2 * pair + ab) * TA, 0, TA, ab, PB["sbr"] + pair, yh, yl)
            spread_vector(dg1, 1)
            pe.wait_ge(br_out, 8)
            pe.wait_ge(spread_out, 4)
            turn("merged2", 8, M2)
            pe.wait_ge(turn_lo, TBASE["merged2"] + 8)
            for pair in range(2):
                for ab in range(2):
                    chunk(BASE["out2"] + (2 * pair + ab) * TC, 0, TC, ab, PB["out2"] + pair, xh, xl)
            spread_vector(dg2, 2)
            pe.wait_ge(normed, 14)
            pe.wait_ge(spread_out, 8)
            turn("h4", 8, N4)
            pe.wait_ge(turn_lo, TBASE["h4"] + 8)
            n0 = BASE["ffn"]

            def up_block(b, n, off=0):
                for half in range(2):
                    if not isinstance(b, int):
                        pe.wait_ge(dn_out, b * 8 + (2 * half - 10))
                    elif b:
                        pe.wait_ge(up_out, b * 4 + (2 * half - 2))
                    for j in range(TC):
                        tile(n + TC * half + j, off, xh, xl, SL * j, 2 * half, j == 0, j == TC - 1)

            def up_turn(b, half):
                pe.wait_ge(up_out, b * 4 + (2 * half + 2))
                if not isinstance(b, int) or b:
                    pe.wait_ge(cv_ok, b * 2 + (half - 1))
                for f in range(4):
                    for t in range(TT):
                        mm = PE_.transpose(ps[:, 4 + 2 * half + f // 2, (f % 2) * S + t * P:(f % 2) * S + (t + 1) * P],
                                           UP[:, half, t, f * P:(f + 1) * P], ident)
                mm.then_inc(up_T, 1)

            def down(b, c, n, off=0, bank=0):
                h, l = (Fh2, Fl2) if isinstance(b, int) and b == FB - 1 else (Fh, Fl)
                if c == 0:
                    pe.wait_ge(fl_ok, b + 1)
                elif c >= 2:
                    pe.wait_ge(dn_out, b * 8 + (2 * c - 2))
                for j in range(TL):
                    tile(n + TL * c + j, off, h, l, SL * j, bank + 2 * (c % 2), j == 0, j == TL - 1)

            def down_and_turn(b, n, off=0):
                up_turn(b + 1, 0)
                down(b, 0, n, off)
                up_turn(b + 1, 1)
                for c in range(1, 4):
                    down(b, c, n, off)

            pe.wait_ge(acc_free[0], 2 * (PB["out2"] + 2))
            pe.wait_ge(acc_free[1], 2 * (PB["out2"] + 2))
            up_block(0, n0)
            for half in range(2):
                up_turn(0, half)
            up_block(1, n0 + 16)
            with pe.Fori(2, FB) as b:
                down_and_turn(b - 2, n0 + 32, b * 24 - 48)
                up_block(b, n0 + 40, b * 24 - 48)
            down_and_turn(FB - 2, n0 + 24 * FB - 16)
            for c in range(4):
                down(FB - 1, c, n0 + 24 * FB - 8, bank=4)


def constants():
    c = np.zeros((P, NCONST), np.float32)

    def put(name, a):
        c[:, KOFF[name]:KOFF[name] + a.shape[-1]] = a

    put("ident", np.eye(P, dtype=np.float32))
    put("ones", np.ones((P, P), np.float32))
    causal = np.where(np.arange(P)[:, None] >= np.arange(P)[None], 0.0, NEG).astype(np.float32)
    put("mask", np.concatenate([causal, np.zeros((P, P), np.float32), causal], 1))
    put("triu", np.triu(np.ones((P, P), np.float32)))
    put("halfpi", np.full((P, 1), math.pi / 2, np.float32))
    put("magic", np.full((P, 1), MAGIC, np.float32))
    put("iota", np.arange(2 * P, dtype=np.float32)[None].repeat(P, 0))
    f = np.float32(10000.0) ** (-np.arange(0, 64, 2, dtype=np.float32) / np.float32(64))
    put("freq", f.astype(np.float32)[None].repeat(P, 0))
    f = np.float32(10000.0) ** (-np.arange(64, dtype=np.float32) / np.float32(64))
    put("freq2", f.astype(np.float32)[None].repeat(P, 0))
    return c


MODS = [0, 1, 3, 4, 2, 5]


def weight_tiles(w):
    k, n = w.shape
    return np.ascontiguousarray(
        w.reshape(k // (SL * P), SL, P, n // CH, CH).transpose(3, 0, 2, 1, 4).reshape(-1, P, TW))


def columns(v):
    return v.reshape(-1, P).T


def prepare(i):
    g = {k: np.asarray(v) for k, v in i.items()}
    a = {}
    a["const"] = constants()
    a["x"] = np.ascontiguousarray(g["x"][0].reshape(TT, P, D).transpose(1, 0, 2))
    a["pos"] = np.ascontiguousarray(np.concatenate([g["positions"].reshape(TT, P).T,
                                                    g["positions_2"].reshape(TT, P).T], 1))
    w = g["w_in"][0]
    o = 2 * LORA
    order = np.concatenate([w[:, 0:o], w[:, o + ROPE:]], 1)
    a["w_in"] = weight_tiles(order)
    a["kpe"] = np.ascontiguousarray(w[:, o:o + ROPE].reshape(KD, P, ROPE).transpose(1, 0, 2).reshape(P, KD * ROPE))
    a["b_gate"] = np.ascontiguousarray(g["b_gate"][0].reshape(4, 2 * CH))
    uq, ukv = g["w_uq"][0], g["w_ukv"][0]
    parts = []
    for r in range(HEADS // GROUP):
        hs = slice(r * GROUP, (r + 1) * GROUP)
        for m in (uq[:, hs, :NOPE], ukv[:, hs, :NOPE], ukv[:, hs, NOPE:]):
            parts.append(weight_tiles(m.reshape(LORA, CH)))
    a["mla"] = np.concatenate(parts)
    a["mla_r"] = np.ascontiguousarray(
        uq[:, :, NOPE:].reshape(TL, SL, P, HEADS // GROUP, GROUP * ROPE).transpose(3, 0, 2, 1, 4)
        .reshape(HEADS // GROUP * TL, P, TW // 2))
    a["w_spatial"] = np.ascontiguousarray(g["w_spatial"][0].transpose(2, 0, 1))
    a["sgu_ln_g"], a["sgu_ln_b"] = g["sgu_ln_g"][0], g["sgu_ln_b"][0]
    a["out"] = weight_tiles(g["w_out"][0])
    a["pq"] = weight_tiles(g["w_peer_q"][0].reshape(D, D))
    a["peer_keys"] = np.ascontiguousarray(g["peer_keys"][0].reshape(16, NKEY, P).transpose(2, 0, 1))
    u = g["peer_u"][0].reshape(P, NBLK, JB, KD, P)
    a["peer_u"] = np.ascontiguousarray(u.transpose(1, 3, 4, 2, 0).reshape(NBLK, TC, SL, P, EB)
                                       .transpose(0, 1, 3, 2, 4).reshape(NBLK * TC, P, TW))
    v = g["peer_v"][0].reshape(P, NBLK, TL, SL, 4, CH)
    a["peer_v"] = np.ascontiguousarray(v.transpose(1, 4, 2, 0, 3, 5).reshape(NBLK * 4 * TL, P, TW))
    a["w_mod"] = np.ascontiguousarray(g["w_mod_2"][0].reshape(KD, P, 6, D).transpose(2, 0, 1, 3)[MODS]
                                      .reshape(6 * KD, P, D))
    a["g_final"] = g["g_final"]
    a["q_norm_g"], a["k_norm_g"] = g["q_norm_g_2"][0], g["k_norm_g_2"][0]
    a["in2"] = weight_tiles(g["w_in_2"][0])
    a["glu"] = weight_tiles(g["w_glu_2"][0])
    a["b_glu"] = np.ascontiguousarray(g["b_glu_2"][0].reshape(1, AW))
    a["abr"] = weight_tiles(g["w_attn_br_2"][0])
    a["sbr"] = weight_tiles(g["w_ssm_br_2"][0])
    a["out2"] = weight_tiles(g["w_out_2"][0])
    wu = weight_tiles(g["w_up_2"][0]).reshape(2, FB, TC, P, TW)
    a["w_up"] = np.ascontiguousarray(wu.transpose(1, 0, 2, 3, 4).reshape(FB * 2 * TC, P, TW))
    wd = g["w_down_2"][0].reshape(FB, TL, SL, P, 4, CH)
    a["w_down"] = np.ascontiguousarray(wd.transpose(0, 4, 1, 3, 2, 5).reshape(FB * 4 * TL, P, TW))

    def states(v):
        return v.reshape(STT, P, *v.shape[2:]).swapaxes(0, 1)

    for n in ("re", "im"):
        a[f"ssm_b_{n}"] = np.ascontiguousarray(states(g[f"ssm_b_{n}_2"][0]))
        a[f"ssm_c_{n}"] = np.ascontiguousarray(states(g[f"ssm_c_{n}_2"][0].swapaxes(1, 2)))
    cols = np.zeros((P, NCOLS), np.float32)

    def put(name, m):
        cols[:, COFF[name]:COFF[name] + m.shape[1]] = m

    put("bmod", columns(g["b_mod_2"][0].reshape(6, D)[MODS].reshape(-1)))
    put("g1", columns(g["g_norm1"][0]))
    put("gqa", columns(g["g_q_a"][0]))
    put("gkva", columns(g["g_kv_a"][0]))
    put("g2", columns(g["g_norm2"][0]))
    put("g3", columns(g["norm1_g_2"][0]))
    put("g4", columns(g["norm2_g_2"][0]))
    put("bsp", g["b_spatial"][0].T)
    put("c", columns(g["c_2"][0]))
    put("dskip", columns(g["ssm_d_2"][0]))
    put("lre", states(g["ssm_lambda_re_2"][0]))
    put("lim", states(g["ssm_lambda_im_2"][0]))
    put("ldt", states(np.broadcast_to(g["ssm_log_dt_2"][0][:, None], (NG, NST))))
    taps = np.concatenate([g["conv_w_2"][0], g["conv_b_2"]], 0)
    taps = taps.reshape(4, 2, FB, 4, P).transpose(4, 2, 1, 3, 0)
    put("conv", taps.reshape(P, FB * 32))
    a["cols"] = cols
    return a


def kernel(**inputs):
    import numpy as _np
    import concourse.bacc as _bacc
    from concourse import mybir as _mybir
    from concourse.bass_utils import run_bass_kernel_spmd as _run

    arrays = prepare(inputs)
    nc = _bacc.Bacc("TRN2", target_bir_lowering=False, num_devices=1)
    aps = {}
    for name, v in arrays.items():
        aps[name] = nc.dram_tensor(f"in_{name}", v.shape, _mybir.dt.from_np(v.dtype), kind="ExternalInput").ap()
    out = nc.dram_tensor("out_0", (S, D), F32, kind="ExternalOutput").ap()
    build(nc, aps, out)
    r = _run(nc, [{f"in_{k}": v for k, v in arrays.items()}], core_ids=[0])
    return _np.asarray(r.results[0]["out_0"]).reshape(1, S, D)
```
